# Optimizing a Trainium2 kernel written in Bass

```python
import math
import jax, jax.numpy as jnp
from jax import lax
import numpy as np

D_MODEL = 1024
BATCH = 1
SEQ = 256
DEPTH = 1

HEAD_DIM = 64
BLOCK_Q = 128
N_SB_HEADS = 4
DIL_PATTERNS = ((128, 1), (512, 4), (2048, 16))
N_DIL_GROUPS = len(DIL_PATTERNS)
N_DIL_HEADS = 4
N_FOX_HEADS = 4
N_DIFF_HEADS = 4
DIFF_QK_DIM = HEAD_DIM // 2
N_BRANCH = 4
BRANCH_WIDTH = 4 * HEAD_DIM
D_FF = 4 * D_MODEL
RMS_EPS = 1e-6
N_ALIBI = N_DIL_GROUPS * N_DIL_HEADS + N_DIFF_HEADS

SB_W = N_SB_HEADS * HEAD_DIM
DIL_W = N_DIL_GROUPS * N_DIL_HEADS * HEAD_DIM
FOX_W = N_FOX_HEADS * HEAD_DIM
DIFF_QK_W = N_DIFF_HEADS * 2 * DIFF_QK_DIM
DIFF_V_W = N_DIFF_HEADS * HEAD_DIM
GATE_W = N_BRANCH * D_MODEL
SPLIT_SIZES = (SB_W,) * 3 + (DIL_W,) * 3 + (FOX_W,) * 3 + (N_FOX_HEADS,) + (DIFF_QK_W, DIFF_QK_W, DIFF_V_W) + (GATE_W,)
D_IN = sum(SPLIT_SIZES)
SPLIT_OFFSETS = tuple(sum(SPLIT_SIZES[:i + 1]) for i in range(len(SPLIT_SIZES) - 1))


def rms_norm(x, g):
    xf = x.astype(jnp.float32)
    y = xf * lax.rsqrt(jnp.mean(xf * xf, axis=-1, keepdims=True) + RMS_EPS)
    return (y * g.astype(jnp.float32)).astype(x.dtype)

def alibi_slopes():
    return jnp.asarray(2.0 ** (-8.0 * np.arange(1, N_ALIBI + 1) / N_ALIBI), dtype=jnp.float32)

def _stick_breaking(q_blk, k, v, dist):
    z = jnp.einsum('bqhd,bshd->bhqs', q_blk, k).astype(jnp.float32) * (HEAD_DIM ** -0.5)
    strict = dist > 0
    log_keep = jnp.where(strict, jax.nn.log_sigmoid(-z), 0.0)
    log_between = lax.cumsum(log_keep, axis=3, reverse=True) - log_keep
    a = jnp.where(strict, jnp.exp(jax.nn.log_sigmoid(z) + log_between), 0.0)
    return jnp.einsum('bhqs,bshd->bqhd', a.astype(v.dtype), v)

def _dilated(q_blk, k, v, t_idx, slopes):
    outs, lses = [], []
    for g, (window, dil) in enumerate(DIL_PATTERNS):
        dists = dil * jnp.arange(window // dil + 1)
        idx = t_idx[:, None] - dists[None, :]
        valid = idx >= 0
        idx = jnp.maximum(idx, 0)
        kg = jnp.take(k[:, :, g], idx, axis=1)
        vg = jnp.take(v[:, :, g], idx, axis=1)
        s = jnp.einsum('bqhd,bqnhd->bhqn', q_blk[:, :, g], kg).astype(jnp.float32) * (HEAD_DIM ** -0.5)
        s = s - slopes[g][:, None, None] * dists.astype(jnp.float32)
        s = jnp.where(valid, s, -jnp.inf)
        lse = jax.nn.logsumexp(s, axis=-1)
        p = jnp.exp(s - lse[..., None])
        outs.append(jnp.einsum('bhqn,bqnhd->bqhd', p.astype(v.dtype), vg))
        lses.append(lse)
    alpha = jax.nn.softmax(jnp.stack(lses, axis=0), axis=0)
    alpha = jnp.transpose(alpha, (0, 1, 3, 2))[..., None]
    return jnp.sum(alpha.astype(v.dtype) * jnp.stack(outs, axis=0), axis=0)

def _forgetting(q_blk, k, v, cum_blk, cum, dist):
    s = jnp.einsum('bqhd,bshd->bhqs', q_blk, k).astype(jnp.float32) * (HEAD_DIM ** -0.5)
    s = s + jnp.transpose(cum_blk, (0, 2, 1))[..., None] - jnp.transpose(cum, (0, 2, 1))[:, :, None, :]
    p = jax.nn.softmax(jnp.where(dist >= 0, s, -jnp.inf), axis=-1)
    return jnp.einsum('bhqs,bshd->bqhd', p.astype(v.dtype), v)

def _differential(q_blk, k, v, dist, slopes, lam):
    s = jnp.einsum('bqhcd,bshcd->bchqs', q_blk, k).astype(jnp.float32) * (DIFF_QK_DIM ** -0.5)
    s = s - slopes[:, None, None] * dist.astype(jnp.float32)
    p = jax.nn.softmax(jnp.where(dist >= 0, s, -jnp.inf), axis=-1)
    w = p[:, 0] - lam * p[:, 1]
    return jnp.einsum('bhqs,bshd->bqhd', w.astype(v.dtype), v)

def _token_mixers(h, w_in, b_forget, lam, diff_g, diff_out_scale, slopes_dil, slopes_diff):
    bsz, seq, _ = h.shape
    proj = h @ w_in
    (qa, ka, va, qb, kb, vb, qc, kc, vc, f_logit, qd, kd, vd, gate_logit) = jnp.split(proj, SPLIT_OFFSETS, axis=-1)
    qa, ka, va = (a.reshape(bsz, seq, N_SB_HEADS, HEAD_DIM) for a in (qa, ka, va))
    qb, kb, vb = (a.reshape(bsz, seq, N_DIL_GROUPS, N_DIL_HEADS, HEAD_DIM) for a in (qb, kb, vb))
    qc, kc, vc = (a.reshape(bsz, seq, N_FOX_HEADS, HEAD_DIM) for a in (qc, kc, vc))
    qd, kd = (a.reshape(bsz, seq, N_DIFF_HEADS, 2, DIFF_QK_DIM) for a in (qd, kd))
    vd = vd.reshape(bsz, seq, N_DIFF_HEADS, HEAD_DIM)
    log_f = jax.nn.log_sigmoid(f_logit.astype(jnp.float32) + b_forget.astype(jnp.float32))
    cum = jnp.cumsum(log_f, axis=1)
    s_idx = jnp.arange(seq)

    def block(q0):
        t_idx = q0 + jnp.arange(BLOCK_Q)
        dist = t_idx[:, None] - s_idx[None, :]
        sl = lambda a: lax.dynamic_slice_in_dim(a, q0, BLOCK_Q, axis=1)
        return (_stick_breaking(sl(qa), ka, va, dist),
                _dilated(sl(qb), kb, vb, t_idx, slopes_dil),
                _forgetting(sl(qc), kc, vc, sl(cum), cum, dist),
                _differential(sl(qd), kd, vd, dist, slopes_diff, lam))

    o_a, o_b, o_c, o_d = lax.map(block, jnp.arange(seq // BLOCK_Q) * BLOCK_Q)
    unblock = lambda o: jnp.moveaxis(o, 0, 1).reshape(bsz, seq, o.shape[3], o.shape[4])
    o_d = rms_norm(unblock(o_d), diff_g) * diff_out_scale
    ys = jnp.stack([unblock(o_a), unblock(o_b), unblock(o_c), o_d], axis=2)
    return ys.reshape(bsz, seq, N_BRANCH, BRANCH_WIDTH), gate_logit

def first_inputs(seed: int = 0) -> dict:
    key = jax.random.key(seed)
    ks = jax.random.split(key, 16)
    nrm = lambda k, shape, scale: jax.random.normal(k, shape, jnp.float32) * scale
    return {
        'x': nrm(ks[0], (BATCH, SEQ, D_MODEL), 1.0),
        'mix_norm_g': 1.0 + nrm(ks[1], (DEPTH, D_MODEL), 0.05),
        'w_in': nrm(ks[2], (DEPTH, D_MODEL, D_IN), D_MODEL ** -0.5),
        'b_forget': jax.random.uniform(ks[3], (DEPTH, N_FOX_HEADS), jnp.float32, 1.0, 4.0),
        'lambda_q1': nrm(ks[4], (DEPTH, DIFF_QK_DIM), 0.1),
        'lambda_k1': nrm(ks[5], (DEPTH, DIFF_QK_DIM), 0.1),
        'lambda_q2': nrm(ks[6], (DEPTH, DIFF_QK_DIM), 0.1),
        'lambda_k2': nrm(ks[7], (DEPTH, DIFF_QK_DIM), 0.1),
        'diff_norm_g': 1.0 + nrm(ks[8], (DEPTH, HEAD_DIM), 0.05),
        'w_branch': nrm(ks[9], (DEPTH, N_BRANCH, BRANCH_WIDTH, D_MODEL), BRANCH_WIDTH ** -0.5),
        'w_out': nrm(ks[10], (DEPTH, D_MODEL, D_MODEL), D_MODEL ** -0.5),
        'mlp_norm_g': 1.0 + nrm(ks[11], (DEPTH, D_MODEL), 0.05),
        'w_up': nrm(ks[12], (DEPTH, D_MODEL, D_FF), D_MODEL ** -0.5),
        'w_down': nrm(ks[13], (DEPTH, D_FF, D_MODEL), D_FF ** -0.5),
        'final_norm_g': 1.0 + nrm(ks[14], (D_MODEL,), 0.05),
    }

def first_block(x, mix_norm_g, w_in, b_forget, lambda_q1, lambda_k1, lambda_q2, lambda_k2, diff_norm_g, w_branch, w_out, mlp_norm_g, w_up, w_down, final_norm_g):
    bsz, seq, _ = x.shape
    slopes = alibi_slopes()
    n0, n1 = N_DIL_HEADS, N_DIL_HEADS + N_DIFF_HEADS
    slopes_dil = jnp.stack([slopes[:n0], slopes[n1:n1 + N_DIL_HEADS], slopes[n1 + N_DIL_HEADS:]], axis=0)
    slopes_diff = slopes[n0:n1]
    for l in range(DEPTH):
        lambda_init = 0.8 - 0.6 * math.exp(-0.3 * l)
        lam = (jnp.exp(jnp.sum(lambda_q1[l].astype(jnp.float32) * lambda_k1[l].astype(jnp.float32)))
               - jnp.exp(jnp.sum(lambda_q2[l].astype(jnp.float32) * lambda_k2[l].astype(jnp.float32))) + lambda_init)
        h = rms_norm(x, mix_norm_g[l])
        ys, gate_logit = _token_mixers(h, w_in[l], b_forget[l], lam, diff_norm_g[l], 1.0 - lambda_init, slopes_dil, slopes_diff)
        branch = jnp.einsum('bsnc,ncd->bsnd', ys, w_branch[l])
        gates = jax.nn.sigmoid(gate_logit.reshape(bsz, seq, N_BRANCH, D_MODEL))
        x = x + jnp.sum(gates * branch, axis=2) @ w_out[l]
        h = rms_norm(x, mlp_norm_g[l])
        x = x + jnp.square(jax.nn.relu(h @ w_up[l])) @ w_down[l]
    return rms_norm(x, final_norm_g)


DEPTH_2 = 2

N_A_LAYERS = DEPTH_2 // 2
N_B_LAYERS = DEPTH_2 - N_A_LAYERS

RET_HEADS = 4
RET_QK_DIM = D_MODEL // RET_HEADS
RET_V_DIM = 2 * D_MODEL // RET_HEADS
RET_CHUNK = 128
RET_IN = 2 * RET_HEADS * RET_QK_DIM + 2 * RET_HEADS * RET_V_DIM

FFN_HIDDEN = ((8 * D_MODEL + 3 * 256 - 1) // (3 * 256)) * 256

NSA_HEADS = 16
NSA_GROUPS = 4
NSA_REP = NSA_HEADS // NSA_GROUPS
NSA_HEAD_DIM = 64
CMP_LEN = 32
CMP_STRIDE = 16
CMP_HIDDEN = 256
SEL_LEN = 64
SEL_TOPK = 16
WINDOW = 512
Q_BLOCK = 128
NSA_IN = NSA_HEADS * NSA_HEAD_DIM + 3 * NSA_HEADS
KV_SHARED_OUT = 6 * NSA_GROUPS * NSA_HEAD_DIM

REL_BUCKETS = 32
REL_MAX_DIST = 128


def rms_norm_2(x, g):
    xf = x.astype(jnp.float32)
    y = xf * lax.rsqrt(jnp.mean(xf * xf, axis=-1, keepdims=True) + RMS_EPS)
    return (y * g.astype(jnp.float32)).astype(x.dtype)

def swiglu_ffn(x, w_in, w_out):
    gate, up = jnp.split(x @ w_in, 2, axis=-1)
    return (jax.nn.silu(gate) * up) @ w_out

def rotate_pairs(x, cos, sin):
    x1 = x[..., 0::2]
    x2 = x[..., 1::2]
    return jnp.stack([x1 * cos - x2 * sin, x1 * sin + x2 * cos], axis=-1).reshape(x.shape)

def t5_bucket(dist):
    n = jnp.maximum(dist, 0)
    max_exact = REL_BUCKETS // 2
    nf = jnp.maximum(n, 1).astype(jnp.float32)
    large = max_exact + (jnp.log(nf / max_exact) / math.log(REL_MAX_DIST / max_exact)
                         * (REL_BUCKETS - max_exact)).astype(jnp.int32)
    large = jnp.minimum(large, REL_BUCKETS - 1)
    return jnp.where(n < max_exact, n, large)

def masked_softmax(logits, mask):
    logits = jnp.where(mask, logits, -jnp.inf)
    m = jnp.max(logits, axis=-1, keepdims=True)
    m = jnp.where(jnp.isfinite(m), m, 0.0)
    p = jnp.exp(logits - m)
    return p / jnp.maximum(jnp.sum(p, axis=-1, keepdims=True), jnp.finfo(jnp.float32).tiny)

def retention_mixer(x, w_in, w_out):
    B, S, _ = x.shape
    h, dk, dv, C = RET_HEADS, RET_QK_DIM, RET_V_DIM, RET_CHUNK
    proj = x @ w_in
    q, k, v, g = jnp.split(proj, [h * dk, 2 * h * dk, 2 * h * dk + h * dv], axis=-1)
    q = q.reshape(B, S, h, dk).astype(jnp.float32)
    k = k.reshape(B, S, h, dk).astype(jnp.float32)
    v = v.reshape(B, S, h, dv).astype(jnp.float32)
    pos = jnp.arange(S, dtype=jnp.float32)
    theta = 1.0 / (10000.0 ** jnp.linspace(0.0, 1.0, dk // 2, dtype=jnp.float32))
    ang = pos[:, None] * theta[None, :]
    cos = jnp.cos(ang)[:, None, :]
    sin = jnp.sin(ang)[:, None, :]
    q = rotate_pairs(q, cos, sin)
    k = rotate_pairs(k, cos, sin) * (dk ** -0.5)
    log_gamma = jnp.log(1.0 - 2.0 ** (-5.0 - jnp.arange(h, dtype=jnp.float32)))
    idx = jnp.arange(C, dtype=jnp.float32)
    rel = idx[:, None] - idx[None, :]
    intra_decay = jnp.where(rel >= 0, jnp.exp(jnp.maximum(rel, 0.0) * log_gamma[:, None, None]), 0.0)
    q_decay = jnp.exp((idx + 1.0)[None, :] * log_gamma[:, None])
    k_decay = jnp.exp((C - 1.0 - idx)[None, :] * log_gamma[:, None])
    chunk_decay = jnp.exp(C * log_gamma)
    nC = S // C

    def to_chunks(t):
        return t.reshape(B, nC, C, h, t.shape[-1]).transpose(1, 0, 3, 2, 4)

    def step(state, inp):
        qc, kc, vc = inp
        scores = jnp.einsum('bhid,bhjd->bhij', qc, kc) * intra_decay
        o = (jnp.einsum('bhij,bhje->bhie', scores, vc)
             + jnp.einsum('bhid,bhde->bhie', qc * q_decay[..., None], state))
        state = (state * chunk_decay[:, None, None]
                 + jnp.einsum('bhjd,bhje->bhde', kc * k_decay[..., None], vc))
        return state, o

    state0 = jnp.zeros((B, h, dk, dv), jnp.float32)
    _, o = lax.scan(step, state0, (to_chunks(q), to_chunks(k), to_chunks(v)))
    o = o.transpose(1, 0, 3, 2, 4).reshape(B, S, h, dv)
    o = o * lax.rsqrt(jnp.mean(o * o, axis=-1, keepdims=True) + RMS_EPS)
    o = (o.reshape(B, S, h * dv) * jax.nn.silu(g.astype(jnp.float32))).astype(x.dtype)
    return o @ w_out

def nsa_shared_kv(h, kv_norm, kv_w, cmp_pe_k, cmp_w1_k, cmp_w2_k, cmp_pe_v, cmp_w1_v, cmp_w2_v):
    B, S, _ = h.shape
    G, d = NSA_GROUPS, NSA_HEAD_DIM
    kv = rms_norm_2(h, kv_norm) @ kv_w
    k_c, v_c, k_s, v_s, k_w, v_w = [t.reshape(B, S, G, d) for t in jnp.split(kv, 6, axis=-1)]
    n_cmp = (S - CMP_LEN) // CMP_STRIDE + 1
    blk_idx = np.arange(n_cmp)[:, None] * CMP_STRIDE + np.arange(CMP_LEN)[None, :]

    def compress(t, pe, w1, w2):
        blocks = t[:, blk_idx] + pe[:, None, :]
        blocks = blocks.transpose(0, 1, 3, 2, 4).reshape(B, n_cmp, G, CMP_LEN * d)
        return jax.nn.silu(blocks @ w1) @ w2

    kc = compress(k_c, cmp_pe_k, cmp_w1_k, cmp_w2_k)
    vc = compress(v_c, cmp_pe_v, cmp_w1_v, cmp_w2_v)
    n_sel = S // SEL_LEN
    ks = k_s.reshape(B, n_sel, SEL_LEN, G, d).transpose(0, 3, 1, 2, 4)
    vs = v_s.reshape(B, n_sel, SEL_LEN, G, d).transpose(0, 3, 1, 2, 4)
    pad = ((0, 0), (WINDOW, 0), (0, 0), (0, 0))
    kw = jnp.pad(k_w, pad)
    vw = jnp.pad(v_w, pad)
    return (kc, vc, ks, vs, kw, vw)

def nsa_mixer(x, w_in, w_out, rel_bias, shared):
    B, S, _ = x.shape
    H, G, R, d = NSA_HEADS, NSA_GROUPS, NSA_REP, NSA_HEAD_DIM
    Q = Q_BLOCK
    kc, vc, ks, vs, kw, vw = shared
    proj = x @ w_in
    q = proj[..., :H * d].reshape(B, S, G, R, d)
    gate = jax.nn.sigmoid(proj[..., H * d:].astype(jnp.float32)).reshape(B, S, G, R, 3)
    n_cmp = kc.shape[1]
    n_sel = ks.shape[2]
    n_top = min(SEL_TOPK, n_sel)
    cmp_end = jnp.arange(n_cmp, dtype=jnp.int32) * CMP_STRIDE + CMP_LEN - 1
    ratio = SEL_LEN // CMP_STRIDE
    lead = CMP_LEN // CMP_STRIDE - 1
    span = ratio + lead
    sel_map = ratio * np.arange(n_sel)[:, None] - lead + np.arange(span)[None, :]
    sel_map = np.where((sel_map >= 0) & (sel_map < n_cmp), sel_map, n_cmp)
    bias_tab = rel_bias.astype(jnp.float32)
    bias_gr = bias_tab.reshape(REL_BUCKETS, G, R).transpose(1, 0, 2)
    scale = d ** -0.5
    gather_blocks = jax.vmap(jax.vmap(lambda kb, ib: kb[ib]))
    kc32 = kc.astype(jnp.float32)
    vc32 = vc.astype(jnp.float32)
    sel_ids = jnp.arange(n_sel, dtype=jnp.int32)
    blk_start = sel_ids * SEL_LEN
    win_off = jnp.arange(WINDOW + Q, dtype=jnp.int32)
    g_ids = jnp.arange(G)[None, :, None, None, None]

    def block(qb):
        start = qb * Q
        t = start + jnp.arange(Q, dtype=jnp.int32)
        qblk = lax.dynamic_slice_in_dim(q, start, Q, 1).astype(jnp.float32) * scale
        gg = lax.dynamic_slice_in_dim(gate, start, Q, 1)
        dist_c = t[:, None] - cmp_end[None, :]
        s = jnp.einsum('bqgrd,bngd->bgrqn', qblk, kc32)
        s = s + bias_tab[t5_bucket(dist_c)].reshape(Q, n_cmp, G, R).transpose(2, 3, 0, 1)
        p_c = masked_softmax(s, dist_c >= 0)
        o_c = jnp.einsum('bgrqn,bngd->bqgrd', p_c, vc32)
        imp_c = jnp.sum(p_c, axis=2)
        imp_c = jnp.concatenate([imp_c, jnp.zeros(imp_c.shape[:-1] + (1,), imp_c.dtype)], axis=-1)
        imp = jnp.sum(imp_c[..., sel_map], axis=-1)
        cur = t // SEL_LEN
        valid = blk_start[None, :] <= t[:, None]
        forced = ((sel_ids[None, :] == 0) | (sel_ids[None, :] == cur[:, None])
                  | (sel_ids[None, :] == cur[:, None] - 1))
        imp = jnp.where(forced, jnp.inf, jnp.where(valid, imp, -jnp.inf))
        _, sel_idx = lax.top_k(imp, n_top)
        k_sel = gather_blocks(ks, sel_idx).astype(jnp.float32)
        v_sel = gather_blocks(vs, sel_idx).astype(jnp.float32)
        pos = sel_idx[..., None] * SEL_LEN + jnp.arange(SEL_LEN, dtype=jnp.int32)
        dist_s = t[None, None, :, None, None] - pos
        s = jnp.einsum('bqgrd,bgqnld->bgrqnl', qblk, k_sel)
        s = s + jnp.moveaxis(bias_gr[g_ids, t5_bucket(dist_s)], -1, 2)
        s = s.reshape(B, G, R, Q, n_top * SEL_LEN)
        mask_s = (dist_s >= 0).reshape(B, G, 1, Q, n_top * SEL_LEN)
        p_s = masked_softmax(s, mask_s).reshape(B, G, R, Q, n_top, SEL_LEN)
        o_s = jnp.einsum('bgrqnl,bgqnld->bqgrd', p_s, v_sel)
        kwin = lax.dynamic_slice_in_dim(kw, start, WINDOW + Q, 1).astype(jnp.float32)
        vwin = lax.dynamic_slice_in_dim(vw, start, WINDOW + Q, 1).astype(jnp.float32)
        kpos = start - WINDOW + win_off
        dist_w = t[:, None] - kpos[None, :]
        s = jnp.einsum('bqgrd,bkgd->bgrqk', qblk, kwin)
        s = s + bias_tab[t5_bucket(dist_w)].reshape(Q, WINDOW + Q, G, R).transpose(2, 3, 0, 1)
        mask_w = (dist_w >= 0) & (dist_w < WINDOW) & (kpos[None, :] >= 0)
        p_w = masked_softmax(s, mask_w)
        o_w = jnp.einsum('bgrqk,bkgd->bqgrd', p_w, vwin)
        o = gg[..., 0:1] * o_c + gg[..., 1:2] * o_s + gg[..., 2:3] * o_w
        return o.reshape(B, Q, H * d)

    o = lax.map(block, jnp.arange(S // Q, dtype=jnp.int32))
    o = o.transpose(1, 0, 2, 3).reshape(B, S, H * d).astype(x.dtype)
    return o @ w_out

def second_inputs(seed: int = 0) -> dict:
    key = jax.random.key(seed)
    ks = jax.random.split(key, 24)
    f32 = jnp.float32

    def dense(k, shape, fan_in):
        return jax.random.normal(k, shape, f32) * (fan_in ** -0.5)

    def gain(k, shape):
        return 1.0 + 0.1 * jax.random.normal(k, shape, f32)

    d = NSA_HEAD_DIM
    return {
        "x": jax.random.normal(ks[0], (BATCH, SEQ, D_MODEL), f32),
        "mix_norm_pre": gain(ks[1], (DEPTH_2, D_MODEL)),
        "mix_norm_post": gain(ks[2], (DEPTH_2, D_MODEL)),
        "ffn_norm_pre": gain(ks[3], (DEPTH_2, D_MODEL)),
        "ffn_norm_post": gain(ks[4], (DEPTH_2, D_MODEL)),
        "ffn_w_in": dense(ks[5], (DEPTH_2, D_MODEL, 2 * FFN_HIDDEN), D_MODEL),
        "ffn_w_out": dense(ks[6], (DEPTH_2, FFN_HIDDEN, D_MODEL), FFN_HIDDEN),
        "ret_w_in": dense(ks[7], (N_A_LAYERS, D_MODEL, RET_IN), D_MODEL),
        "ret_w_out": dense(ks[8], (N_A_LAYERS, RET_HEADS * RET_V_DIM, D_MODEL), RET_HEADS * RET_V_DIM),
        "kv_norm": gain(ks[9], (D_MODEL,)),
        "kv_w": dense(ks[10], (D_MODEL, KV_SHARED_OUT), D_MODEL),
        "cmp_pe_k": 0.5 * jax.random.normal(ks[11], (CMP_LEN, d), f32),
        "cmp_w1_k": dense(ks[12], (CMP_LEN * d, CMP_HIDDEN), CMP_LEN * d),
        "cmp_w2_k": dense(ks[13], (CMP_HIDDEN, d), CMP_HIDDEN),
        "cmp_pe_v": 0.5 * jax.random.normal(ks[14], (CMP_LEN, d), f32),
        "cmp_w1_v": dense(ks[15], (CMP_LEN * d, CMP_HIDDEN), CMP_LEN * d),
        "cmp_w2_v": dense(ks[16], (CMP_HIDDEN, d), CMP_HIDDEN),
        "nsa_w_in": dense(ks[17], (N_B_LAYERS, D_MODEL, NSA_IN), D_MODEL),
        "nsa_w_out": dense(ks[18], (N_B_LAYERS, NSA_HEADS * d, D_MODEL), NSA_HEADS * d),
        "rel_bias": 0.5 * jax.random.normal(ks[19], (REL_BUCKETS, NSA_HEADS), f32),
    }

def second_block(x, mix_norm_pre, mix_norm_post, ffn_norm_pre, ffn_norm_post, ffn_w_in, ffn_w_out,
              ret_w_in, ret_w_out, kv_norm, kv_w, cmp_pe_k, cmp_w1_k, cmp_w2_k,
              cmp_pe_v, cmp_w1_v, cmp_w2_v, nsa_w_in, nsa_w_out, rel_bias):
    h = x
    shared = None
    for layer in range(DEPTH_2):
        if layer == N_A_LAYERS:
            shared = nsa_shared_kv(h, kv_norm, kv_w, cmp_pe_k, cmp_w1_k, cmp_w2_k,
                                   cmp_pe_v, cmp_w1_v, cmp_w2_v)
        normed = rms_norm_2(h, mix_norm_pre[layer])
        if layer < N_A_LAYERS:
            mixed = retention_mixer(normed, ret_w_in[layer], ret_w_out[layer])
        else:
            j = layer - N_A_LAYERS
            mixed = nsa_mixer(normed, nsa_w_in[j], nsa_w_out[j], rel_bias, shared)
        h = h + rms_norm_2(mixed, mix_norm_post[layer])
        normed = rms_norm_2(h, ffn_norm_pre[layer])
        h = h + rms_norm_2(swiglu_ffn(normed, ffn_w_in[layer], ffn_w_out[layer]), ffn_norm_post[layer])
    return h


def setup_inputs(seed=0):
    out = dict(first_inputs(seed))
    for name, value in second_inputs(seed + 1).items():
        if name != "x":
            out[name + "_2"] = value
    return out


def reference(
    x, mix_norm_g, w_in, b_forget, lambda_q1, lambda_k1, lambda_q2, lambda_k2, diff_norm_g,
    w_branch, w_out, mlp_norm_g, w_up, w_down, final_norm_g, mix_norm_pre_2, mix_norm_post_2,
    ffn_norm_pre_2, ffn_norm_post_2, ffn_w_in_2, ffn_w_out_2, ret_w_in_2, ret_w_out_2,
    kv_norm_2, kv_w_2, cmp_pe_k_2, cmp_w1_k_2, cmp_w2_k_2, cmp_pe_v_2, cmp_w1_v_2, cmp_w2_v_2,
    nsa_w_in_2, nsa_w_out_2, rel_bias_2,
):
    x = first_block(
        x, mix_norm_g, w_in, b_forget, lambda_q1, lambda_k1, lambda_q2, lambda_k2, diff_norm_g,
        w_branch, w_out, mlp_norm_g, w_up, w_down, final_norm_g,
    )
    return second_block(
        x, mix_norm_pre_2, mix_norm_post_2, ffn_norm_pre_2, ffn_norm_post_2, ffn_w_in_2,
        ffn_w_out_2, ret_w_in_2, ret_w_out_2, kv_norm_2, kv_w_2, cmp_pe_k_2, cmp_w1_k_2,
        cmp_w2_k_2, cmp_pe_v_2, cmp_w1_v_2, cmp_w2_v_2, nsa_w_in_2, nsa_w_out_2, rel_bias_2,
    )


_drawn_inputs = setup_inputs


def setup_inputs(seed=0):
    import zlib

    import numpy as np

    out = dict(_drawn_inputs(seed))
    spreads = {}
    factors = {'lambda_q2': 3.128, 'lambda_k2': 2.994}
    for name, (base, spread) in spreads.items():
        noise = np.random.default_rng([zlib.crc32(name.encode()), seed]).standard_normal(out[name].shape)
        drawn = base * np.exp(spread * noise) if base else spread * noise
        out[name] = __import__('jax').numpy.asarray(drawn.astype(out[name].dtype))
    for name, factor in factors.items():
        out[name] = (out[name] * factor).astype(out[name].dtype)
    return out
```

```python
from contextlib import ExitStack

import numpy as np

import concourse.bass as bass
from concourse import mybir

F32 = mybir.dt.float32
F32R = mybir.dt.float32r
ALU = mybir.AluOpType
ACT = mybir.ActivationFunctionType
AX_X = mybir.AxisListType.X

P = 128
SEQ = 256
D = 1024
KT = D // P
TT = SEQ // P
HD = 64
CW = 256
CHUNK = KT * CW
SLOTS = 4
AHEAD = 3
EPS = 1e-6
MASKED = -1e30
N_CMP, CMP_LEN, CMP_STRIDE, CMP_HIDDEN = 15, 32, 16, 256
GROUPS = 4
RET_HEADS, RET_DV = 4, 512
FFN = 2816
FFN_KT = FFN // P
D_FF = 4096
LAMBDA_INIT = 0.8 - 0.6

PHASES = [("qkv", 18), ("gates", 16), ("branch", 4), ("out", 4), ("up", 16), ("down", 16),
          ("ret", 24), ("ret_out", 8), ("ffn_in_0", 22), ("ffn_out_0", 12),
          ("kv", 6), ("cmp", 4), ("nsa_q", 4), ("nsa_out", 4), ("ffn_in_1", 22), ("ffn_out_1", 12)]
START = {}
N_CHUNKS = 0
for _name, _n in PHASES:
    START[_name] = N_CHUNKS
    N_CHUNKS += _n

GROUP_COUNT = {"qkv": 18, "gates": 16, "branch": 16, "out": 4, "up": 16, "down": 4, "ret": 24, "ret_out": 4,
               "ffn_in_0": 22, "ffn_out_0": 4, "kv": 6, "cmp": 0, "nsa_q": 4, "nsa_out": 4,
               "ffn_in_1": 22, "ffn_out_1": 4}
GROUP = {}
_g = 0
for _name, _n in PHASES:
    GROUP[_name] = _g
    _g += GROUP_COUNT[_name]

NORMS = ["mix", "mlp", "ret", "ffn0", "nsa", "ffn1"]


class At:

    def __init__(self, const, step=0, it=None):
        self.const, self.step, self.it = const, step, it

    def __add__(self, n):
        return At(self.const + n, self.step, self.it)

    def __sub__(self, n):
        return self + (-n)

    def __mul__(self, n):
        return At(self.const * n, self.step * n, self.it)

    def mod(self, m):
        assert self.step % m == 0
        return self.const % m

    def div(self, m):
        assert self.step % m == 0
        return At(self.const // m, self.step // m, self.it)

    @property
    def value(self):
        return self.const if self.it is None or self.step == 0 else self.it * self.step + self.const


def wait(engine, semaphore, at):
    if isinstance(at, int):
        at = At(at)
    if at.const > 0 or at.step > 0:
        engine.wait_ge(semaphore, at.value)


def build(nc, io):
    with ExitStack() as ctx:
        def sb(name, shape, dt=F32, where=None):
            return (where or ctx).enter_context(nc.sbuf_tensor(name, shape, dt))

        def sem(name):
            return ctx.enter_context(nc.semaphore(name))

        raw = sb("raw", [P, SLOTS, CHUNK])
        wh = sb("wh", [P, SLOTS, CHUNK], F32R)
        wl = sb("wl", [P, SLOTS, CHUNK], F32R)
        x = sb("x", [P, TT, D])
        hh = sb("hh", [P, KT, SEQ], F32R)
        hl = sb("hl", [P, KT, SEQ], F32R)
        ident = sb("ident", [P, P])
        gains = sb("gains", [P, len(NORMS) + 1, KT])
        sums = sb("sums", [P, 2 * TT])
        means = sb("means", [P, TT])
        rstd = sb("rstd", [P, TT])
        mhalf = sb("mhalf", [P, 8])
        psums = sb("psums", [P, TT, 4])
        psum1 = sb("psum1", [P, TT])
        w_f = sb("w_f", [P, KT, 4])
        w_gate = sb("w_gate", [P, KT, 48])
        w2k = sb("w2k", [P, 2, HD])
        w2v = sb("w2v", [P, 2, HD])
        b_f = sb("b_f", [P, 4])
        lams = sb("lams", [P, 4, 32])
        lam = sb("lam", [P, 8])
        lamp = sb("lamp", [P, 2, 32])
        diff_g = sb("diff_g", [P, HD])
        ones = sb("ones", [1, SEQ])
        negmax = sb("negmax", [P, 8, 8])
        rowsum = sb("rowsum", [P, 8, 8])
        coef = sb("coef", [P, 8, 8])
        small = sb("small", [P, 8, 8])
        logf = sb("logf", [P, TT, 4])
        fsmall = sb("fsmall", [P, 2, TT, 4])

        def arena(*tensors):
            with ExitStack() as scope:
                return [sb(n, s, dt, scope) for n, s, dt in tensors]

        xn, = arena(("xn", [P, TT, D], F32))
        def arena_after(used, *tensors):
            with ExitStack() as scope:
                sb(f"skip_{tensors[0][0]}", [P, used // 4], F32, scope)
                return [sb(n, s, dt, scope) for n, s, dt in tensors]

        gate, = arena(("gate", [P, 32, SEQ], F32))
        after_xn, upper, after_gate = 8 * 1024, 16 * 1024, 32 * 1024
        cumrow, = arena_after(after_xn, ("cumrow", [1, 2, 4, SEQ], F32))
        q_b, k_b = arena_after(upper, ("q_b", [HD, 2, 4, SEQ], F32), ("k_b", [HD, 2, 4, SEQ], F32))
        (v_b, s_b1, pt_b1, bias_b, ys1, og, tri) = arena_after(
            after_gate, ("v_b", [P, 2, TT, CW], F32), ("s_b1", [P, 6 * CW], F32), ("pt_b1", [P, 3, 512], F32),
            ("bias_b", [P, 2, 4, SEQ], F32), ("ys1", [P, TT, D], F32), ("og", [P, 3, TT, CW], F32),
            ("tri", [P, TT, SEQ], F32))
        ysh1, ysl1 = arena_after(after_gate, ("ysh1", [P, KT, SEQ], F32R), ("ysl1", [P, KT, SEQ], F32R))
        hid1h, hid1l, r1, grow1 = arena(("hid1h", [P, 32, SEQ], F32R), ("hid1l", [P, 32, SEQ], F32R),
                                        ("r1", [P, 2, 2, 2, SEQ], F32), ("grow1", [P, D], F32))
        (yth, ytl, rq, rk, ra, cs, decay, rv, rg, ry, rst, mixed0, grow0) = arena(
            ("yth", [P, 16, SEQ], F32R), ("ytl", [P, 16, SEQ], F32R), ("rq", [P, 2, SEQ], F32),
            ("rk", [P, 2, SEQ], F32), ("ra", [P, 2, 2, SEQ], F32), ("cs", [P, 2, SEQ], F32),
            ("decay", [P, RET_HEADS, SEQ], F32), ("rv", [P, TT, RET_DV], F32), ("rg", [P, TT, RET_DV], F32),
            ("ry", [P, TT, RET_DV], F32), ("rst", [P, 384], F32), ("mixed0", [P, TT, D], F32),
            ("grow0", [P, D], F32))
        (hid2h, hid2l, ft, fsil, mixed2, grow2) = arena(
            ("hid2h", [P, FFN_KT, SEQ], F32R), ("hid2l", [P, FFN_KT, SEQ], F32R), ("ft", [P, 2, SEQ], F32),
            ("fsil", [P, 2, SEQ], F32), ("mixed2", [P, TT, D], F32), ("grow2", [P, D], F32))
        (ksw, vsw, nbias, cbias, ys2, relb, hot, stripsb, kct, vct, peb, hidc, pe_in, gate_n, o_n, flip, gate_f) = arena(
            ("ksw", [HD, 2, GROUPS, SEQ], F32), ("vsw", [P, 2, TT, CW], F32), ("nbias", [P, 16, SEQ], F32),
            ("cbias", [P, TT, 16, N_CMP], F32), ("ys2", [P, TT, D], F32), ("relb", [33, 16], F32),
            ("hot", [33, 384], F32), ("stripsb", [16, 384], F32), ("kct", [HD, 60], F32),
            ("vct", [N_CMP, GROUPS, HD], F32), ("peb", [P, 2, 2], F32), ("hidc", [P, 2, 2, 60], F32),
            ("pe_in", [P, 2, 16, 2], F32), ("gate_n", [P, TT, 48], F32), ("o_n", [P, TT, CW], F32),
            ("flip", [P, P], F32), ("gate_f", [P, TT, 48], F32))
        after_nsa = 47 * 1024
        nq, ns, npt = arena_after(after_nsa, ("nq", [HD, 4, 4, SEQ], F32), ("ns", [P, 2, 6 * CW], F32),
                                  ("npt", [P, 3, 512], F32))
        kvh, kvl, rgh, rgl = arena_after(after_nsa, ("kvh", [P, KT, SEQ], F32R), ("kvl", [P, KT, SEQ], F32R),
                                         ("rgh", [P, 2, 16, 62], F32R), ("rgl", [P, 2, 16, 62], F32R))
        t2, = arena_after(30 * 1024, ("t2", [P, GROUPS, SEQ], F32))
        chot, = arena_after(12 * 1024, ("chot", [33, 30 * P], F32))
        ysh2, ysl2, mixed1, growb = arena_after(after_nsa, ("ysh2", [P, KT, SEQ], F32R), ("ysl2", [P, KT, SEQ], F32R),
                                                ("mixed1", [P, TT, D], F32), ("growb", [P, D], F32))

        acc = [ctx.enter_context(nc.psum_tensor(f"acc{i}", [P, 512], F32)) for i in range(2)]
        aux = ctx.enter_context(nc.psum_tensor("aux", [P, 6, 512], F32))

        full = [sem(f"full{i}") for i in range(SLOTS)]
        hi_ready, lo_ready = sem("hi_ready"), sem("lo_ready")
        mm_done = sem("mm_done")
        acc_out = [sem("acc_out0"), sem("acc_out1")]
        const_in, table_in = sem("const_in"), sem("table_in")
        x_in = sem("x_in")
        setup = sem("setup")
        squares, rstd_step, rstd_ready, xn_ready = sem("squares"), sem("rstd_step"), sem("rstd_ready"), sem("xn_ready")
        turned, norm_hi, norm_lo = sem("turned"), sem("norm_hi"), sem("norm_lo")
        dve_step = sem("dve_step")
        act_step = sem("act_step")
        bias_in = [sem("bias_in0"), sem("bias_in1")]
        v_ready = sem("v_ready")
        scores_done, scores_out = sem("scores_done"), sem("scores_out")
        probs_max, probs_ready = sem("probs_max"), sem("probs_ready")
        probs_turned, pt_ready, pv_done, o_out = sem("probs_turned"), sem("pt_ready"), sem("pv_done"), sem("o_out")
        sb_l, sb_c, sb_e = sem("sb_l"), sem("sb_c"), sem("sb_e")
        f_done, f_in, f_e, f_ready, cum_done, cum_out = (sem("f_done"), sem("f_in"), sem("f_e"), sem("f_ready"),
                                                         sem("cum_done"), sem("cum_out"))
        ys_ready, ys_turned, ys_hi, ys_lo = sem("ys_ready"), sem("ys_turned"), sem("ys_hi"), sem("ys_lo")
        branch_done = sem("branch_done")
        mix_sum, mix_ready = sem("mix_sum"), sem("mix_ready")
        relu_out, sq_ready, hid_hi, hid_lo = sem("relu_out"), sem("sq_ready"), sem("hid_hi"), sem("hid_lo")
        rot_out = sem("rot_out")
        ret_const = sem("ret_const")
        st_done, st_out = sem("st_done"), sem("st_out")
        ro_done, ro_sq, ro_r, ro_y = sem("ro_done"), sem("ro_sq"), sem("ro_r"), sem("ro_y")
        ry_turned, yt_hi, yt_lo = sem("ry_turned"), sem("yt_hi"), sem("yt_lo")
        post_sq, post_r, post_done = sem("post_sq"), sem("post_r"), sem("post_done")
        first_done = sem("first_done")
        post_g, post_step = sem("post_g"), sem("post_step")
        grow_in = [sem(f"grow_in{i}") for i in range(5)]
        sil_out = sem("sil_out")
        nsa_const, strip_mm, strip_out, strip_io, nbias_in = (sem("nsa_const"), sem("strip_mm"), sem("strip_out"),
                                                              sem("strip_io"), sem("nbias_in"))
        chot_in, cb_mm, cb_out = sem("chot_in"), sem("cb_mm"), sem("cb_out")
        t2_out, gath, cmp_mm, cmp_b, cmp_hid, cmp_kv, kct_out = (sem("t2_out"), sem("gath"), sem("cmp_mm"), sem("cmp_b"),
                                                                 sem("cmp_hid"), sem("cmp_kv"), sem("kct_out"))
        ng_mm, ng_out = sem("ng_mm"), sem("ng_out")
        n_scores, n_sout, n_max, n_exp, n_turn, n_pt, n_pv, n_o = (sem("n_scores"), sem("n_sout"), sem("n_max"), sem("n_exp"),
                                                                   sem("n_turn"), sem("n_pt"), sem("n_pv"), sem("n_o"))
        nys_ready, nys_turned, nys_hi, nys_lo = sem("nys_ready"), sem("nys_turned"), sem("nys_hi"), sem("nys_lo")
        y_out = sem("y_out")

        def group_out(engine, g):
            g = g if isinstance(g, At) else At(g)
            wait(engine, acc_out[g.mod(2)], g.div(2) + 1)

        def turned_back(k):
            return aux[:, k // 2, (k % 2) * SEQ:(k % 2 + 1) * SEQ].rearrange("p (t n) -> p t n", t=2)[:, :, ::-1]

        def n_turn_bank(j):
            return acc[0][:, :] if j == 2 else aux[:, 3 + j, :]

        def n_turns_before(b):
            return 3 * min(b, 8) + 2 * max(b - 8, 0)

        def n_batch(b):
            return (b // 2, b % 2) if b < 8 else (b - 8, 2)

        def backwards(ap):
            return ap[:, :, :, ::-1]

        def split_hi(act, c):
            c = c if isinstance(c, At) else At(c)
            if c.it is None and c.const >= N_CHUNKS:
                return
            s = c.mod(SLOTS)
            wait(act, full[s], (c.div(SLOTS) + 1) * 16)
            wait(act, mm_done, c - (SLOTS - 1))
            nc.scalar.activation(wh[:, s, :], raw[:, s, :], ACT.Copy).then_inc(hi_ready, 1)

        def split_lo(dve, c):
            c = c if isinstance(c, At) else At(c)
            if c.it is None and c.const >= N_CHUNKS:
                return
            s = c.mod(SLOTS)
            wait(dve, hi_ready, c + 1)
            nc.vector.tensor_tensor(wl[:, s, :], raw[:, s, :], wh[:, s, :].bitcast(F32),
                                    ALU.subtract).then_inc(lo_ready, 1)

        def take(pe, c):
            wait(pe, lo_ready, c + 1)

        def claim(pe, g):
            wait(pe, acc_out[g.mod(2)], g.div(2))
            return acc[g.mod(2)]

        def mm(*args, start=False, stop=False):
            return nc.tensor.matmul(*args, start=start, stop=stop)

        def product_t(pe, c, g, ah, al):
            c, g = (c if isinstance(c, At) else At(c)), (g if isinstance(g, At) else At(g))
            take(pe, c)
            bank, s = claim(pe, g), c.mod(SLOTS)
            for sub in range(2):
                out = bank[:, sub * SEQ:(sub + 1) * SEQ]
                for k in range(KT):
                    cols = slice(k * CW + sub * P, k * CW + (sub + 1) * P)
                    mm(out, wh[:, s, cols], ah[:, k, :], start=(k == 0))
                    mm(out, wh[:, s, cols], al[:, k, :])
                    last = mm(out, wl[:, s, cols], ah[:, k, :], stop=(k == KT - 1))
            last.then_inc(mm_done, 1)

        def product_n(pe, c, g, ah, al, k0=0, nk=KT, total=KT):
            c, g = (c if isinstance(c, At) else At(c)), (g if isinstance(g, At) else At(g))
            take(pe, c)
            if k0 == 0:
                claim(pe, g)
            bank, s = acc[g.mod(2)], c.mod(SLOTS)
            for t in range(TT):
                out = bank[:, t * CW:(t + 1) * CW]
                tok = slice(t * P, (t + 1) * P)
                for kk in range(nk):
                    k = k0 + kk
                    cols = slice(kk * CW, (kk + 1) * CW)
                    nc.tensor.matmul(out, ah[:, k, tok], wh[:, s, cols], start=(k == 0 and t == 0), stop=False,
                                     skip_group_check=True)
                    nc.tensor.matmul(out, ah[:, k, tok], wl[:, s, cols], start=False, stop=False,
                                     skip_group_check=True)
                    last = nc.tensor.matmul(out, al[:, k, tok], wh[:, s, cols], start=False,
                                            stop=(k == total - 1), skip_group_check=True)
            last.then_inc(mm_done, 1)

        def norm_act_squares(act, n, x_waits):
            for s, v in x_waits:
                act.wait_ge(s, v)
            for t in range(TT):
                nc.scalar.activation(xn[:, t, :], x[:, t, :], ACT.Square,
                                     accum_out=sums[:, t:t + 1]).then_inc(squares, 1)

        def norm_pool(pool, n):
            pool.wait_ge(squares, TT * (n + 1))
            nc.gpsimd.tensor_scalar(means[:], sums[:, 0:TT], 1.0 / D, EPS, ALU.mult, ALU.add).then_inc(rstd_step, 1)
            pool.wait_ge(rstd_step, n + 1)
            nc.gpsimd.tensor_tensor(rstd[:], means[:], mhalf[:, 0:TT], ALU.pow).then_inc(rstd_ready, 1)

        def norm_dve_scale(dve, n):
            dve.wait_ge(rstd_ready, n + 1)
            for t in range(TT):
                nc.vector.tensor_scalar(xn[:, t, :], x[:, t, :], rstd[:, t:t + 1], None,
                                        ALU.mult).then_inc(xn_ready, 1)

        def norm_pe(pe, n):
            pe.wait_ge(xn_ready, TT * (n + 1))
            for k in range(KT):
                for t in range(TT):
                    c0 = (k % 2) * SEQ + t * P
                    tr = nc.tensor.transpose(aux[:, k // 2, c0:c0 + P], xn[:, t, k * P:(k + 1) * P], ident[:])
                if k % 2:
                    tr.then_inc(turned, 1)

        def norm_act_hi(act, n, count, slot, dst):
            for k in range(KT):
                if k % 2 == 0:
                    act.wait_ge(turned, 4 * n + k // 2 + 1)
                nc.scalar.activation(dst[:, k, :], aux[:, k // 2, (k % 2) * SEQ:(k % 2 + 1) * SEQ], ACT.Copy,
                                     scale=gains[:, slot, k:k + 1]).then_inc(norm_hi, 1)

        def norm_dve_lo(dve, count, slot, dst, hi):
            for k in range(KT):
                if k % 2 == 0:
                    dve.wait_ge(norm_hi, KT * count + k + 2)
                nc.vector.scalar_tensor_tensor(dst[:, k, :], aux[:, k // 2, (k % 2) * SEQ:(k % 2 + 1) * SEQ],
                                               gains[:, slot, k:k + 1], hi[:, k, :].bitcast(F32),
                                               ALU.mult, ALU.subtract).then_inc(norm_lo, 1)

        def norm_taken(pe, count):
            pe.wait_ge(norm_lo, KT * (count + 1))

        batches1 = ["sb", "d0", "d1", "d2", "fox", "diff0", "diff1"]

        block = ctx.enter_context(nc.Block())

        @block.sync
        def _(sp):
            sp.dma_start(x[:], io["x"].rearrange("(t p) d -> p t d", p=P)).then_inc(x_in, 16)
            sp.dma_start(ident[:], io["ident"]).then_inc(const_in, 16)
            sp.dma_start(gains[:], io["gains"]).then_inc(const_in, 16)
            for s in range(SLOTS):
                sp.dma_start(raw[:, s, :], io["stream"][s]).then_inc(full[s], 16)
            with sp.Fori(1, N_CHUNKS // SLOTS) as it:
                for s in range(SLOTS):
                    c = At(s, SLOTS, it)
                    wait(sp, lo_ready, c - (SLOTS - 1))
                    sp.dma_start(raw[:, s, :], io["stream"][bass.ds(c.value, 1)].rearrange("a p n -> p (a n)")
                                 ).then_inc(full[s], 16)
            sp.wait_ge(post_done, 4 * TT)
            sp.dma_start(io["out"].rearrange("(t p) d -> p t d", p=P), x[:]).then_inc(y_out, 16)
            sp.wait_ge(y_out, 16)

        @block.gpsimd
        def _(pool):
            g = nc.gpsimd

            def load(dst, src, s):
                pool.dma_start(dst, src).then_inc(s, 16)

            load(w_f[:], io["w_f"], table_in)
            load(tri[:], io["tri"], table_in)
            load(b_f[:], io["b_forget"].rearrange("(a n) -> a n", a=1).broadcast_to([P, 4]), table_in)
            load(lams[:], io["lams"].rearrange("(a m) n -> a m n", a=1).broadcast_to([P, 4, 32]), table_in)
            load(diff_g[:], io["diff_g"].rearrange("(a n) -> a n", a=1).broadcast_to([P, HD]), table_in)
            load(bias_b[:, 0], io["bias1"][0], bias_in[0])
            load(bias_b[:, 1], io["bias1"][1], bias_in[1])
            load(w_gate[:], io["w_gate"], table_in)
            load(w2k[:], io["w2k"], table_in)
            load(w2v[:], io["w2v"], table_in)
            g.memset(mhalf[:], -0.5).then_inc(setup, 1)
            g.memset(small[:, 6, 0:1], 0.0).then_inc(hid_lo, 1)
            g.memset(small[:, 6, 1:2], 0.0).then_inc(hid_lo, 1)
            g.memset(ones[:], 1.0).then_inc(setup, 1)
            pool.wait_ge(setup, 1)
            norm_pool(pool, 0)
            for b in range(2, 7):
                pool.wait_ge(scores_out, b - 1)
                load(bias_b[:, b % 2], io["bias1"][b], bias_in[b % 2])
            pool.wait_ge(ro_sq, 1)
            g.tensor_scalar(small[:, 0, :], small[:, 1, :], 1.0 / HD, EPS, ALU.mult, ALU.add).then_inc(rstd_step, 1)
            pool.wait_ge(rstd_step, 2)
            g.tensor_tensor(small[:, 2, :], small[:, 0, :], mhalf[:], ALU.pow).then_inc(ro_r, 1)
            for n in range(1, 3):
                for j in range(4):
                    group_out(pool, GROUP["branch"] + 4 * n + j)
                    if n == 2:
                        pool.wait_ge(mix_sum, j + 1)
                    a, b = gate[:, 2 * j:2 * j + 2, :], gate[:, n * KT + 2 * j:n * KT + 2 * j + 2, :]
                    g.tensor_tensor(a, a, b, ALU.add).then_inc(mix_sum, 1)
            norm_pool_steps = [1]

            def norm(n):
                pool.wait_ge(squares, TT * (n + 1))
                g.tensor_scalar(means[:], sums[:, 0:TT], 1.0 / D, EPS, ALU.mult, ALU.add).then_inc(rstd_step, 1)
                norm_pool_steps[0] += 1
                pool.wait_ge(rstd_step, norm_pool_steps[0] + 1)
                g.tensor_tensor(rstd[:], means[:], mhalf[:, 0:TT], ALU.pow).then_inc(rstd_ready, 1)

            def hid_lo_step(dst_l, full_value, dst_h, n):
                wait(pool, hid_hi, n + 1)
                g.tensor_tensor(dst_l, full_value, dst_h.bitcast(F32), ALU.subtract).then_inc(hid_lo, 1)

            norm(1)
            with pool.Fori(0, 4) as it:
                for s in range(4):
                    n = At(s, 4, it)
                    tile = bass.ds((n * 2).value, 2)
                    hid_lo_step(hid1l[:, tile, :], r1[:, s % 2, 1], hid1h[:, tile, :], n)
            load(grow1[:], io["grows"][0:1, :].broadcast_to([P, D]), grow_in[0])
            pool.wait_ge(squares, TT * 3)
            g.tensor_scalar(means[:], sums[:, 0:TT], 1.0 / D, EPS, ALU.mult, ALU.add).then_inc(rstd_step, 1)
            norm_pool_steps[0] += 1
            pool.wait_ge(rstd_step, norm_pool_steps[0] + 1)
            g.tensor_tensor(rstd[:], means[:], mhalf[:, 0:TT], ALU.pow).then_inc(rstd_ready, 1)
            pool.wait_ge(mm_done, START["ret"])
            load(cs[:], io["cs"], ret_const)
            load(decay[:], io["decay"], ret_const)
            load(grow0[:], io["grows"][1:2, :].broadcast_to([P, D]), grow_in[1])
            norm(3)
            for h in range(RET_HEADS):
                for i in range(2):
                    n = 2 * h + i
                    group_out(pool, GROUP["ret"] + 6 * h + i)
                    dst = (rq, rk)[i]
                    if h:
                        pool.wait_ge(st_done, h)
                    g.tensor_tensor(dst[:, 0, :], ra[:, 0, 0, :], ra[:, 1, 1, :], ALU.subtract)
                    g.tensor_tensor(dst[:, 1, :], ra[:, 1, 0, :], ra[:, 0, 1, :], ALU.add).then_inc(rot_out, 1)
                pool.wait_ge(ro_sq, 1 + 2 * (h + 1))
                g.tensor_scalar(small[:, 3, 0:2], small[:, 4, 0:2], 1.0 / RET_DV, EPS, ALU.mult, ALU.add
                                ).then_inc(rstd_step, 1)
                norm_pool_steps[0] += 1
                pool.wait_ge(rstd_step, norm_pool_steps[0] + 1)
                g.tensor_tensor(small[:, 5, 0:2], small[:, 3, 0:2], mhalf[:, 0:2], ALU.pow).then_inc(ro_r, 1)

            def post(n, mixed, grow):
                pool.wait_ge(grow_in[n + 1], 16)
                for cb in range(4):
                    pool.wait_ge(post_sq, 8 * n + 2 * cb + 2)
                    cols = slice(cb * CW, (cb + 1) * CW)
                    for t in range(TT):
                        ins = g.tensor_tensor(mixed[:, t, cols], mixed[:, t, cols], grow[:, cols], ALU.mult)
                ins.then_inc(post_g, 1)
                pool.wait_ge(post_step, n + 1)
                g.tensor_scalar(means[:], psum1[:], 1.0 / D, EPS, ALU.mult, ALU.add).then_inc(rstd_step, 1)
                norm_pool_steps[0] += 1
                pool.wait_ge(rstd_step, norm_pool_steps[0] + 1)
                g.tensor_tensor(rstd[:], means[:], mhalf[:, 0:TT], ALU.pow).then_inc(post_r, 1)

            def ffn_pool(layer):
                n0 = 16 + FFN_KT * layer
                with pool.Fori(0, 5) as it:
                    for s in range(4):
                        n = At(n0 + s, 4, it)
                        tile = bass.ds((At(s, 4, it)).value, 1)
                        hid_lo_step(hid2l[:, tile, :], ft[:, s % 2:s % 2 + 1, :], hid2h[:, tile, :], n)
                for s in range(20, 22):
                    hid_lo_step(hid2l[:, s:s + 1, :], ft[:, s % 2:s % 2 + 1, :], hid2h[:, s:s + 1, :], At(n0 + s))

            post(0, mixed0, grow0)
            pool.wait_ge(post_done, TT)
            load(grow2[:], io["grows"][2:3, :].broadcast_to([P, D]), grow_in[2])
            norm(4)
            ffn_pool(0)
            post(1, mixed2, grow2)
            pool.wait_ge(mm_done, START["kv"])
            pool.wait_ge(post_done, 2 * TT)
            load(relb[0:32, :], io["rel_bias"], nsa_const)
            load(relb[32:33, :], io["masked"], nsa_const)
            load(hot[:], io["hot"], nsa_const)
            load(pe_in[:], io["pe_in"], nsa_const)
            load(flip[:], io["flip"], nsa_const)
            load(chot[:], io["chot"], nsa_const)
            norm(5)
            pool.wait_ge(strip_out, 1)
            pool.wait_ge(cb_out, 1)
            load(io["strip"], stripsb[:], strip_io)
            pool.wait_ge(strip_io, 16)
            load(nbias[:], bass.AP(io["strip"].tensor, 0, [[1, P], [384, 16], [1, SEQ]]), nbias_in)
            pool.wait_ge(nys_lo, KT)
            load(growb[:], io["grows"][3:4, :].broadcast_to([P, D]), grow_in[3])
            post(2, mixed1, growb)
            pool.wait_ge(post_done, 3 * TT)
            load(grow2[:], io["grows"][4:5, :].broadcast_to([P, D]), grow_in[4])
            norm(6)
            ffn_pool(1)
            post(3, mixed2, grow2)

        @block.scalar
        def _(act):
            a = nc.scalar
            for c in range(AHEAD):
                split_hi(act, c)
            norm_act_squares(act, 0, [(x_in, 16)])
            act.wait_ge(const_in, 16 * 2)
            norm_act_hi(act, 0, 0, 0, hh)
            act.wait_ge(dve_step, 2)
            a.activation(lam[:, 2:4], lam[:, 0:2], ACT.Exp).then_inc(act_step, 1)
            act.wait_ge(f_in, 1)
            a.activation(fsmall[:, 1], fsmall[:, 0], ACT.Abs).then_inc(f_e, 1)
            act.wait_ge(f_e, 1)
            a.activation(fsmall[:, 1], fsmall[:, 1], ACT.Exp, scale=-1.0).then_inc(f_e, 1)
            act.wait_ge(f_e, 2)
            a.activation(fsmall[:, 1], fsmall[:, 1], ACT.Ln, bias=1.0).then_inc(f_e, 1)

            def q_out(p):
                g = GROUP["qkv"] + 3 * p
                act.wait_ge(mm_done, 3 * p + 1)
                wait(act, scores_done, p - 1)
                bank = acc[g % 2]
                if p < 5:
                    for half in range(2):
                        ins = a.activation(
                            q_b[:, p % 2].rearrange("p (s h) n -> p s h n", h=2)[:, :, half, :],
                            bank[HD * half:HD * half + HD, :].rearrange("p (s n) -> p s n", s=2),
                            ACT.Copy, scale=HD ** -0.5)
                    ins.then_inc(acc_out[g % 2], 1)
                else:
                    act.wait_ge(scores_done, 5)
                    for head in range(4):
                        for comp in range(2):
                            ins = a.activation(q_b[0:32, (p + comp) % 2, head, :],
                                               bank[32 * head:32 * head + 32, comp * SEQ:(comp + 1) * SEQ],
                                               ACT.Copy, scale=32 ** -0.5)
                    ins.then_inc(acc_out[g % 2], 1)

            def v_out(p):
                g = GROUP["qkv"] + 3 * p + 2
                act.wait_ge(mm_done, 3 * p + 3)
                wait(act, pv_done, p - 1)
                a.activation(v_b[:, p % 2].rearrange("p t n -> p (t n)"), acc[g % 2][:],
                             ACT.Copy).then_inc(acc_out[g % 2], 1)

            def exps(b):
                if b == 0:
                    t = pt_b1[:].rearrange("p a n -> p (a n)")
                    act.wait_ge(scores_out, 1)
                    a.activation(t, s_b1[:], ACT.Abs).then_inc(sb_l, 1)
                    act.wait_ge(sb_l, 1)
                    a.activation(t, t, ACT.Exp, scale=-1.0).then_inc(sb_l, 1)
                    act.wait_ge(sb_l, 2)
                    a.activation(t, t, ACT.Ln, bias=1.0).then_inc(sb_l, 1)
                    act.wait_ge(sb_e, 1)
                    a.activation(s_b1[:], s_b1[:], ACT.Exp).then_inc(probs_ready, 1)
                    return
                act.wait_ge(probs_max, 2 * b)
                for t in range(TT):
                    for h in range(4):
                        w = P * (t + 1)
                        lo = h * P if t == 0 else 512 + h * SEQ
                        ins = a.activation(s_b1[:, lo:lo + w], s_b1[:, lo:lo + w], ACT.Exp,
                                           bias=negmax[:, b, 4 * t + h:4 * t + h + 1],
                                           accum_out=rowsum[:, b, 4 * t + h:4 * t + h + 1])
                ins.then_inc(probs_ready, 1)

            def pt_out(b):
                for j in range(3):
                    act.wait_ge(probs_turned, 3 * b + j + 1)
                    a.activation(pt_b1[:, j, :], aux[:, (3, 4, 0)[j], :], ACT.Copy).then_inc(pt_ready, 1)

            for p in range(6):
                split_hi(act, 3 * p + 3)
                q_out(p)
                split_hi(act, 3 * p + 4)
                if p:
                    pt_out(p - 1)
                split_hi(act, 3 * p + 5)
                v_out(p)
                exps(p)
                if p == 4:
                    act.wait_ge(sb_c, 1)
                    a.activation(small[:, 2:5, :], small[:, 2:5, :], ACT.Exp).then_inc(act_step, 1)

            def gate_out(c):
                n = c - START["gates"]
                g = n + GROUP["gates"]
                wait(act, mm_done, c + 1)
                a.activation(gate[:, bass.ds((n * 2).value, 2), :].rearrange("p k n -> p (k n)"), acc[g.mod(2)][:],
                             ACT.Sigmoid).then_inc(acc_out[g.mod(2)], 1)

            c = START["gates"]
            split_hi(act, c + 3)
            gate_out(At(c))
            pt_out(5)
            split_hi(act, c + 4)
            gate_out(At(c + 1))
            split_hi(act, c + 5)
            exps(6)
            gate_out(At(c + 2))
            pt_out(6)
            split_hi(act, c + 6)
            gate_out(At(c + 3))
            with act.Fori(0, 3) as it:
                for s in range(4):
                    cc = At(c + 4 + s, 4, it)
                    split_hi(act, cc + 3)
                    gate_out(cc)
            for k in range(KT):
                if k % 2 == 0:
                    act.wait_ge(ys_turned, k // 2 + 1)
                a.activation(ysh1[:, k, :], aux[:, k // 2, (k % 2) * SEQ:(k % 2 + 1) * SEQ], ACT.Copy).then_inc(ys_hi, 1)
            for i in range(4):
                split_hi(act, START["branch"] + i + 3)
            for j in range(4):
                act.wait_ge(mix_ready, j + 1)
                a.activation(hh[:, 2 * j:2 * j + 2, :], gate[:, 2 * j:2 * j + 2, :], ACT.Copy).then_inc(norm_hi, 1)
            for i in range(4):
                split_hi(act, START["out"] + i + 3)

            def norm(n, extra, slot, dst, x_waits):
                norm_act_squares(act, n, x_waits)
                hi_part(n, slot, dst)

            def hi_part(n, slot, dst):
                m = n if n < 3 else n - 1
                for k in range(KT):
                    if k % 2 == 0:
                        act.wait_ge(turned, 4 * m + k // 2 + 1)
                    a.activation(dst[:, k, :], aux[:, k // 2, (k % 2) * SEQ:(k % 2 + 1) * SEQ], ACT.Copy,
                                 scale=gains[:, slot, k:k + 1]).then_inc(norm_hi, 1)

            def x_after(name):
                g = GROUP[name] + GROUP_COUNT[name] - 1
                return [(acc_out[g % 2], g // 2 + 1), (acc_out[(g - 1) % 2], (g - 1) // 2 + 1)]

            norm(1, 4, 1, hh, x_after("out"))
            with act.Fori(0, 4) as it:
                for s in range(4):
                    c = At(START["up"] + s, 4, it)
                    n = At(s, 4, it)
                    g = At(GROUP["up"] + s, 4, it)
                    split_hi(act, c + 3)
                    wait(act, mm_done, c + 1)
                    a.activation(r1[:, s % 2, 0].rearrange("p a n -> p (a n)"), acc[g.mod(2)][:], ACT.Relu
                                 ).then_inc(acc_out[g.mod(2)], 1)
                    wait(act, sq_ready, n + 1)
                    a.activation(hid1h[:, bass.ds((n * 2).value, 2), :], r1[:, s % 2, 1], ACT.Copy).then_inc(hid_hi, 1)
            for i in range(16):
                split_hi(act, START["down"] + i + 3)
            norm_act_squares(act, 2, x_after("down"))
            norm(3, 0, 2, hh, [(first_done, TT)])
            for h in range(RET_HEADS):
                c0, g0 = START["ret"] + 6 * h, GROUP["ret"] + 6 * h
                for i in range(6):
                    split_hi(act, c0 + i + 3)
                    g = g0 + i
                    if i in (2, 3):
                        act.wait_ge(mm_done, c0 + i + 1)
                        wait(act, ro_done, 2 * h)
                        a.activation(rv[:, :, (i - 2) * CW:(i - 1) * CW],
                                     acc[g % 2][:].rearrange("p (t n) -> p t n", t=2), ACT.Copy).then_inc(acc_out[g % 2], 1)
                    if i in (4, 5):
                        act.wait_ge(mm_done, c0 + i + 1)
                        wait(act, ro_y, 2 * h)
                        a.activation(rg[:, :, (i - 4) * CW:(i - 3) * CW],
                                     acc[g % 2][:].rearrange("p (t n) -> p t n", t=2), ACT.Silu).then_inc(acc_out[g % 2], 1)
                    if i == 4:
                        for t in range(TT):
                            act.wait_ge(ro_done, 2 * h + t + 1)
                            wait(act, ry_turned, 2 * h)
                            a.activation(ry[:, t, :], aux[:, 3 + t, :], ACT.Square,
                                         accum_out=small[:, 4, t:t + 1]).then_inc(ro_sq, 1)
                for kk in range(4):
                    if kk % 2 == 0:
                        act.wait_ge(ry_turned, 2 * h + kk // 2 + 1)
                    a.activation(yth[:, 4 * h + kk, :], aux[:, 1 + kk // 2, (kk % 2) * SEQ:(kk % 2 + 1) * SEQ],
                                 ACT.Copy).then_inc(yt_hi, 1)

            def post(n, name, per, mixed, junk):
                c0 = START[name]
                for cb in range(4):
                    for i in range(per):
                        split_hi(act, c0 + per * cb + i + 3)
                    group_out(act, GROUP[name] + cb)
                    wait(act, post_sq, 8 * n + 2 * cb)
                    for t in range(TT):
                        a.activation(junk[:, t, 0:CW], mixed[:, t, cb * CW:(cb + 1) * CW], ACT.Square,
                                     accum_out=psums[:, t, cb:cb + 1]).then_inc(post_sq, 1)

            def ffn_act(layer):
                name = f"ffn_in_{layer}"
                n0 = 16 + FFN_KT * layer

                def one(c, g, n, s, tile, first):
                    split_hi(act, c + 3)
                    wait(act, mm_done, c + 1)
                    a.activation(fsil[:, s % 2, :], acc[g.mod(2)][:, 0:SEQ], ACT.Silu).then_inc(sil_out, 1)
                    group_out(act, g)
                    a.activation(hid2h[:, tile, :], ft[:, s % 2:s % 2 + 1, :], ACT.Copy).then_inc(hid_hi, 1)
                with act.Fori(0, 5) as it:
                    for s in range(4):
                        one(At(START[name] + s, 4, it), At(GROUP[name] + s, 4, it), At(n0 + s, 4, it), s,
                            bass.ds(At(s, 4, it).value, 1), False)
                for s in range(20, 22):
                    one(At(START[name] + s), At(GROUP[name] + s), At(n0 + s), s, slice(s, s + 1), False)

            post(0, "ret_out", 2, mixed0, ry)
            norm(4, 0, 3, hh, [(post_done, TT)])
            ffn_act(0)
            post(1, "ffn_out_0", 3, mixed2, ft)
            norm_act_squares(act, 5, [(post_done, 2 * TT)])
            for k in range(0, KT, 2):
                act.wait_ge(turned, 4 * 4 + k // 2 + 1)
                for slot, dst in ((6, kvh), (4, hh)):
                    for kk in (k, k + 1):
                        a.activation(dst[:, kk, :], aux[:, kk // 2, (kk % 2) * SEQ:(kk % 2 + 1) * SEQ], ACT.Copy,
                                     scale=gains[:, slot, kk:kk + 1]).then_inc(norm_hi, 1)
            for i in range(6):
                split_hi(act, START["kv"] + i + 3)
                if i == 1:
                    act.wait_ge(ng_mm, 1)
                    a.activation(gate_f[:].rearrange("p t n -> p (t n)"), aux[:, 0, 0:96], ACT.Sigmoid).then_inc(ng_out, 1)
            for i in range(4):
                split_hi(act, START["cmp"] + i + 3)
                if i in (1, 3):
                    j = i // 2
                    act.wait_ge(cmp_b, j + 1)
                    for sub in range(2):
                        a.activation(hidc[:, j, sub, :], aux[:, 2 * j + sub, 0:60], ACT.Silu,
                                     bias=peb[:, j, sub:sub + 1]).then_inc(cmp_hid, 1)
            for i in range(4):
                split_hi(act, START["nsa_q"] + i + 3)
                g = GROUP["nsa_q"] + i
                act.wait_ge(mm_done, START["nsa_q"] + i + 1)
                bank = acc[g % 2]
                for half in range(2):
                    ins = a.activation(nq[:, i].rearrange("p (s h) (t n) -> p s h t n", h=2, t=2)[:, :, half],
                                       backwards(bank[HD * half:HD * half + HD, :]
                                                 .rearrange("p (s t n) -> p s t n", s=2, t=2)),
                                       ACT.Copy, scale=HD ** -0.5)
                ins.then_inc(acc_out[g % 2], 1)

            def n_exps(b):
                act.wait_ge(n_max, b + 1)
                for t in range(TT):
                    for h in range(4):
                        if b >= 8:
                            lo, w = (t * 4 + h) * N_CMP, N_CMP
                        else:
                            w = P * (t + 1)
                            lo = h * P if t == 0 else 512 + h * SEQ
                        ins = a.activation(ns[:, b % 2, lo:lo + w], ns[:, b % 2, lo:lo + w], ACT.Exp,
                                           bias=negmax[:, b % 4, 4 * t + h:4 * t + h + 1],
                                           accum_out=rowsum[:, b % 4, 4 * t + h:4 * t + h + 1])
                ins.then_inc(n_exp, 1)

            n_exps(0)
            for b in range(12):
                if b + 1 < 12:
                    n_exps(b + 1)
                for j in range(3 if b < 8 else 2):
                    act.wait_ge(n_turn, n_turns_before(b) + j + 1)
                    if b >= 8:
                        a.activation(npt[0:N_CMP, j, :], aux[0:N_CMP, 3 + j, :], ACT.Copy).then_inc(n_pt, 1)
                    else:
                        a.activation(npt[:, j, :], n_turn_bank(j), ACT.Copy).then_inc(n_pt, 1)
            for k in range(KT):
                if k % 2 == 0:
                    act.wait_ge(nys_turned, k // 2 + 1)
                a.activation(ysh2[:, k, :].rearrange("p (t n) -> p t n", t=2), turned_back(k), ACT.Copy).then_inc(nys_hi, 1)
            post(2, "nsa_out", 1, mixed1, o_n)
            norm(6, 0, 5, hh, [(post_done, 3 * TT)])
            ffn_act(1)
            post(3, "ffn_out_1", 3, mixed2, ft)

        @block.vector
        def _(dve):
            v = nc.vector
            steps = [0]

            def chain(ins):
                steps[0] += 1
                ins.then_inc(dve_step, 1)
                dve.wait_ge(dve_step, steps[0])

            for c in range(AHEAD):
                split_lo(dve, c)
            norm_dve_scale(dve, 0)
            dve.wait_ge(const_in, 16 * 2)
            norm_dve_lo(dve, 0, 0, hl, hh)
            dve.wait_ge(table_in, 16 * 8)
            chain(v.tensor_tensor(lamp[:], lams[:, 0:4:2, :], lams[:, 1:4:2, :], ALU.mult))
            chain(v.tensor_reduce(lam[:, 0:2], lamp[:], AX_X, ALU.add))
            dve.wait_ge(f_done, 1)
            v.tensor_tensor(fsmall[:, 0], aux[:, 4, 0:8].rearrange("p (t h) -> p t h", t=2),
                            b_f[:].rearrange("p (a h) -> p a h", a=1).broadcast_to([P, 2, 4]), ALU.add).then_inc(f_in, 1)
            dve.wait_ge(f_e, 3)
            v.scalar_tensor_tensor(logf[:], fsmall[:, 0], 0.0, fsmall[:, 1], ALU.min, ALU.subtract).then_inc(f_ready, 1)
            dve.wait_ge(act_step, 1)
            chain(v.tensor_tensor(lam[:, 4:5], lam[:, 2:3], lam[:, 3:4], ALU.subtract))
            chain(v.tensor_scalar(lam[:, 5:6], lam[:, 4:5], LAMBDA_INIT, -1.0, ALU.add, ALU.mult))
            dve.wait_ge(cum_done, 1)
            row = aux[0:1, 3:5, :].rearrange("p a (h n) -> p (a h) n", h=2)
            v.tensor_copy(cumrow[:, 0], row)
            v.tensor_scalar(cumrow[:, 1], row, -1.0, None, ALU.mult).then_inc(cum_out, 1)

            def k_out(p):
                g = GROUP["qkv"] + 3 * p + 1
                dve.wait_ge(mm_done, 3 * p + 2)
                wait(dve, scores_done, p - 1)
                bank = acc[g % 2]
                if p < 5:
                    for half in range(2):
                        ins = v.tensor_copy(k_b[:, p % 2].rearrange("p (s h) n -> p s h n", h=2)[:, :, half, :],
                                            bank[HD * half:HD * half + HD, :].rearrange("p (s n) -> p s n", s=2))
                    ins.then_inc(acc_out[g % 2], 1)
                else:
                    dve.wait_ge(scores_done, 5)
                    for head in range(4):
                        for comp in range(2):
                            ins = v.tensor_copy(k_b[0:32, (p + comp) % 2, head, :],
                                                bank[32 * head:32 * head + 32, comp * SEQ:(comp + 1) * SEQ])
                    ins.then_inc(acc_out[g % 2], 1)

            def heads(ap):
                return ap.rearrange("p (h n) -> p h n", h=4)

            def softmax_in(b):
                dve.wait_ge(scores_done, b + 1)
                dve.wait_ge(bias_in[b % 2], 16 * (b // 2 + 1))
                wait(dve, probs_turned, 3 * b)
                bias = bias_b[:, b % 2]
                chain(v.tensor_tensor(heads(s_b1[:, 0:512]), heads(aux[:, 0, :]), bias[:, :, P:SEQ], ALU.add))
                ins = v.tensor_tensor(s_b1[:, 512:1536].rearrange("p (h n) -> p h n", h=4),
                                      aux[:, 1:3, :].rearrange("p a (h n) -> p (a h) n", h=2), bias, ALU.add)
                ins.then_inc(scores_out, 1)
                dve.wait_ge(scores_out, b + 1)
                if b == 0:
                    t = pt_b1[:].rearrange("p a n -> p (a n)")
                    dve.wait_ge(sb_l, 3)
                    chain(v.scalar_tensor_tensor(t, s_b1[:], 0.0, t, ALU.max, ALU.add))
                    for tt in range(TT):
                        for h in range(4):
                            w = P * (tt + 1)
                            lo = h * P if tt == 0 else 512 + h * SEQ
                            seg = t[:, lo:lo + w][:, ::-1]
                            ins = v.tensor_tensor_scan(seg, seg, seg, 0.0, ALU.add, ALU.max)
                    chain(ins)
                    v.tensor_tensor(s_b1[:], s_b1[:], t, ALU.subtract).then_inc(sb_e, 1)
                    return
                v.tensor_reduce(negmax[:, b, 0:4], heads(s_b1[:, 0:512]), AX_X, ALU.max, negate=True).then_inc(probs_max, 1)
                v.tensor_reduce(negmax[:, b, 4:8], heads(s_b1[:, 512:1536]), AX_X, ALU.max, negate=True).then_inc(probs_max, 1)

            def cols(ap, branch):
                return ap[:, :, branch * CW:(branch + 1) * CW].rearrange("p t (h d) -> p t h d", h=4)

            def per_row(c):
                return c.rearrange("p (t h a) -> p t h a", t=2, a=1).broadcast_to([P, 2, 4, HD])

            def o_bank():
                return aux[:, 5, :].rearrange("p (t h d) -> p t h d", t=2, h=4)

            def og_of(i):
                return og[:, i].rearrange("p t (h d) -> p t h d", h=4)

            def attn_out(b):
                dve.wait_ge(pv_done, b + 1)
                if b == 0:
                    v.tensor_copy(cols(ys1, 0), o_bank()).then_inc(o_out, 1)
                elif b < 4:
                    v.tensor_copy(og_of(b - 1), o_bank()).then_inc(o_out, 1)
                elif b == 4:
                    chain(v.reciprocal(coef[:, 4, :], rowsum[:, 4, :]))
                    v.tensor_tensor(cols(ys1, 2), o_bank(), per_row(coef[:, 4, :]), ALU.mult).then_inc(o_out, 1)
                elif b == 5:
                    chain(v.reciprocal(coef[:, 5, :], rowsum[:, 5, :]))
                    v.tensor_tensor(og_of(0), o_bank(), per_row(coef[:, 5, :]), ALU.mult).then_inc(o_out, 1)
                else:
                    chain(v.reciprocal(coef[:, 6, :], rowsum[:, 6, :]))
                    chain(v.tensor_scalar(coef[:, 7, :], coef[:, 6, :], lam[:, 5:6], None, ALU.mult))
                    v.tensor_tensor(og_of(1), o_bank(), per_row(coef[:, 7, :]), ALU.mult).then_inc(o_out, 1)

            def dilated():
                m = small[:, 0, :]
                dve.wait_ge(o_out, 4)
                chain(v.tensor_tensor(small[:, 1, :], negmax[:, 1, :], negmax[:, 2, :], ALU.min))
                chain(v.tensor_tensor(m, small[:, 1, :], negmax[:, 3, :], ALU.min))
                for i in range(3):
                    ins = v.tensor_tensor(small[:, 2 + i, :], m, negmax[:, 1 + i, :], ALU.subtract)
                ins.then_inc(sb_c, 1)
                dve.wait_ge(act_step, 2)
                for i in range(3):
                    ins = v.tensor_tensor(small[:, 5 + i, :], small[:, 2 + i, :], rowsum[:, 1 + i, :], ALU.mult)
                chain(ins)
                chain(v.tensor_tensor(small[:, 5, :], small[:, 5, :], small[:, 6, :], ALU.add))
                chain(v.tensor_tensor(small[:, 5, :], small[:, 5, :], small[:, 7, :], ALU.add))
                chain(v.reciprocal(small[:, 6, :], small[:, 5, :]))
                for i in range(3):
                    ins = v.tensor_tensor(coef[:, i, :], small[:, 2 + i, :], small[:, 6, :], ALU.mult)
                chain(ins)
                for i in range(3):
                    ins = v.tensor_tensor(og_of(i), og_of(i), per_row(coef[:, i, :]), ALU.mult)
                chain(ins)
                chain(v.tensor_tensor(og[:, 0], og[:, 0], og[:, 1], ALU.add))
                chain(v.tensor_tensor(ys1[:, :, CW:2 * CW], og[:, 0], og[:, 2], ALU.add))

            def differential():
                dve.wait_ge(o_out, 7)
                chain(v.tensor_tensor(og[:, 2], og[:, 0], og[:, 1], ALU.add))
                chain(v.tensor_tensor(og[:, 0], og[:, 2], og[:, 2], ALU.mult))
                v.tensor_reduce(small[:, 1, :], og_of(0).rearrange("p t h d -> p (t h) d"), AX_X, ALU.add).then_inc(ro_sq, 1)
                chain(v.tensor_tensor(og_of(1), og_of(2), diff_g[:].rearrange("p (a b d) -> p a b d", a=1, b=1)
                                      .broadcast_to([P, 2, 4, HD]), ALU.mult))
                dve.wait_ge(ro_r, 1)
                chain(v.tensor_scalar(small[:, 3, :], small[:, 2, :], 1.0 - LAMBDA_INIT, None, ALU.mult))
                v.tensor_tensor(cols(ys1, 3), og_of(1), per_row(small[:, 3, :]), ALU.mult).then_inc(ys_ready, 1)

            for p in range(6):
                split_lo(dve, 3 * p + 3)
                split_lo(dve, 3 * p + 4)
                k_out(p)
                split_lo(dve, 3 * p + 5)
                if p:
                    attn_out(p - 1)
                softmax_in(p)
                if p == 4:
                    dilated()
            c = START["gates"]
            split_lo(dve, c + 3)
            split_lo(dve, c + 4)
            attn_out(5)
            softmax_in(6)
            split_lo(dve, c + 5)
            split_lo(dve, c + 6)
            attn_out(6)
            differential()
            with dve.Fori(0, 3) as it:
                for s in range(4):
                    split_lo(dve, At(c + 7 + s, 4, it))
            for k in range(KT):
                if k % 2 == 0:
                    dve.wait_ge(ys_hi, k + 2)
                v.tensor_tensor(ysl1[:, k, :], aux[:, k // 2, (k % 2) * SEQ:(k % 2 + 1) * SEQ],
                                ysh1[:, k, :].bitcast(F32), ALU.subtract).then_inc(ys_lo, 1)
            for n in range(4):
                split_lo(dve, START["branch"] + n + 3)
                for j in range(4):
                    g = GROUP["branch"] + 4 * n + j
                    if j < 3:
                        dve.wait_ge(branch_done, 3 * n + j + 1)
                    else:
                        dve.wait_ge(mm_done, START["branch"] + n + 1)
                    if n == 0:
                        group_out(dve, GROUP["gates"] + 14)
                        group_out(dve, GROUP["gates"] + 15)
                    gg = gate[:, n * KT + 2 * j:n * KT + 2 * j + 2, :].rearrange("p k n -> p (k n)")
                    v.tensor_tensor(gg, gg, acc[g % 2][:], ALU.mult).then_inc(acc_out[g % 2], 1)
                    if n == 3:
                        dve.wait_ge(mix_sum, 4 + j + 1)
                        dve.wait_ge(acc_out[g % 2], g // 2 + 1)
                        aa = gate[:, 2 * j:2 * j + 2, :]
                        v.tensor_tensor(aa, aa, gate[:, n * KT + 2 * j:n * KT + 2 * j + 2, :], ALU.add).then_inc(mix_ready, 1)
                        dve.wait_ge(norm_hi, KT + j + 1)
                        v.tensor_tensor(hl[:, 2 * j:2 * j + 2, :], aa, hh[:, 2 * j:2 * j + 2, :].bitcast(F32),
                                        ALU.subtract).then_inc(norm_lo, 1)

            def add_to_x(name, per):
                c0, g0 = START[name], GROUP[name]
                for cb in range(4):
                    for i in range(per):
                        split_lo(dve, c0 + per * cb + i + 3)
                    g = g0 + cb
                    dve.wait_ge(mm_done, c0 + per * (cb + 1))
                    xs = x[:, :, cb * CW:(cb + 1) * CW]
                    v.tensor_tensor(xs, xs, acc[g % 2][:].rearrange("p (t n) -> p t n", t=2), ALU.add
                                    ).then_inc(acc_out[g % 2], 1)

            def lo_part(slot, dst, hi, before):
                for k in range(KT):
                    if k % 2 == 0:
                        dve.wait_ge(norm_hi, before + k + 2)
                    v.scalar_tensor_tensor(dst[:, k, :], aux[:, k // 2, (k % 2) * SEQ:(k % 2 + 1) * SEQ],
                                           gains[:, slot, k:k + 1], hi[:, k, :].bitcast(F32),
                                           ALU.mult, ALU.subtract).then_inc(norm_lo, 1)

            add_to_x("out", 1)
            norm_dve_scale(dve, 1)
            lo_part(1, hl, hh, 12)
            with dve.Fori(0, 4) as it:
                for s in range(4):
                    c = At(START["up"] + s, 4, it)
                    n = At(s, 4, it)
                    g = At(GROUP["up"] + s, 4, it)
                    split_lo(dve, c + 3)
                    wait(dve, acc_out[g.mod(2)], g.div(2) + 1)
                    wait(dve, hid_lo, n + 1)
                    rr = r1[:, s % 2, 0]
                    v.tensor_tensor(r1[:, s % 2, 1], rr, rr, ALU.mult).then_inc(sq_ready, 1)
            add_to_x("down", 4)
            dve.wait_ge(rstd_ready, 3)
            dve.wait_ge(grow_in[0], 16)
            for t in range(TT):
                v.scalar_tensor_tensor(x[:, t, :], x[:, t, :], rstd[:, t:t + 1], grow1[:], ALU.mult,
                                       ALU.mult).then_inc(first_done, 1)
            xn_scaled = [2]

            def scale(n_ready):
                dve.wait_ge(rstd_ready, n_ready)
                for t in range(TT):
                    v.tensor_scalar(xn[:, t, :], x[:, t, :], rstd[:, t:t + 1], None, ALU.mult).then_inc(xn_ready, 1)

            scale(4)
            lo_part(2, hl, hh, 20)
            dve.wait_ge(ret_const, 32)
            for h in range(RET_HEADS):
                c0, g0 = START["ret"] + 6 * h, GROUP["ret"] + 6 * h
                for i in range(6):
                    split_lo(dve, c0 + i + 3)
                    g = g0 + i
                    if i < 2:
                        dve.wait_ge(mm_done, c0 + i + 1)
                        wait(dve, rot_out, 2 * h + i)
                        both = acc[g % 2][:].rearrange("p (a n) -> p a n", a=2)
                        v.tensor_tensor(ra[:, 0], both, cs[:, 0:1, :].broadcast_to([P, 2, SEQ]), ALU.mult)
                        v.tensor_tensor(ra[:, 1], both, cs[:, 1:2, :].broadcast_to([P, 2, SEQ]), ALU.mult
                                        ).then_inc(acc_out[g % 2], 1)
                    if i == 2:
                        dve.wait_ge(st_done, h + 1)
                        wait(dve, ro_done, 2 * h)
                        v.tensor_tensor(rst[:, 0:SEQ], aux[:, 0, 0:SEQ], decay[:, h, :], ALU.mult)
                        v.tensor_tensor(rst[:, SEQ:384], aux[:, 0, SEQ:384], decay[:, h, 0:P], ALU.mult).then_inc(st_out, 1)
                for t in range(TT):
                    dve.wait_ge(ro_r, 1 + h + 1)
                    dve.wait_ge(ro_sq, 1 + 2 * (h + 1))
                    if t == 0:
                        for i in (4, 5):
                            group_out(dve, g0 + i)
                    v.scalar_tensor_tensor(ry[:, t, :], aux[:, 3 + t, :], small[:, 5, t:t + 1], rg[:, t, :],
                                           ALU.mult, ALU.mult).then_inc(ro_y, 1)
                for kk in range(4):
                    if kk % 2 == 0:
                        dve.wait_ge(yt_hi, 4 * h + kk + 2)
                    v.tensor_tensor(ytl[:, 4 * h + kk, :], aux[:, 1 + kk // 2, (kk % 2) * SEQ:(kk % 2 + 1) * SEQ],
                                    yth[:, 4 * h + kk, :].bitcast(F32), ALU.subtract).then_inc(yt_lo, 1)

            def post(n, name, per, mixed):
                c0, g0 = START[name], GROUP[name]
                for cb in range(4):
                    for i in range(per):
                        split_lo(dve, c0 + per * cb + i + 3)
                    g = g0 + cb
                    dve.wait_ge(mm_done, c0 + per * (cb + 1))
                    v.tensor_copy(mixed[:, :, cb * CW:(cb + 1) * CW],
                                  acc[g % 2][:].rearrange("p (t n) -> p t n", t=2)).then_inc(acc_out[g % 2], 1)
                dve.wait_ge(post_sq, 8 * (n + 1))
                v.tensor_reduce(psum1[:], psums[:], AX_X, ALU.add).then_inc(post_step, 1)
                dve.wait_ge(post_r, n + 1)
                dve.wait_ge(post_g, n + 1)
                for t in range(TT):
                    v.scalar_tensor_tensor(x[:, t, :], mixed[:, t, :], rstd[:, t:t + 1], x[:, t, :], ALU.mult,
                                           ALU.add).then_inc(post_done, 1)

            def ffn_dve(layer):
                name = f"ffn_in_{layer}"
                n0 = 16 + FFN_KT * layer
                s0 = FFN_KT * layer

                def one(c, g, n, m, s):
                    split_lo(dve, c + 3)
                    wait(dve, sil_out, m + 1)
                    wait(dve, hid_lo, n + 1)
                    v.tensor_tensor(ft[:, s % 2, :], fsil[:, s % 2, :], acc[g.mod(2)][:, SEQ:2 * SEQ], ALU.mult
                                    ).then_inc(acc_out[g.mod(2)], 1)
                with dve.Fori(0, 5) as it:
                    for s in range(4):
                        one(At(START[name] + s, 4, it), At(GROUP[name] + s, 4, it), At(n0 + s, 4, it), At(s0 + s, 4, it),
                            s)
                for s in range(20, 22):
                    one(At(START[name] + s), At(GROUP[name] + s), At(n0 + s), At(s0 + s), s)

            post(0, "ret_out", 2, mixed0)
            scale(5)
            lo_part(3, hl, hh, 28)
            ffn_dve(0)
            post(1, "ffn_out_0", 3, mixed2)
            scale(6)
            for k in range(0, KT, 2):
                dve.wait_ge(norm_hi, 36 + 2 * k + 4)
                for slot, dst, hi in ((6, kvl, kvh), (4, hl, hh)):
                    for kk in (k, k + 1):
                        v.scalar_tensor_tensor(dst[:, kk, :], aux[:, kk // 2, (kk % 2) * SEQ:(kk % 2 + 1) * SEQ],
                                               gains[:, slot, kk:kk + 1], hi[:, kk, :].bitcast(F32),
                                               ALU.mult, ALU.subtract).then_inc(norm_lo, 1)
            kv, g0 = START["kv"], GROUP["kv"]

            def t2_take(i):
                g = g0 + i
                dve.wait_ge(mm_done, kv + i + 1)
                if i:
                    dve.wait_ge(gath, 4 * i)
                bank = acc[g % 2]
                for half in range(2):
                    for sh in range(2):
                        ins = v.tensor_copy(
                            t2[HD * sh:HD * sh + HD].rearrange("p (s h) n -> p s h n", h=2)[:, :, half, 0:SEQ - sh],
                            bank[HD * half:HD * half + HD, :].rearrange("p (s n) -> p s n", s=2)[:, :, sh:SEQ])
                ins.then_inc(acc_out[g % 2], 1)
                dve.wait_ge(acc_out[g % 2], g // 2 + 1)
                src = t2[:].rearrange("p g (n r) -> p r g n", r=CMP_STRIDE)
                for half in range(2):
                    s_ap = src[:, 0:CMP_STRIDE:2, :, half:half + N_CMP]
                    v.tensor_copy(rgh[:, i, 8 * half:8 * half + 8, 0:60].rearrange("p j (g n) -> p j g n", g=4), s_ap
                                  ).then_inc(gath, 1)
                v.tensor_copy(rgh[:, i, :, 60:62], pe_in[:, i]).then_inc(gath, 1)
                dve.wait_ge(gath, 4 * i + 3)
                for half in range(2):
                    s_ap = src[:, 0:CMP_STRIDE:2, :, half:half + N_CMP]
                    part = lambda r: r[:, i, 8 * half:8 * half + 8, 0:60].rearrange("p j (g n) -> p j g n", g=4)
                    v.tensor_tensor(part(rgl), s_ap, part(rgh).bitcast(F32), ALU.subtract)
                v.tensor_tensor(rgl[:, i, :, 60:62], pe_in[:, i], rgh[:, i, :, 60:62].bitcast(F32), ALU.subtract).then_inc(gath, 1)

            def plain_k(i, dst):
                g = g0 + i
                dve.wait_ge(mm_done, kv + i + 1)
                for half in range(2):
                    ins = v.tensor_copy(dst.rearrange("p (s h) n -> p s h n", h=2)[:, :, half, :],
                                        acc[g % 2][HD * half:HD * half + HD, :].rearrange("p (s n) -> p s n", s=2))
                ins.then_inc(acc_out[g % 2], 1)

            def plain_v(i, dst):
                g = g0 + i
                dve.wait_ge(mm_done, kv + i + 1)
                v.tensor_copy(dst.rearrange("p t n -> p (t n)"), acc[g % 2][:]).then_inc(acc_out[g % 2], 1)

            def cmp_bias(j):
                dve.wait_ge(mm_done, START["cmp"] + 2 * (j + 1))
                v.tensor_copy(peb[:, j, 0:2], aux[:, 2 * j:2 * j + 2, 60]).then_inc(cmp_b, 1)

            dve.wait_ge(nsa_const, 16 * 6)
            split_lo(dve, kv + 3)
            t2_take(0)
            split_lo(dve, kv + 4)
            t2_take(1)
            split_lo(dve, kv + 5)
            dve.wait_ge(strip_mm, 1)
            v.tensor_copy(stripsb[:], aux[0:16, 4, 0:384]).then_inc(strip_out, 1)
            dve.wait_ge(cb_mm, 1)
            v.tensor_copy(cbias[:].rearrange("p t h n -> p t n h"),
                          aux[:, 5, 0:480].rearrange("p (t n h) -> p t n h", t=2, n=N_CMP)).then_inc(cb_out, 1)
            plain_k(2, ksw[:, 0])
            split_lo(dve, kv + 6)
            plain_v(3, vsw[:, 0])
            split_lo(dve, kv + 7)
            plain_k(4, ksw[:, 1])
            split_lo(dve, kv + 8)
            plain_v(5, vsw[:, 1])
            for j in range(2):
                split_lo(dve, START["cmp"] + 2 * j + 3)
                split_lo(dve, START["cmp"] + 2 * j + 4)
                cmp_bias(j)
            split_lo(dve, START["nsa_q"] + 3)
            dve.wait_ge(cmp_kv, 1)
            v.tensor_copy(kct[:], aux[0:HD, 4, 0:60])
            v.tensor_copy(vct[:], aux[0:N_CMP, 5, 0:256].rearrange("p (g d) -> p g d", g=4)).then_inc(kct_out, 1)
            for i in range(1, 4):
                split_lo(dve, START["nsa_q"] + i + 3)
            dve.wait_ge(ng_mm, 2)
            chain(v.tensor_copy(gate_n[:].rearrange("p t n -> p (t n)"), aux[:, 4, 0:96]))
            dve.wait_ge(nbias_in, 16)

            def n_softmax(b):
                g, kind = n_batch(b)
                dve.wait_ge(n_scores, b + 1)
                nm, nsb = negmax[:, b % 4, :], ns[:, b % 2]
                if kind < 2:
                    bias = nbias[:, 4 * g:4 * g + 4, :]
                    chain(v.tensor_tensor(heads(nsb[:, 0:512]), heads(aux[:, 0, :]), bias[:, :, P:SEQ], ALU.add))
                    v.tensor_tensor(nsb[:, 512:1536].rearrange("p (h n) -> p h n", h=4),
                                    aux[:, 1:3, :].rearrange("p a (h n) -> p (a h) n", h=2), bias, ALU.add
                                    ).then_inc(n_sout, 1)
                    dve.wait_ge(n_sout, b + 1)
                    v.tensor_reduce(nm[:, 0:4], heads(nsb[:, 0:512]), AX_X, ALU.max, negate=True)
                    v.tensor_reduce(nm[:, 4:8], heads(nsb[:, 512:1536]), AX_X, ALU.max, negate=True).then_inc(n_max, 1)
                else:
                    s = nsb[:, 0:120].rearrange("p (t h n) -> p t h n", t=2, h=4)
                    v.tensor_tensor(s, aux[:, 0, 0:120].rearrange("p (t h n) -> p t h n", t=2, h=4),
                                    cbias[:, :, 4 * g:4 * g + 4, :], ALU.add).then_inc(n_sout, 1)
                    dve.wait_ge(n_sout, b + 1)
                    chain(v.tensor_reduce(nm, nsb[:, 0:120].rearrange("p (t n) -> p t n", n=N_CMP), AX_X, ALU.max,
                                          negate=True))
                    v.tensor_scalar(nm, nm, 1e20, None, ALU.min).then_inc(n_max, 1)

            def n_out(b):
                g, kind = n_batch(b)
                dve.wait_ge(n_pv, b + 1)
                cc = coef[:, b % 2, :]
                which = (1, 2, 0)[kind]
                chain(v.tensor_scalar(small[:, 0, :], rowsum[:, b % 4, :], 1.1754944e-38, None, ALU.max))
                chain(v.reciprocal(small[:, 1, :], small[:, 0, :]))
                gg = gate_n[:, :, 12 * g:12 * g + 12].rearrange("p t (h b) -> p t h b", b=3)[:, :, :, which]
                chain(v.tensor_tensor(cc.rearrange("p (t h) -> p t h", t=2),
                                      small[:, 1, :].rearrange("p (t h) -> p t h", t=2), gg, ALU.mult))
                dst = cols(ys2, g)
                if kind == 0:
                    v.tensor_tensor(dst, o_bank(), per_row(cc), ALU.mult).then_inc(n_o, 1)
                else:
                    tmp = o_n[:].rearrange("p t (h d) -> p t h d", h=4)
                    v.tensor_tensor(tmp, o_bank(), per_row(cc), ALU.mult).then_inc(n_o, 1)
                    dve.wait_ge(n_o, b + 1)
                    ins = v.tensor_tensor(dst, dst, tmp, ALU.add)
                    if b == 11:
                        ins.then_inc(nys_ready, 1)
                    else:
                        chain(ins)

            n_softmax(0)
            n_softmax(1)
            for b in range(12):
                if b + 2 < 12:
                    n_softmax(b + 2)
                n_out(b)
            for k in range(KT):
                if k % 2 == 0:
                    dve.wait_ge(nys_hi, k + 2)
                v.tensor_tensor(ysl2[:, k, :].rearrange("p (t n) -> p t n", t=2), turned_back(k),
                                ysh2[:, k, :].bitcast(F32).rearrange("p (t n) -> p t n", t=2), ALU.subtract).then_inc(nys_lo, 1)
            post(2, "nsa_out", 1, mixed1)
            scale(7)
            lo_part(5, hl, hh, 52)
            ffn_dve(1)
            post(3, "ffn_out_1", 3, mixed2)

        @block.tensor
        def _(pe):
            pe.wait_ge(const_in, 16 * 2)
            norm_pe(pe, 0)
            norm_taken(pe, 0)

            def few_columns(w, n, bank, c0):
                for t in range(TT):
                    out = aux[:, bank, c0 + t * n:c0 + (t + 1) * n]
                    for k in range(KT):
                        for part in (hh, hl):
                            last = mm(out, part[:, k, t * P:(t + 1) * P].bitcast(F32), w[:, k, :],
                                      start=(k == 0 and part is hh), stop=(k == KT - 1 and part is hl))
                return last

            def running_sums():
                pe.wait_ge(f_ready, 1)
                for h in range(4):
                    out = aux[0:1, 3 + h // 2, (h % 2) * SEQ:(h % 2 + 1) * SEQ]
                    for t in range(TT):
                        last = mm(out, logf[:, t, h:h + 1], tri[:, t, :], start=(t == 0), stop=(t == 1))
                last.then_inc(cum_done, 1)

            def scores(b):
                p = min(b, 5)
                group_out(pe, GROUP["qkv"] + 3 * p)
                group_out(pe, GROUP["qkv"] + 3 * p + 1)
                wait(pe, scores_out, b)
                if b:
                    wait(pe, pt_ready, 3 * b if b < 6 else 3 * 6)
                n = 32 if b > 4 else HD
                q, k = q_b[0:n, b % 2], k_b[0:n, b % 2]
                if b == 4:
                    pe.wait_ge(cum_out, 1)
                for h in range(4):
                    for t in range(TT):
                        w = P * (t + 1)
                        out = (aux[:, 0, h * P:(h + 1) * P] if t == 0 else
                               aux[:, 1 + h // 2, (h % 2) * SEQ:(h % 2 + 1) * SEQ])
                        toks = slice(t * P, (t + 1) * P)
                        last = mm(out, q[:, h, toks], k[:, h, 0:w], start=True, stop=(b != 4))
                        if b == 4:
                            mm(out, cumrow[:, 0, h, toks], ones[:, 0:w])
                            last = mm(out, ones[:, 0:P], cumrow[:, 1, h, 0:w], stop=True)
                last.then_inc(scores_done, 1)

            def turn_probs(s, ready, count, turned_sem):
                wait(pe, ready, count)
                for j in range(3):
                    for h in range(4):
                        src = s[:, h * P:(h + 1) * P] if j == 0 else s[:, 512 + h * SEQ + (j - 1) * P:512 + h * SEQ + j * P]
                        tr = nc.tensor.transpose(aux[:, (3, 4, 0)[j], h * P:(h + 1) * P], src, ident[:])
                    tr.then_inc(turned_sem, 1)

            def turn(b):
                turn_probs(s_b1, probs_ready, b + 1, probs_turned)

            def pv(b):
                p = min(b, 5)
                group_out(pe, GROUP["qkv"] + 3 * p + 2)
                wait(pe, o_out, b)
                for h in range(4):
                    vh = lambda kt: v_b[:, p % 2, kt, h * HD:(h + 1) * HD]
                    if h == 0:
                        pe.wait_ge(pt_ready, 3 * b + 3)
                    mm(aux[:, 5, h * HD:(h + 1) * HD], pt_b1[:, 0, h * P:(h + 1) * P], vh(0), start=True, stop=True)
                    out = aux[:, 5, 256 + h * HD:256 + (h + 1) * HD]
                    mm(out, pt_b1[:, 1, h * P:(h + 1) * P], vh(0), start=True)
                    last = mm(out, pt_b1[:, 2, h * P:(h + 1) * P], vh(1), stop=True)
                last.then_inc(pv_done, 1)

            for p in range(6):
                product_t(pe, 3 * p, GROUP["qkv"] + 3 * p, hh, hl)
                if p == 0:
                    pe.wait_ge(table_in, 16 * 8)
                    pe.wait_ge(setup, 2)
                    few_columns(w_f, 4, 4, 0).then_inc(f_done, 1)
                product_t(pe, 3 * p + 1, GROUP["qkv"] + 3 * p + 1, hh, hl)
                if p:
                    turn(p - 1)
                else:
                    running_sums()
                product_n(pe, 3 * p + 2, GROUP["qkv"] + 3 * p + 2, hh, hl)
                if p:
                    pv(p - 1)
                scores(p)
            c, g = START["gates"], GROUP["gates"]
            product_t(pe, c, g, hh, hl)
            turn(5)
            product_t(pe, c + 1, g + 1, hh, hl)
            pv(5)
            scores(6)
            product_t(pe, c + 2, g + 2, hh, hl)
            turn(6)
            product_t(pe, c + 3, g + 3, hh, hl)
            pv(6)
            with pe.Fori(0, 3) as it:
                for s in range(4):
                    product_t(pe, At(c + 4 + s, 4, it), At(g + 4 + s, 4, it), hh, hl)

            def turn_ys(ys, sem_, ready):
                pe.wait_ge(ready, 1)
                for k in range(KT):
                    for t in range(TT):
                        c0 = (k % 2) * SEQ + t * P
                        tr = nc.tensor.transpose(aux[:, k // 2, c0:c0 + P], ys[:, t, k * P:(k + 1) * P], ident[:])
                    if k % 2:
                        tr.then_inc(sem_, 1)

            turn_ys(ys1, ys_turned, ys_ready)
            pe.wait_ge(ys_lo, KT)
            for n in range(4):
                c = At(START["branch"] + n)
                take(pe, c)
                s = c.mod(SLOTS)
                for j in range(4):
                    g = At(GROUP["branch"] + 4 * n + j)
                    bank = claim(pe, g)
                    if n == 0:
                        group_out(pe, GROUP["gates"] + 15)
                        group_out(pe, GROUP["gates"] + 14)
                    for sub in range(2):
                        out = bank[:, sub * SEQ:(sub + 1) * SEQ]
                        for k in range(2):
                            w = slice(k * D + (2 * j + sub) * P, k * D + (2 * j + sub + 1) * P)
                            mm(out, wh[:, s, w], ysh1[:, 2 * n + k, :], start=(k == 0))
                            mm(out, wh[:, s, w], ysl1[:, 2 * n + k, :])
                            last = mm(out, wl[:, s, w], ysh1[:, 2 * n + k, :], stop=(k == 1))
                    last.then_inc(branch_done if j < 3 else mm_done, 1)
            pe.wait_ge(norm_lo, KT + 4)
            for i in range(4):
                product_n(pe, START["out"] + i, GROUP["out"] + i, hh, hl)

            def turn_norm(n):
                pe.wait_ge(xn_ready, TT * (n + 1))
                for k in range(KT):
                    for t in range(TT):
                        c0 = (k % 2) * SEQ + t * P
                        tr = nc.tensor.transpose(aux[:, k // 2, c0:c0 + P], xn[:, t, k * P:(k + 1) * P], ident[:])
                    if k % 2:
                        tr.then_inc(turned, 1)

            turn_norm(1)
            pe.wait_ge(norm_lo, 12 + KT)
            with pe.Fori(0, 4) as it:
                for s in range(4):
                    product_t(pe, At(START["up"] + s, 4, it), At(GROUP["up"] + s, 4, it), hh, hl)
            pe.wait_ge(hid_lo, 2 + 16)
            with pe.Fori(0, 2) as it:
                for cb in range(2):
                    for i in range(4):
                        product_n(pe, At(START["down"] + 4 * cb + i, 8, it), At(GROUP["down"] + cb, 2, it),
                                  hid1h, hid1l, KT * i, KT, 4 * KT)
            turn_norm(2)
            pe.wait_ge(norm_lo, 20 + KT)
            for h in range(RET_HEADS):
                c0, g0 = START["ret"] + 6 * h, GROUP["ret"] + 6 * h
                product_t(pe, c0, g0, hh, hl)
                product_t(pe, c0 + 1, g0 + 1, hh, hl)
                product_n(pe, c0 + 2, g0 + 2, hh, hl)
                pe.wait_ge(rot_out, 2 * h + 2)
                wait(pe, st_out, h)
                for half in range(2):
                    mm(aux[:, 0, 0:SEQ], rk[:, half, 0:P], rq[:, half, :], start=(half == 0), stop=(half == 1))
                for half in range(2):
                    last = mm(aux[:, 0, SEQ:384], rk[:, half, P:SEQ], rq[:, half, P:SEQ], start=(half == 0), stop=(half == 1))
                last.then_inc(st_done, 1)
                product_n(pe, c0 + 3, g0 + 3, hh, hl)
                pe.wait_ge(st_out, h + 1)
                group_out(pe, g0 + 2)
                group_out(pe, g0 + 3)
                wait(pe, ro_y, 2 * h)
                mm(aux[:, 3, :], rst[:, 0:P], rv[:, 0, :], start=True, stop=True).then_inc(ro_done, 1)
                mm(aux[:, 4, :], rst[:, P:SEQ], rv[:, 0, :], start=True)
                mm(aux[:, 4, :], rst[:, SEQ:384], rv[:, 1, :], stop=True).then_inc(ro_done, 1)
                product_n(pe, c0 + 4, g0 + 4, hh, hl)
                product_n(pe, c0 + 5, g0 + 5, hh, hl)
                pe.wait_ge(ro_y, 2 * h + 2)
                wait(pe, yt_lo, 4 * h)
                for kk in range(4):
                    for t in range(TT):
                        cc = (kk % 2) * SEQ + t * P
                        tr = nc.tensor.transpose(aux[:, 1 + kk // 2, cc:cc + P], ry[:, t, kk * P:(kk + 1) * P], ident[:])
                    if kk % 2:
                        tr.then_inc(ry_turned, 1)
            pe.wait_ge(yt_lo, 16)
            for cb in range(4):
                for i in range(2):
                    product_n(pe, START["ret_out"] + 2 * cb + i, GROUP["ret_out"] + cb, yth, ytl, KT * i, KT, 2 * KT)

            def ffn_pe(layer):
                i0, g0 = START[f"ffn_in_{layer}"], GROUP[f"ffn_in_{layer}"]
                with pe.Fori(0, 5) as it:
                    for s in range(4):
                        product_t(pe, At(i0 + s, 4, it), At(g0 + s, 4, it), hh, hl)
                for s in range(20, 22):
                    product_t(pe, i0 + s, g0 + s, hh, hl)
                pe.wait_ge(hid_lo, 2 + 16 + FFN_KT * (layer + 1))
                o0, g0 = START[f"ffn_out_{layer}"], GROUP[f"ffn_out_{layer}"]
                for cb in range(4):
                    for i in range(3):
                        product_n(pe, o0 + 3 * cb + i, g0 + cb, hid2h, hid2l, KT * i, min(KT, FFN_KT - KT * i), FFN_KT)

            turn_norm(3)
            pe.wait_ge(norm_lo, 28 + KT)
            ffn_pe(0)
            turn_norm(4)
            pe.wait_ge(norm_lo, 36 + 2 * KT)
            kv, g0 = START["kv"], GROUP["kv"]
            product_t(pe, kv, g0, kvh, kvl)
            pe.wait_ge(nsa_const, 16 * 6)
            few_columns(w_gate, 48, 0, 0).then_inc(ng_mm, 1)
            mm(aux[0:16, 4, 0:384], relb[:], hot[:], start=True, stop=True).then_inc(strip_mm, 1)
            for t in range(TT):
                for n in range(N_CMP):
                    j = t * N_CMP + n
                    last = mm(aux[:, 5, 16 * j:16 * j + 16], chot[:, j * P:(j + 1) * P], relb[:], start=True, stop=True)
            last.then_inc(cb_mm, 1)
            product_t(pe, kv + 1, g0 + 1, kvh, kvl)
            product_t(pe, kv + 2, g0 + 2, kvh, kvl)
            product_n(pe, kv + 3, g0 + 3, kvh, kvl)
            product_t(pe, kv + 4, g0 + 4, kvh, kvl)
            product_n(pe, kv + 5, g0 + 5, kvh, kvl)
            pe.wait_ge(ng_out, 1)
            for i in range(2):
                pe.wait_ge(gath, 4 * (i + 1))
                for ch in range(2):
                    c = At(START["cmp"] + 2 * i + ch)
                    take(pe, c)
                    s = c.mod(SLOTS)
                    for sub in range(2):
                        out = aux[:, 2 * i + sub, 0:62]
                        for jj in range(8):
                            j = 8 * ch + jj
                            w = slice(jj * CW + sub * P, jj * CW + (sub + 1) * P)
                            mm(out, wh[:, s, w], rgh[:, i, j, :], start=(j == 0))
                            mm(out, wh[:, s, w], rgl[:, i, j, :])
                            last = mm(out, wl[:, s, w], rgh[:, i, j, :], stop=(j == 15))
                    last.then_inc(mm_done, 1)
            product_t(pe, START["nsa_q"], GROUP["nsa_q"], hh, hl)
            pe.wait_ge(cmp_hid, 4)
            pe.wait_ge(strip_out, 1)
            pe.wait_ge(cb_out, 1)
            for sub in range(2):
                mm(aux[0:HD, 4, 0:60], w2k[:, sub, :], hidc[:, 0, sub, :], start=(sub == 0), stop=(sub == 1))
            for g in range(GROUPS):
                for sub in range(2):
                    last = mm(aux[0:N_CMP, 5, g * HD:(g + 1) * HD], hidc[:, 1, sub, g * N_CMP:(g + 1) * N_CMP],
                              w2v[:, sub, :], start=(sub == 0), stop=(sub == 1))
            last.then_inc(cmp_kv, 1)
            for i in range(1, 4):
                product_t(pe, START["nsa_q"] + i, GROUP["nsa_q"] + i, hh, hl)
                if i == 1:
                    pe.wait_ge(kct_out, 1)
                    mm(aux[:, 4, 0:96], flip[:], gate_f[:].rearrange("p t n -> p (t n)"), start=True, stop=True
                       ).then_inc(ng_mm, 1)
            for i in range(4):
                group_out(pe, GROUP["nsa_q"] + i)

            def n_scores_of(b):
                g, kind = n_batch(b)
                wait(pe, n_sout, b)
                for h in range(4):
                    for t in range(TT):
                        toks = slice(t * P, (t + 1) * P)
                        if kind == 2:
                            out, rhs = aux[:, 0, (t * 4 + h) * N_CMP:(t * 4 + h + 1) * N_CMP], kct[:, g * N_CMP:(g + 1) * N_CMP]
                        else:
                            out = (aux[:, 0, h * P:(h + 1) * P] if t == 0 else
                                   aux[:, 1 + h // 2, (h % 2) * SEQ:(h % 2 + 1) * SEQ])
                            rhs = ksw[:, kind, g, 0:P * (t + 1)]
                        last = mm(out, nq[:, g, h, toks], rhs, start=True, stop=True)
                last.then_inc(n_scores, 1)

            def n_turn_of(b):
                pe.wait_ge(n_exp, b + 1)
                s = ns[:, b % 2]
                for j in range(3 if b < 8 else 2):
                    for h in range(4):
                        if b >= 8:
                            lo = (j * 4 + h) * N_CMP
                            tr = nc.tensor.transpose(aux[0:N_CMP, 3 + j, h * P:(h + 1) * P], s[:, lo:lo + N_CMP], ident[:])
                        else:
                            lo = h * P if j == 0 else 512 + h * SEQ + (j - 1) * P
                            tr = nc.tensor.transpose(n_turn_bank(j)[:, h * P:(h + 1) * P], s[:, lo:lo + P], ident[:])
                    tr.then_inc(n_turn, 1)

            def n_pv_of(b):
                g, kind = n_batch(b)
                pe.wait_ge(n_pt, n_turns_before(b + 1))
                wait(pe, n_o, b)
                for h in range(4):
                    o0, o1 = aux[:, 5, h * HD:(h + 1) * HD], aux[:, 5, 256 + h * HD:256 + (h + 1) * HD]
                    if kind == 2:
                        mm(o0, npt[0:N_CMP, 0, h * P:(h + 1) * P], vct[:, g, :], start=True, stop=True)
                        last = mm(o1, npt[0:N_CMP, 1, h * P:(h + 1) * P], vct[:, g, :], start=True, stop=True)
                    else:
                        vv = lambda kt: vsw[:, kind, kt, g * HD:(g + 1) * HD]
                        mm(o0, npt[:, 0, h * P:(h + 1) * P], vv(0), start=True, stop=True)
                        mm(o1, npt[:, 1, h * P:(h + 1) * P], vv(0), start=True)
                        last = mm(o1, npt[:, 2, h * P:(h + 1) * P], vv(1), stop=True)
                last.then_inc(n_pv, 1)

            n_scores_of(0)
            n_scores_of(1)
            for b in range(12):
                n_turn_of(b)
                if b + 2 < 12:
                    n_scores_of(b + 2)
                n_pv_of(b)
            turn_ys(ys2, nys_turned, nys_ready)
            pe.wait_ge(nys_lo, KT)
            for i in range(4):
                product_n(pe, START["nsa_out"] + i, GROUP["nsa_out"] + i, ysh2, ysl2)
            turn_norm(5)
            pe.wait_ge(norm_lo, 52 + KT)
            ffn_pe(1)


def alibi(n=16):
    return 2.0 ** (-8.0 * np.arange(1, n + 1) / n)


def t5_bucket(dist):
    n = np.maximum(dist, 0)
    nf = np.maximum(n, 1).astype(np.float32)
    large = 16 + (np.log(nf / np.float32(16)) / np.float32(np.log(8.0)) * np.float32(16)).astype(np.int32)
    return np.where(n < 16, n, np.minimum(large, 31))


def shape_constants():
    f = np.float32
    dist = np.arange(P)[:, None] + P - np.arange(SEQ)[None, :]
    slopes = alibi()

    def tiles(valid, by_head):
        return np.stack([np.where(valid, -s * dist, MASKED) for s in by_head], axis=1)

    zero = np.zeros(4)
    bias = [tiles(dist > 0, zero)]
    for (window, dil), first in zip(((128, 1), (512, 4), (2048, 16)), (0, 8, 12)):
        bias.append(tiles((dist >= 0) & (dist <= window) & (dist % dil == 0), slopes[first:first + 4]))
    bias.append(tiles(dist >= 0, zero))
    bias += [tiles(dist >= 0, slopes[4:8])] * 2
    tok = np.arange(SEQ)
    tri = (np.arange(SEQ).reshape(TT, P, 1) <= tok).astype(f).transpose(1, 0, 2)
    theta = (1.0 / (f(10000.0) ** np.linspace(0.0, 1.0, P, dtype=f))).astype(f)
    ang = tok.astype(f)[None, :] * theta[:, None]
    rel = tok[None, :] - np.arange(P)[:, None]
    log_gamma = np.log(1.0 - 2.0 ** (-5.0 - np.arange(RET_HEADS)))
    decay = np.stack([np.where(rel >= 0, np.exp(np.maximum(rel, 0) * g), 0.0) / 16.0 for g in log_gamma], axis=1)

    def one_hot(d):
        hot = np.zeros((33,) + d.shape, f)
        for b in range(32):
            hot[b] = (t5_bucket(d) == b) & (d >= 0)
        hot[32] = d < 0
        return hot

    chot = one_hot(np.stack([t * P + P - 1 - np.arange(P) - (CMP_STRIDE * n + CMP_LEN - 1)
                             for t in range(TT) for n in range(N_CMP)]))
    return {
        "ident": np.eye(P, dtype=f), "flip": np.ascontiguousarray(np.eye(P, dtype=f)[::-1]), "bias1": np.stack(bias).astype(f), "tri": tri,
        "cs": np.stack([np.cos(ang), np.sin(ang)], axis=1).astype(f), "decay": decay.astype(f),
        "hot": one_hot(SEQ - 1 - np.arange(384)), "chot": chot.reshape(33, 30 * P),
        "masked": np.full((1, 16), MASKED, f),
    }


def k_tiles(w, c0, k0=0, nk=KT, cols=CW):
    part = w[k0 * P:(k0 + nk) * P, c0:c0 + cols].reshape(nk, P, cols).transpose(1, 0, 2).reshape(P, nk * cols)
    if part.shape[1] == CHUNK:
        return part
    return np.concatenate([part, np.zeros((P, CHUNK - part.shape[1]), part.dtype)], axis=1)


def lay_out(a):
    w = a["w_in"][0]
    off = np.cumsum([0, 256, 256, 256, 768, 768, 768, 256, 256, 256, 4, 256, 256, 256, 4096])
    qa, ka, va, qb, kb, vb, qc, kc, vc, ff, qd, kd, vd, gates = off[:14]

    def by_component(c0):
        m = w[:, c0:c0 + CW].reshape(D, 4, 2, 32).transpose(0, 2, 1, 3).reshape(D, CW)
        return k_tiles(m, 0)

    ch = [k_tiles(w, c) for c in (qa, ka, va)]
    for g in range(3):
        ch += [k_tiles(w, c + CW * g) for c in (qb, kb, vb)]
    ch += [k_tiles(w, c) for c in (qc, kc, vc)]
    ch += [by_component(qd), by_component(kd), k_tiles(w, vd)]
    ch += [k_tiles(w, gates + CW * i) for i in range(16)]
    ch += [k_tiles(a["w_branch"][0, n], 0, 0, 2, D) for n in range(4)]
    ch += [k_tiles(a["w_out"][0], CW * i) for i in range(4)]
    ch += [k_tiles(a["w_up"][0], CW * i) for i in range(16)]
    ch += [k_tiles(a["w_down"][0], CW * cb, KT * i) for cb in range(4) for i in range(4)]
    r = a["ret_w_in_2"][0]
    for h in range(RET_HEADS):
        for c0 in (CW * h, D + CW * h):
            head = r[:, c0:c0 + CW]
            ch.append(k_tiles(np.concatenate([head[:, 0::2], head[:, 1::2]], axis=1), 0))
        ch += [k_tiles(r, 2 * D + RET_DV * h + CW * i) for i in range(2)]
        ch += [k_tiles(r, 4 * D + RET_DV * h + CW * i) for i in range(2)]
    ch += [k_tiles(a["ret_w_out_2"][0], CW * cb, KT * i) for cb in range(4) for i in range(2)]

    def ffn(layer):
        win, wout = a["ffn_w_in_2"][layer], a["ffn_w_out_2"][layer]
        res = [k_tiles(np.concatenate([win[:, P * j:P * (j + 1)], win[:, FFN + P * j:FFN + P * (j + 1)]], axis=1), 0)
               for j in range(FFN_KT)]
        return res + [k_tiles(wout, CW * cb, KT * i, min(KT, FFN_KT - KT * i)) for cb in range(4) for i in range(3)]

    ch += ffn(0)
    kv = a["kv_w_2"]
    ch += [k_tiles(kv, CW * i) for i in range(6)]
    ch += [k_tiles(a["cmp_w1_k_2"], 0, KT * i) for i in range(2)] + [k_tiles(a["cmp_w1_v_2"], 0, KT * i) for i in range(2)]
    nsa = a["nsa_w_in_2"][0]
    ch += [k_tiles(nsa, CW * i) for i in range(4)]
    ch += [k_tiles(a["nsa_w_out_2"][0], CW * i) for i in range(4)]
    ch += ffn(1)
    assert len(ch) == N_CHUNKS

    def columns(g):
        return g.reshape(KT, P).T

    def pairs(pe):
        m = pe.reshape(16, P).T
        return np.stack([m, m], axis=2)

    def narrow(m):
        return m.reshape(KT, P, m.shape[1]).transpose(1, 0, 2)

    return {
        "x": a["x"][0], "stream": np.stack(ch),
        "gains": np.stack([columns(g) for g in (
            a["mix_norm_g"][0], a["mlp_norm_g"][0], a["mix_norm_pre_2"][0], a["ffn_norm_pre_2"][0],
            a["mix_norm_pre_2"][1], a["ffn_norm_pre_2"][1], a["kv_norm_2"])], axis=1),
        "grows": np.stack([a["final_norm_g"], a["mix_norm_post_2"][0], a["ffn_norm_post_2"][0],
                           a["mix_norm_post_2"][1], a["ffn_norm_post_2"][1]]),
        "w_f": narrow(w[:, ff:ff + 4]), "w_gate": narrow(nsa[:, D:D + 48]),
        "w2k": a["cmp_w2_k_2"].reshape(2, P, HD).transpose(1, 0, 2),
        "w2v": a["cmp_w2_v_2"].reshape(2, P, HD).transpose(1, 0, 2),
        "b_forget": a["b_forget"][0],
        "lams": np.stack([a["lambda_q1"][0], a["lambda_k1"][0], a["lambda_q2"][0], a["lambda_k2"][0]]),
        "diff_g": a["diff_norm_g"][0], "rel_bias": a["rel_bias_2"],
        "pe_in": np.stack([pairs(a["cmp_pe_k_2"]), pairs(a["cmp_pe_v_2"])], axis=1),
    }


def program(nc, arrays):
    io = {n: nc.dram_tensor(f"in_{n}", v.shape, F32, kind="ExternalInput").ap() for n, v in arrays.items()}
    io["strip"] = nc.dram_tensor("strip", (16, 384), F32, kind="Internal").ap()
    io["out"] = nc.dram_tensor("y", (SEQ, D), F32, kind="ExternalOutput").ap()
    build(nc, io)


def kernel(**inputs):
    import concourse.bacc as bacc
    from concourse.bass_utils import run_bass_kernel_spmd

    arrays = lay_out({n: np.asarray(v) for n, v in inputs.items()})
    arrays.update(shape_constants())
    arrays = {n: np.ascontiguousarray(v) for n, v in arrays.items()}
    nc = bacc.Bacc("TRN2", target_bir_lowering=False, num_devices=1)
    program(nc, arrays)
    r = run_bass_kernel_spmd(nc, [{f"in_{n}": v for n, v in arrays.items()}], core_ids=[0])
    return r.results[0]["y"].reshape(1, SEQ, D)
```

```python
from contextlib import ExitStack

import numpy as np

import concourse.bass as bass
from concourse import mybir

F32 = mybir.dt.float32
F32R = mybir.dt.float32r
ALU = mybir.AluOpType
ACT = mybir.ActivationFunctionType
AX_X = mybir.AxisListType.X

P = 128
SEQ = 256
D = 1024
KT = D // P
TT = SEQ // P
HD = 64
CW = 256
CHUNK = KT * CW
SLOTS = 4
AHEAD = 3
EPS = 1e-6
MASKED = -1e30
N_CMP, CMP_LEN, CMP_STRIDE, CMP_HIDDEN = 15, 32, 16, 256
GROUPS = 4
RET_HEADS, RET_DV = 4, 512
FFN = 2816
FFN_KT = FFN // P
D_FF = 4096
LAMBDA_INIT = 0.8 - 0.6

PHASES = [("qkv", 18), ("gates", 16), ("branch", 4), ("out", 4), ("up", 16), ("down", 16),
          ("ret", 24), ("ret_out", 8), ("ffn_in_0", 22), ("ffn_out_0", 12),
          ("kv", 6), ("cmp", 4), ("nsa_q", 4), ("nsa_out", 4), ("ffn_in_1", 22), ("ffn_out_1", 12)]
START = {}
N_CHUNKS = 0
for _name, _n in PHASES:
    START[_name] = N_CHUNKS
    N_CHUNKS += _n

GROUP_COUNT = {"qkv": 18, "gates": 16, "branch": 0, "out": 4, "up": 16, "down": 4, "ret": 24, "ret_out": 4,
               "ffn_in_0": 22, "ffn_out_0": 4, "kv": 6, "cmp": 0, "nsa_q": 4, "nsa_out": 4,
               "ffn_in_1": 22, "ffn_out_1": 4}
GROUP = {}
_g = 0
for _name, _n in PHASES:
    GROUP[_name] = _g
    _g += GROUP_COUNT[_name]

NORMS = ["mix", "mlp", "ret", "ffn0", "nsa", "ffn1"]


class At:

    def __init__(self, const, step=0, it=None):
        self.const, self.step, self.it = const, step, it

    def __add__(self, n):
        return At(self.const + n, self.step, self.it)

    def __sub__(self, n):
        return self + (-n)

    def __mul__(self, n):
        return At(self.const * n, self.step * n, self.it)

    def mod(self, m):
        assert self.step % m == 0
        return self.const % m

    def div(self, m):
        assert self.step % m == 0
        return At(self.const // m, self.step // m, self.it)

    @property
    def value(self):
        return self.const if self.it is None or self.step == 0 else self.it * self.step + self.const


def wait(engine, semaphore, at):
    if isinstance(at, int):
        at = At(at)
    if at.const > 0 or at.step > 0:
        engine.wait_ge(semaphore, at.value)


def build(nc, io):
    with ExitStack() as ctx:
        def sb(name, shape, dt=F32, where=None):
            return (where or ctx).enter_context(nc.sbuf_tensor(name, shape, dt))

        def sem(name):
            return ctx.enter_context(nc.semaphore(name))

        raw = sb("raw", [P, SLOTS, CHUNK])
        wh = sb("wh", [P, SLOTS, CHUNK], F32R)
        wl = sb("wl", [P, SLOTS, CHUNK], F32R)
        x = sb("x", [P, TT, D])
        hh = sb("hh", [P, KT, SEQ], F32R)
        hl = sb("hl", [P, KT, SEQ], F32R)
        ident = sb("ident", [P, P])
        gains = sb("gains", [P, len(NORMS) + 1, KT])
        sums = sb("sums", [P, 2 * TT])
        means = sb("means", [P, TT])
        rstd = sb("rstd", [P, TT])
        mhalf = sb("mhalf", [P, 8])
        psums = sb("psums", [P, TT, 5])
        psum1 = sb("psum1", [P, TT])
        w_f = sb("w_f", [P, KT, 4])
        wfh, wfl = sb("wfh", [P, KT, 4], F32R), sb("wfl", [P, KT, 4], F32R)
        w2k = sb("w2k", [P, 2, HD])
        w2v = sb("w2v", [P, 2, HD])
        b_f = sb("b_f", [4, 1])
        lams = sb("lams", [P, 4, 32])
        lam = sb("lam", [P, 8])
        lamp = sb("lamp", [P, 2, 32])
        diff_g = sb("diff_g", [P, HD])
        negmax = sb("negmax", [P, 8, 8])
        rowsum = sb("rowsum", [P, 8, 8])
        coef = sb("coef", [P, 8, 8])
        small = sb("small", [P, 8, 8])

        def arena(*tensors):
            with ExitStack() as scope:
                return [sb(n, s, dt, scope) for n, s, dt in tensors]

        xn, = arena(("xn", [P, TT, D], F32))
        def arena_after(used, *tensors):
            with ExitStack() as scope:
                sb(f"skip_{tensors[0][0]}", [P, used // 4], F32, scope)
                return [sb(n, s, dt, scope) for n, s, dt in tensors]

        gate, = arena(("gate", [P, 32, SEQ], F32))
        after_xn, upper, after_gate = 8 * 1024, 16 * 1024, 32 * 1024
        fz, cum = arena_after(after_xn, ("fz", [4, 2, SEQ], F32), ("cum", [4, 2, SEQ], F32))
        q_b, k_b = arena_after(upper, ("q_b", [HD + 2, 2, 4, SEQ], F32), ("k_b", [HD + 2, 2, 4, SEQ], F32))
        (v_b, s_b1, pt_b1, bias_b, ys1, og) = arena_after(
            after_gate, ("v_b", [P, 2, TT, CW], F32), ("s_b1", [P, 6 * CW], F32), ("pt_b1", [P, 3, 512], F32),
            ("bias_b", [P, 2, 4, SEQ], F32), ("ys1", [P, TT, D], F32), ("og", [P, 3, TT, CW], F32))
        ysh1, ysl1 = arena_after(after_gate, ("ysh1", [P, KT, SEQ], F32R), ("ysl1", [P, KT, SEQ], F32R))
        hid1h, hid1l, r1, grow1 = arena(("hid1h", [P, 32, SEQ], F32R), ("hid1l", [P, 32, SEQ], F32R),
                                        ("r1", [P, 2, 2, 2, SEQ], F32), ("grow1", [P, D], F32))
        (yth, ytl, rq, rk, ra, cs, decay, rv, rg, ry, rst, mixed0, grow0) = arena(
            ("yth", [P, 16, SEQ], F32R), ("ytl", [P, 16, SEQ], F32R), ("rq", [P, 2, SEQ], F32),
            ("rk", [P, 2, SEQ], F32), ("ra", [P, 2, 2, SEQ], F32), ("cs", [P, 2, SEQ], F32),
            ("decay", [P, RET_HEADS, SEQ], F32), ("rv", [P, TT, RET_DV], F32), ("rg", [P, TT, RET_DV], F32),
            ("ry", [P, TT, RET_DV], F32), ("rst", [P, 384], F32), ("mixed0", [P, TT, D], F32),
            ("grow0", [P, D], F32))
        (hid2h, hid2l, ft, fsil, mixed2, grow2) = arena(
            ("hid2h", [P, FFN_KT, SEQ], F32R), ("hid2l", [P, FFN_KT, SEQ], F32R), ("ft", [P, 2, SEQ], F32),
            ("fsil", [P, 2, SEQ], F32), ("mixed2", [P, TT, D], F32), ("grow2", [P, D], F32))
        (ksw, vsw, nbias, cbias, ys2, relb, hot, stripsb, kct, vct, peb, hidc, pe_in, gate_n, o_n, gate_f) = arena(
            ("ksw", [HD, 2, GROUPS, SEQ], F32), ("vsw", [P, 2, TT, CW], F32), ("nbias", [P, 16, SEQ], F32),
            ("cbias", [P, TT, 16, N_CMP], F32), ("ys2", [P, TT, D], F32), ("relb", [33, 16], F32),
            ("hot", [33, 384], F32), ("stripsb", [16, 384], F32), ("kct", [HD, 60], F32),
            ("vct", [N_CMP, GROUPS, HD], F32), ("peb", [P, 2, 2], F32), ("hidc", [P, 2, 2, 60], F32),
            ("pe_in", [P, 2, 16, 2], F32), ("gate_n", [P, TT, 48], F32), ("o_n", [P, TT, CW], F32),
            ("gate_f", [48, SEQ], F32))
        after_nsa = 47 * 1024
        nq, ns, npt = arena_after(after_nsa, ("nq", [HD, 4, 4, SEQ], F32), ("ns", [P, 2, 6 * CW], F32),
                                  ("npt", [P, 3, 512], F32))
        kvh, kvl, rgh, rgl = arena_after(after_nsa, ("kvh", [P, KT, SEQ], F32R), ("kvl", [P, KT, SEQ], F32R),
                                         ("rgh", [P, 2, 16, 62], F32R), ("rgl", [P, 2, 16, 62], F32R))
        t2, w_gate, cmp_s = arena_after(30 * 1024, ("t2", [P, GROUPS, SEQ], F32), ("w_gate", [P, KT, 48], F32),
                                        ("cmp_s", [62, 2, CW], F32))
        wgh, wgl = arena_after(12 * 1024, ("wgh", [P, KT, 48], F32R), ("wgl", [P, KT, 48], F32R))
        ysh2, ysl2, mixed1, growb = arena_after(after_nsa, ("ysh2", [P, KT, SEQ], F32R), ("ysl2", [P, KT, SEQ], F32R),
                                                ("mixed1", [P, TT, D], F32), ("growb", [P, D], F32))

        acc = [ctx.enter_context(nc.psum_tensor(f"acc{i}", [P, 512], F32)) for i in range(2)]
        aux = ctx.enter_context(nc.psum_tensor("aux", [P, 6, 512], F32))

        full = [sem(f"full{i}") for i in range(SLOTS)]
        hi_ready, lo_ready = sem("hi_ready"), sem("lo_ready")
        mm_done = sem("mm_done")
        acc_out = [sem("acc_out0"), sem("acc_out1")]
        const_in, table_in = sem("const_in"), sem("table_in")
        x_in = [sem("x_in0"), sem("x_in1")]
        setup = sem("setup")
        squares, rstd_step, rstd_ready, xn_ready = sem("squares"), sem("rstd_step"), sem("rstd_ready"), sem("xn_ready")
        turned, norm_hi, norm_lo = sem("turned"), sem("norm_hi"), sem("norm_lo")
        dve_step = sem("dve_step")
        act_step = sem("act_step")
        bias_in = [sem("bias_in0"), sem("bias_in1")]
        scores_done, scores_out = sem("scores_done"), sem("scores_out")
        probs_max, probs_ready = sem("probs_max"), sem("probs_ready")
        probs_turned, pt_ready, pv_done, o_out = sem("probs_turned"), sem("pt_ready"), sem("pv_done"), sem("o_out")
        sb_l, sb_c, sb_e = sem("sb_l"), sem("sb_c"), sem("sb_e")
        wf_ready, f_done, f_in, f_e, cum_out = (sem("wf_ready"), sem("f_done"), sem("f_in"), sem("f_e"),
                                                sem("cum_out"))
        cum_in = sem("cum_in")
        ys_ready, ys_turned, ys_hi, ys_lo = sem("ys_ready"), sem("ys_turned"), sem("ys_hi"), sem("ys_lo")
        branch_done, branch_out = sem("branch_done"), sem("branch_out")
        mix_sum, mix_ready = sem("mix_sum"), sem("mix_ready")
        sq_ready, hid_hi, hid_lo = sem("sq_ready"), sem("hid_hi"), sem("hid_lo")
        rot_out = sem("rot_out")
        ret_const = sem("ret_const")
        st_done, st_out = sem("st_done"), sem("st_out")
        ro_done, ro_sq, ro_r, ro_y = sem("ro_done"), sem("ro_sq"), sem("ro_r"), sem("ro_y")
        ry_turned, yt_hi, yt_lo = sem("ry_turned"), sem("yt_hi"), sem("yt_lo")
        post_sq, post_r, post_done = sem("post_sq"), sem("post_r"), sem("post_done")
        first_done = sem("first_done")
        post_step = sem("post_step")
        grow_in = [sem(f"grow_in{i}") for i in range(5)]
        sil_out = sem("sil_out")
        nsa_const, strip_mm, strip_out, strip_io, nbias_in = (sem("nsa_const"), sem("strip_mm"), sem("strip_out"),
                                                              sem("strip_io"), sem("nbias_in"))
        wg_ready, cb_out = sem("wg_ready"), sem("cb_out")
        gath, cmp_raw, cmp_turned, cmp_b, cmp_hid, cmp_kv, kct_out = (sem("gath"), sem("cmp_raw"), sem("cmp_turned"), sem("cmp_b"),
                                                                 sem("cmp_hid"), sem("cmp_kv"), sem("kct_out"))
        ng_mm, ng_out = sem("ng_mm"), sem("ng_out")
        n_scores, n_sout, n_max, n_exp, n_turn, n_pt, n_pv, n_o = (sem("n_scores"), sem("n_sout"), sem("n_max"), sem("n_exp"),
                                                                   sem("n_turn"), sem("n_pt"), sem("n_pv"), sem("n_o"))
        nys_ready, nys_turned, nys_hi, nys_lo = sem("nys_ready"), sem("nys_turned"), sem("nys_hi"), sem("nys_lo")
        y_out = sem("y_out")

        def group_out(engine, g):
            g = g if isinstance(g, At) else At(g)
            wait(engine, acc_out[g.mod(2)], g.div(2) + 1)

        def branch_bank(m):
            return (aux[:, 4, :], aux[:, 5, :], acc[0][:, :], acc[1][:, :])[m % 4]

        def turned_back(k):
            return aux[:, k // 2, (k % 2) * SEQ:(k % 2 + 1) * SEQ].rearrange("p (t n) -> p t n", t=2)[:, :, ::-1]

        def n_turn_bank(b, j):
            return aux[:, 3 + j, :] if j < 2 else aux[:, 0, :] if b < 2 else acc[0][:, :]

        def n_turn_order(b):
            return (0, 1) if b % 3 == 2 else (2, 0, 1)

        def n_turns_before(b):
            return 8 * (b // 3) + 3 * (b % 3)

        def n_batch(b):
            return b // 3, b % 3

        def backwards(ap):
            return ap[:, :, :, ::-1]

        def split_hi(act, c):
            c = c if isinstance(c, At) else At(c)
            if c.it is None and c.const >= N_CHUNKS:
                return
            s = c.mod(SLOTS)
            wait(act, full[s], (c.div(SLOTS) + 1) * 16)
            wait(act, mm_done, c - (SLOTS - 1))
            nc.scalar.activation(wh[:, s, :], raw[:, s, :], ACT.Copy).then_inc(hi_ready, 1)

        def split_lo(dve, c):
            c = c if isinstance(c, At) else At(c)
            if c.it is None and c.const >= N_CHUNKS:
                return
            s = c.mod(SLOTS)
            wait(dve, hi_ready, c + 1)
            nc.vector.tensor_tensor(wl[:, s, :], raw[:, s, :], wh[:, s, :].bitcast(F32),
                                    ALU.subtract).then_inc(lo_ready, 1)

        def take(pe, c):
            wait(pe, lo_ready, c + 1)

        def claim(pe, g):
            wait(pe, acc_out[g.mod(2)], g.div(2))
            return acc[g.mod(2)]

        def mm(*args, start=False, stop=False):
            return nc.tensor.matmul(*args, start=start, stop=stop)

        def product_t(pe, c, g, ah, al, ready=None):
            c, g = (c if isinstance(c, At) else At(c)), (g if isinstance(g, At) else At(g))
            take(pe, c)
            bank, s = claim(pe, g), c.mod(SLOTS)
            for sub in range(2):
                out = bank[:, sub * SEQ:(sub + 1) * SEQ]
                for k in range(KT):
                    if ready and sub == 0:
                        pe.wait_ge(*ready(k))
                    cols = slice(k * CW + sub * P, k * CW + (sub + 1) * P)
                    mm(out, wh[:, s, cols], ah[:, k, :], start=(k == 0))
                    mm(out, wh[:, s, cols], al[:, k, :])
                    last = mm(out, wl[:, s, cols], ah[:, k, :], stop=(k == KT - 1))
            last.then_inc(mm_done, 1)

        def product_n(pe, c, g, ah, al, k0=0, nk=KT, total=KT, ready=None):
            c, g = (c if isinstance(c, At) else At(c)), (g if isinstance(g, At) else At(g))
            take(pe, c)
            if k0 == 0:
                claim(pe, g)
            bank, s = acc[g.mod(2)], c.mod(SLOTS)
            for t in range(TT):
                out = bank[:, t * CW:(t + 1) * CW]
                tok = slice(t * P, (t + 1) * P)
                for kk in range(nk):
                    k = k0 + kk
                    if ready and t == 0:
                        pe.wait_ge(*ready(k))
                    cols = slice(kk * CW, (kk + 1) * CW)
                    nc.tensor.matmul(out, ah[:, k, tok], wh[:, s, cols], start=(k == 0 and t == 0), stop=False,
                                     skip_group_check=True)
                    nc.tensor.matmul(out, ah[:, k, tok], wl[:, s, cols], start=False, stop=False,
                                     skip_group_check=True)
                    last = nc.tensor.matmul(out, al[:, k, tok], wh[:, s, cols], start=False,
                                            stop=(k == total - 1), skip_group_check=True)
            last.then_inc(mm_done, 1)

        def norm_act_squares(act, n, x_waits):
            for t in range(TT):
                for s, v in x_waits(t):
                    act.wait_ge(s, v)
                nc.scalar.activation(xn[:, t, :], x[:, t, :], ACT.Square,
                                     accum_out=sums[:, t:t + 1]).then_inc(squares, 1)

        def norm_pool(pool, n):
            for t in range(TT):
                pool.wait_ge(squares, TT * n + t + 1)
                nc.gpsimd.tensor_scalar(means[:, t:t + 1], sums[:, t:t + 1], 1.0 / D, EPS, ALU.mult, ALU.add
                                        ).then_inc(rstd_step, 1)
                rstd_steps[0] += 1
                pool.wait_ge(rstd_step, rstd_steps[0])
                nc.gpsimd.tensor_tensor(rstd[:, t:t + 1], means[:, t:t + 1], mhalf[:, 0:1], ALU.pow
                                        ).then_inc(rstd_ready, 1)

        def norm_dve_scale(dve, n):
            for t in range(TT):
                dve.wait_ge(rstd_ready, TT * n + t + 1)
                nc.vector.tensor_scalar(xn[:, t, :], x[:, t, :], rstd[:, t:t + 1], None,
                                        ALU.mult).then_inc(xn_ready, 1)

        def norm_pe(pe, m):
            for t in range(TT):
                pe.wait_ge(xn_ready, TT * m + t + 1)
                for k in range(KT):
                    c0 = (k % 2) * SEQ + t * P
                    tr = nc.tensor.transpose(aux[:, k // 2, c0:c0 + P], xn[:, t, k * P:(k + 1) * P], ident[:])
                    if t == TT - 1 and k % 2:
                        tr.then_inc(turned, 1)

        def norm_act_hi(act, n, count, slot, dst):
            for k in range(KT):
                if k % 2 == 0:
                    act.wait_ge(turned, 4 * n + k // 2 + 1)
                nc.scalar.activation(dst[:, k, :], aux[:, k // 2, (k % 2) * SEQ:(k % 2 + 1) * SEQ], ACT.Copy,
                                     scale=gains[:, slot, k:k + 1]).then_inc(norm_hi, 1)

        def norm_dve_lo(dve, count, slot, dst, hi):
            for k in range(KT):
                if k % 2 == 0:
                    dve.wait_ge(norm_hi, KT * count + k + 2)
                nc.vector.scalar_tensor_tensor(dst[:, k, :], aux[:, k // 2, (k % 2) * SEQ:(k % 2 + 1) * SEQ],
                                               gains[:, slot, k:k + 1], hi[:, k, :].bitcast(F32),
                                               ALU.mult, ALU.subtract).then_inc(norm_lo, 1)

        def normed(before):
            return lambda k: (norm_lo, before + k + 1)

        rstd_steps = [0]

        batches1 = ["sb", "d0", "d1", "d2", "fox", "diff0", "diff1"]

        block = ctx.enter_context(nc.Block())

        @block.sync
        def _(sp):
            for t in range(TT):
                sp.dma_start(x[:, t, :], io["x"][t * P:(t + 1) * P]).then_inc(x_in[t], 16)
            sp.dma_start(ident[:], io["ident"]).then_inc(const_in, 16)
            sp.dma_start(gains[:], io["gains"]).then_inc(const_in, 16)
            for s in range(SLOTS):
                sp.dma_start(raw[:, s, :], io["stream"][s]).then_inc(full[s], 16)
                if s == 0:
                    for dst, src in ((w_f[:], io["w_f"]), (b_f[:], io["b_forget"].rearrange("(n a) -> n a", a=1)),
                                     (lams[:], io["lams"].rearrange("(a m) n -> a m n", a=1).broadcast_to([P, 4, 32])),
                                     (diff_g[:], io["diff_g"].rearrange("(a n) -> a n", a=1).broadcast_to([P, HD])),
                                     (w2k[:], io["w2k"]), (w2v[:], io["w2v"])):
                        sp.dma_start(dst, src).then_inc(table_in, 16)
            with sp.Fori(1, N_CHUNKS // SLOTS) as it:
                for s in range(SLOTS):
                    c = At(s, SLOTS, it)
                    wait(sp, lo_ready, c - (SLOTS - 1))
                    sp.dma_start(raw[:, s, :], io["stream"][bass.ds(c.value, 1)].rearrange("a p n -> p (a n)")
                                 ).then_inc(full[s], 16)
            sp.wait_ge(post_done, 4 * TT)
            sp.dma_start(io["out"].rearrange("(t p) d -> p t d", p=P), x[:]).then_inc(y_out, 16)
            sp.wait_ge(y_out, 16)

        @block.gpsimd
        def _(pool):
            g = nc.gpsimd

            def load(dst, src, s):
                pool.dma_start(dst, src).then_inc(s, 16)

            g.memset(mhalf[:], -0.5).then_inc(setup, 1)
            g.memset(small[:, 6, 0:1], 0.0).then_inc(hid_lo, 1)
            g.memset(small[:, 6, 1:2], 0.0).then_inc(hid_lo, 1)
            pool.wait_ge(setup, 1)
            g.memset(psums[:, :, 4:5], EPS).then_inc(setup, 1)
            norm_pool(pool, 0)
            load(bias_b[:, 0], io["bias1"][0], bias_in[0])
            load(bias_b[:, 1], io["bias1"][1], bias_in[1])
            pool.wait_ge(cum_out, 1)
            load(q_b[HD:HD + 1, 0, :, :], cum[:, 0, :], cum_in)
            load(k_b[HD + 1:HD + 2, 0, :, :], cum[:, 1, :], cum_in)
            for b in range(2, 7):
                pool.wait_ge(scores_out, b - 1)
                load(bias_b[:, b % 2], io["bias1"][b], bias_in[b % 2])
            pool.wait_ge(ro_sq, 1)
            g.tensor_scalar(small[:, 0, :], small[:, 1, :], 1.0 / HD, EPS, ALU.mult, ALU.add).then_inc(rstd_step, 1)
            rstd_steps[0] += 1
            pool.wait_ge(rstd_step, rstd_steps[0])
            g.tensor_tensor(small[:, 2, :], small[:, 0, :], mhalf[:], ALU.pow).then_inc(ro_r, 1)
            for n in range(1, 3):
                for j in range(4):
                    pool.wait_ge(branch_out, 4 * n + j + 1)
                    if n == 2:
                        pool.wait_ge(mix_sum, j + 1)
                    a, b = gate[:, 2 * j:2 * j + 2, :], gate[:, n * KT + 2 * j:n * KT + 2 * j + 2, :]
                    g.tensor_tensor(a, a, b, ALU.add).then_inc(mix_sum, 1)
            def hid_lo_step(dst_l, full_value, dst_h, n):
                wait(pool, hid_hi, n + 1)
                g.tensor_tensor(dst_l, full_value, dst_h.bitcast(F32), ALU.subtract).then_inc(hid_lo, 1)

            norm_pool(pool, 1)
            with pool.Fori(0, 4) as it:
                for s in range(4):
                    n = At(s, 4, it)
                    tile = bass.ds((n * 2).value, 2)
                    hid_lo_step(hid1l[:, tile, :], r1[:, s % 2, 1], hid1h[:, tile, :], n)
            load(grow1[:], io["grows"][0:1, :].broadcast_to([P, D]), grow_in[0])
            norm_pool(pool, 2)
            pool.wait_ge(mm_done, START["ret"])
            load(cs[:], io["cs"], ret_const)
            load(decay[:], io["decay"], ret_const)
            load(grow0[:], io["grows"][1:2, :].broadcast_to([P, D]), grow_in[1])
            norm_pool(pool, 3)
            for h in range(RET_HEADS):
                for i in range(2):
                    n = 2 * h + i
                    group_out(pool, GROUP["ret"] + 6 * h + i)
                    dst = (rq, rk)[i]
                    if h:
                        pool.wait_ge(st_done, h)
                    g.tensor_tensor(dst[:, 0, :], ra[:, 0, 0, :], ra[:, 1, 1, :], ALU.subtract)
                    g.tensor_tensor(dst[:, 1, :], ra[:, 1, 0, :], ra[:, 0, 1, :], ALU.add).then_inc(rot_out, 1)
                pool.wait_ge(ro_sq, 1 + 2 * (h + 1))
                g.tensor_scalar(small[:, 3, 0:2], small[:, 4, 0:2], 1.0 / RET_DV, EPS, ALU.mult, ALU.add
                                ).then_inc(rstd_step, 1)
                rstd_steps[0] += 1
                pool.wait_ge(rstd_step, rstd_steps[0])
                g.tensor_tensor(small[:, 5, 0:2], small[:, 3, 0:2], mhalf[:, 0:2], ALU.pow).then_inc(ro_r, 1)

            def post(n):
                pool.wait_ge(post_step, n + 1)
                g.tensor_tensor(rstd[:], psum1[:], mhalf[:, 0:TT], ALU.pow).then_inc(post_r, 1)

            def ffn_pool(layer):
                n0 = 16 + FFN_KT * layer
                with pool.Fori(0, 5) as it:
                    for s in range(4):
                        n = At(n0 + s, 4, it)
                        tile = bass.ds((At(s, 4, it)).value, 1)
                        hid_lo_step(hid2l[:, tile, :], ft[:, s % 2:s % 2 + 1, :], hid2h[:, tile, :], n)
                for s in range(20, 22):
                    hid_lo_step(hid2l[:, s:s + 1, :], ft[:, s % 2:s % 2 + 1, :], hid2h[:, s:s + 1, :], At(n0 + s))

            post(0)
            pool.wait_ge(post_done, TT)
            load(grow2[:], io["grows"][2:3, :].broadcast_to([P, D]), grow_in[2])
            norm_pool(pool, 4)
            ffn_pool(0)
            post(1)
            norm_pool(pool, 5)
            pool.wait_ge(strip_out, 1)
            pool.wait_ge(ng_mm, 1)
            first_late = (P - CMP_LEN) // CMP_STRIDE + 1
            g.memset(cbias[:, 0, :, first_late:N_CMP], MASKED)
            load(io["strip"], stripsb[:], strip_io)
            pool.wait_ge(strip_io, 16)
            load(nbias[:], bass.AP(io["strip"].tensor, 0, [[1, P], [384, 16], [1, SEQ]]), nbias_in)
            pool.wait_ge(nbias_in, 16)
            for t, n in ((0, first_late), (1, N_CMP)):
                key = CMP_LEN - 1 + P * (1 - t)
                ins = g.tensor_copy(cbias[:, t, :, 0:n], nbias[:, :, key:key + CMP_STRIDE * (n - 1) + 1:CMP_STRIDE])
            ins.then_inc(cb_out, 1)
            pool.wait_ge(nys_lo, KT)
            load(growb[:], io["grows"][3:4, :].broadcast_to([P, D]), grow_in[3])
            post(2)
            pool.wait_ge(post_done, 3 * TT)
            load(grow2[:], io["grows"][4:5, :].broadcast_to([P, D]), grow_in[4])
            norm_pool(pool, 6)
            ffn_pool(1)
            post(3)

        @block.scalar
        def _(act):
            a = nc.scalar
            norm_act_squares(act, 0, lambda t: [(x_in[t], 16)])
            split_hi(act, 0)
            act.wait_ge(const_in, 16 * 2)
            norm_act_hi(act, 0, 0, 0, hh)
            for c in range(1, AHEAD):
                split_hi(act, c)

            def forget_act():
                act.wait_ge(dve_step, 2)
                a.activation(lam[:, 2:4], lam[:, 0:2], ACT.Exp).then_inc(act_step, 1)
                act.wait_ge(f_in, 1)
                a.activation(fz[:, 1], fz[:, 0], ACT.Abs).then_inc(f_e, 1)
                act.wait_ge(f_e, 1)
                a.activation(fz[:, 1], fz[:, 1], ACT.Exp, scale=-1.0).then_inc(f_e, 1)
                act.wait_ge(f_e, 2)
                a.activation(fz[:, 1], fz[:, 1], ACT.Ln, bias=1.0).then_inc(f_e, 1)

            def q_out(p):
                g = GROUP["qkv"] + 3 * p
                act.wait_ge(mm_done, 3 * p + 1)
                wait(act, scores_done, p - 1)
                bank = acc[g % 2]
                if p < 5:
                    for half in range(2):
                        ins = a.activation(
                            q_b[0:HD, p % 2].rearrange("p (s h) n -> p s h n", h=2)[:, :, half, :],
                            bank[HD * half:HD * half + HD, :].rearrange("p (s n) -> p s n", s=2),
                            ACT.Copy, scale=HD ** -0.5)
                    ins.then_inc(acc_out[g % 2], 1)
                else:
                    act.wait_ge(scores_done, 5)
                    for head in range(4):
                        for comp in range(2):
                            ins = a.activation(q_b[0:32, (p + comp) % 2, head, :],
                                               bank[32 * head:32 * head + 32, comp * SEQ:(comp + 1) * SEQ],
                                               ACT.Copy, scale=32 ** -0.5)
                    ins.then_inc(acc_out[g % 2], 1)

            def v_out(p):
                g = GROUP["qkv"] + 3 * p + 2
                act.wait_ge(mm_done, 3 * p + 3)
                wait(act, pv_done, p - 1)
                a.activation(v_b[:, p % 2].rearrange("p t n -> p (t n)"), acc[g % 2][:],
                             ACT.Copy).then_inc(acc_out[g % 2], 1)

            def exps(b):
                if b == 0:
                    t = pt_b1[:].rearrange("p a n -> p (a n)")
                    act.wait_ge(scores_out, 1)
                    a.activation(t, s_b1[:], ACT.Abs).then_inc(sb_l, 1)
                    act.wait_ge(sb_l, 1)
                    a.activation(t, t, ACT.Exp, scale=-1.0).then_inc(sb_l, 1)
                    act.wait_ge(sb_l, 2)
                    a.activation(t, t, ACT.Ln, bias=1.0).then_inc(sb_l, 1)
                    return
                act.wait_ge(probs_max, 2 * b)
                for t in range(TT):
                    for h in range(4):
                        w = P * (t + 1)
                        lo = h * P if t == 0 else 512 + h * SEQ
                        ins = a.activation(s_b1[:, lo:lo + w], s_b1[:, lo:lo + w], ACT.Exp,
                                           bias=negmax[:, b, 4 * t + h:4 * t + h + 1],
                                           accum_out=rowsum[:, b, 4 * t + h:4 * t + h + 1])
                ins.then_inc(probs_ready, 1)

            def pt_out(b):
                for j in range(3):
                    act.wait_ge(probs_turned, 3 * b + j + 1)
                    a.activation(pt_b1[:, j, :], aux[:, (3, 4, 0)[j], :], ACT.Copy).then_inc(pt_ready, 1)

            for p in range(6):
                split_hi(act, 3 * p + 3)
                q_out(p)
                split_hi(act, 3 * p + 4)
                if p == 0:
                    forget_act()
                if p == 1:
                    act.wait_ge(sb_e, 1)
                    a.activation(s_b1[:], s_b1[:], ACT.Exp).then_inc(probs_ready, 1)
                if p > 1:
                    pt_out(p - 1)
                split_hi(act, 3 * p + 5)
                v_out(p)
                if p == 1:
                    pt_out(0)
                exps(p)
                if p == 4:
                    act.wait_ge(sb_c, 1)
                    a.activation(small[:, 2:5, :], small[:, 2:5, :], ACT.Exp).then_inc(act_step, 1)

            def gate_out(c):
                n = c - START["gates"]
                g = n + GROUP["gates"]
                wait(act, mm_done, c + 1)
                a.activation(gate[:, bass.ds((n * 2).value, 2), :].rearrange("p k n -> p (k n)"), acc[g.mod(2)][:],
                             ACT.Sigmoid).then_inc(acc_out[g.mod(2)], 1)

            c = START["gates"]
            split_hi(act, c + 3)
            gate_out(At(c))
            pt_out(5)
            split_hi(act, c + 4)
            gate_out(At(c + 1))
            split_hi(act, c + 5)
            exps(6)
            gate_out(At(c + 2))
            split_hi(act, c + 6)
            gate_out(At(c + 3))
            pt_out(6)
            with act.Fori(0, 3) as it:
                for s in range(4):
                    cc = At(c + 4 + s, 4, it)
                    split_hi(act, cc + 3)
                    gate_out(cc)
            for k in range(KT):
                if k % 2 == 0:
                    act.wait_ge(ys_turned, k // 2 + 1)
                a.activation(ysh1[:, k, :], aux[:, k // 2, (k % 2) * SEQ:(k % 2 + 1) * SEQ], ACT.Copy).then_inc(ys_hi, 1)
            for i in range(4):
                split_hi(act, START["branch"] + i + 3)
            for j in range(4):
                act.wait_ge(mix_ready, j + 1)
                a.activation(hh[:, 2 * j:2 * j + 2, :], gate[:, 2 * j:2 * j + 2, :], ACT.Copy).then_inc(norm_hi, 1)
            for i in range(4):
                split_hi(act, START["out"] + i + 3)

            def norm(n, extra, slot, dst, x_waits):
                norm_act_squares(act, n, x_waits)
                hi_part(n, slot, dst)

            def hi_part(n, slot, dst):
                m = n if n < 3 else n - 1
                for k in range(KT):
                    if k % 2 == 0:
                        act.wait_ge(turned, 4 * m + k // 2 + 1)
                    a.activation(dst[:, k, :], aux[:, k // 2, (k % 2) * SEQ:(k % 2 + 1) * SEQ], ACT.Copy,
                                 scale=gains[:, slot, k:k + 1]).then_inc(norm_hi, 1)

            def x_after(name):
                g = GROUP[name] + GROUP_COUNT[name] - 1
                return lambda t: [(acc_out[g % 2], g // 2 + 1), (acc_out[(g - 1) % 2], (g - 1) // 2 + 1)]

            norm(1, 4, 1, hh, x_after("out"))
            with act.Fori(0, 4) as it:
                for s in range(4):
                    c = At(START["up"] + s, 4, it)
                    n = At(s, 4, it)
                    g = At(GROUP["up"] + s, 4, it)
                    split_hi(act, c + 3)
                    wait(act, mm_done, c + 1)
                    a.activation(r1[:, s % 2, 0].rearrange("p a n -> p (a n)"), acc[g.mod(2)][:], ACT.Relu
                                 ).then_inc(acc_out[g.mod(2)], 1)
                    wait(act, sq_ready, n + 1)
                    a.activation(hid1h[:, bass.ds((n * 2).value, 2), :], r1[:, s % 2, 1], ACT.Copy).then_inc(hid_hi, 1)
            for i in range(16):
                split_hi(act, START["down"] + i + 3)
            norm_act_squares(act, 2, x_after("down"))
            norm(3, 0, 2, hh, lambda t: [(first_done, t + 1)])
            def yt_out(h):
                for kk in range(4):
                    if kk % 2 == 0:
                        act.wait_ge(ry_turned, 2 * h + kk // 2 + 1)
                    a.activation(yth[:, 4 * h + kk, :], aux[:, 1 + kk // 2, (kk % 2) * SEQ:(kk % 2 + 1) * SEQ],
                                 ACT.Copy).then_inc(yt_hi, 1)

            for h in range(RET_HEADS):
                c0, g0 = START["ret"] + 6 * h, GROUP["ret"] + 6 * h
                for i in range(6):
                    split_hi(act, c0 + i + 3)
                    if i == 1 and h:
                        yt_out(h - 1)
                    g = g0 + i
                    if i in (2, 3):
                        act.wait_ge(mm_done, c0 + i + 1)
                        wait(act, ro_done, 2 * h)
                        a.activation(rv[:, :, (i - 2) * CW:(i - 1) * CW],
                                     acc[g % 2][:].rearrange("p (t n) -> p t n", t=2), ACT.Copy).then_inc(acc_out[g % 2], 1)
                    if i in (4, 5):
                        act.wait_ge(mm_done, c0 + i + 1)
                        wait(act, ro_y, 2 * h)
                        a.activation(rg[:, :, (i - 4) * CW:(i - 3) * CW],
                                     acc[g % 2][:].rearrange("p (t n) -> p t n", t=2), ACT.Silu).then_inc(acc_out[g % 2], 1)
                    if i == 4:
                        for t in range(TT):
                            act.wait_ge(ro_done, 2 * h + t + 1)
                            wait(act, ry_turned, 2 * h)
                            a.activation(ry[:, t, :], aux[:, 3 + t, :], ACT.Square,
                                         accum_out=small[:, 4, t:t + 1]).then_inc(ro_sq, 1)
            yt_out(RET_HEADS - 1)

            def post(n, name, per, junk):
                c0, g0 = START[name], GROUP[name]
                for cb in range(4):
                    for i in range(per):
                        split_hi(act, c0 + per * cb + i + 3)
                    act.wait_ge(mm_done, c0 + per * (cb + 1))
                    g = g0 + cb
                    wait(act, post_sq, 8 * n + 2 * cb)
                    for t in range(TT):
                        a.activation(junk[:, t, 0:CW], acc[g % 2][:, t * CW:(t + 1) * CW], ACT.Square, scale=D ** -0.5,
                                     accum_out=psums[:, t, cb:cb + 1]
                                     ).then_inc(post_sq, 1)

            def ffn_act(layer):
                name = f"ffn_in_{layer}"
                n0 = 16 + FFN_KT * layer

                def one(c, g, n, s, tile, first):
                    split_hi(act, c + 3)
                    wait(act, mm_done, c + 1)
                    a.activation(fsil[:, s % 2, :], acc[g.mod(2)][:, 0:SEQ], ACT.Silu).then_inc(sil_out, 1)
                    group_out(act, g)
                    a.activation(hid2h[:, tile, :], ft[:, s % 2:s % 2 + 1, :], ACT.Copy).then_inc(hid_hi, 1)
                with act.Fori(0, 5) as it:
                    for s in range(4):
                        one(At(START[name] + s, 4, it), At(GROUP[name] + s, 4, it), At(n0 + s, 4, it), s,
                            bass.ds(At(s, 4, it).value, 1), False)
                for s in range(20, 22):
                    one(At(START[name] + s), At(GROUP[name] + s), At(n0 + s), s, slice(s, s + 1), False)

            post(0, "ret_out", 2, ry)
            norm(4, 0, 3, hh, lambda t: [(post_done, t + 1)])
            ffn_act(0)
            post(1, "ffn_out_0", 3, ft)
            act.wait_ge(mm_done, START["kv"])
            for dst, src in ((relb[0:32, :], io["rel_bias"]), (relb[32:33, :], io["masked"]), (hot[:], io["hot"]),
                             (pe_in[:], io["pe_in"]), (w_gate[:], io["w_gate"])):
                act.dma_start(dst, src).then_inc(nsa_const, 16)
            norm_act_squares(act, 5, lambda t: [(post_done, TT + t + 1)])
            for slot, dst in ((6, kvh), (4, hh)):
                for k in range(KT):
                    if k % 2 == 0:
                        act.wait_ge(turned, 4 * 4 + k // 2 + 1)
                        if slot == 4:
                            act.wait_ge(norm_lo, 36 + k + 2)
                    a.activation(dst[:, k, :], aux[:, k // 2, (k % 2) * SEQ:(k % 2 + 1) * SEQ], ACT.Copy,
                                 scale=gains[:, slot, k:k + 1]).then_inc(norm_hi, 1)
            for i in range(6):
                split_hi(act, START["kv"] + i + 3)
                if i == 1:
                    act.wait_ge(ng_mm, 1)
                    a.activation(gate_f[:].rearrange("p (t n) -> p t n", t=2),
                                 aux[0:48, 0, 0:SEQ].rearrange("p (t n) -> p t n", t=2)[:, :, ::-1],
                                 ACT.Sigmoid).then_inc(ng_out, 1)
            for i in range(4):
                split_hi(act, START["cmp"] + i + 3)
            def n_exps(b):
                act.wait_ge(n_max, b + 1)
                if b % 3 == 2:
                    a.activation(ns[:, b % 2, 0:8 * N_CMP], ns[:, b % 2, 0:8 * N_CMP], ACT.Exp).then_inc(n_exp, 1)
                    return
                for t in range(TT):
                    for h in range(4):
                        w = P * (t + 1)
                        lo = h * P if t == 0 else 512 + h * SEQ
                        ins = a.activation(ns[:, b % 2, lo:lo + w], ns[:, b % 2, lo:lo + w], ACT.Exp,
                                           bias=negmax[:, b % 4, 4 * t + h:4 * t + h + 1],
                                           accum_out=rowsum[:, b % 4, 4 * t + h:4 * t + h + 1])
                ins.then_inc(n_exp, 1)

            def n_pt_out(b):
                for i, j in enumerate(n_turn_order(b)):
                    act.wait_ge(n_turn, n_turns_before(b) + i + 1)
                    rows = N_CMP if b % 3 == 2 else P
                    a.activation(npt[0:rows, j, :], n_turn_bank(b, j)[0:rows], ACT.Copy).then_inc(n_pt, 1)

            def nq_out(i):
                g = GROUP["nsa_q"] + i
                act.wait_ge(mm_done, START["nsa_q"] + i + 1)
                bank = acc[g % 2]
                for half in range(2):
                    ins = a.activation(nq[:, i].rearrange("p (s h) (t n) -> p s h t n", h=2, t=2)[:, :, half],
                                       backwards(bank[HD * half:HD * half + HD, :]
                                                 .rearrange("p (s t n) -> p s t n", s=2, t=2)),
                                       ACT.Copy, scale=HD ** -0.5)
                ins.then_inc(acc_out[g % 2], 1)

            def hidden(i):
                act.wait_ge(cmp_b, i + 1)
                for sub in range(2):
                    a.activation(hidc[:, i, sub, :], aux[:, 2 + i, 64 * sub:64 * sub + 60], ACT.Silu,
                                 bias=peb[:, i, sub:sub + 1]).then_inc(cmp_hid, 1)

            q = START["nsa_q"]
            split_hi(act, q + 3)
            hidden(0)
            nq_out(0)
            split_hi(act, q + 4)
            hidden(1)
            nq_out(1)
            split_hi(act, q + 5)
            n_exps(0)
            nq_out(2)
            n_pt_out(0)
            split_hi(act, q + 6)
            n_exps(1)
            nq_out(3)
            for b in range(1, 12):
                n_pt_out(b)
                if b + 1 < 12:
                    n_exps(b + 1)
            for k in range(KT):
                if k % 2 == 0:
                    act.wait_ge(nys_turned, k // 2 + 1)
                a.activation(ysh2[:, k, :].rearrange("p (t n) -> p t n", t=2), turned_back(k), ACT.Copy).then_inc(nys_hi, 1)
            post(2, "nsa_out", 1, o_n)
            norm(6, 0, 5, hh, lambda t: [(post_done, 2 * TT + t + 1)])
            ffn_act(1)
            post(3, "ffn_out_1", 3, ft)

        @block.vector
        def _(dve):
            v = nc.vector
            steps = [0]

            def chain(ins):
                steps[0] += 1
                ins.then_inc(dve_step, 1)
                dve.wait_ge(dve_step, steps[0])

            dve.wait_ge(const_in, 16 * 2)
            norm_dve_scale(dve, 0)
            split_lo(dve, 0)
            norm_dve_lo(dve, 0, 0, hl, hh)
            for c in range(1, AHEAD):
                split_lo(dve, c)
            dve.wait_ge(table_in, 16 * 6)
            chain(v.tensor_tensor(lamp[:], lams[:, 0:4:2, :], lams[:, 1:4:2, :], ALU.mult))
            chain(v.tensor_reduce(lam[:, 0:2], lamp[:], AX_X, ALU.add))
            v.tensor_copy(wfh[:], w_f[:]).then_inc(wf_ready, 1)
            dve.wait_ge(wf_ready, 1)
            v.tensor_tensor(wfl[:], w_f[:], wfh[:].bitcast(F32), ALU.subtract).then_inc(wf_ready, 1)

            def forget_z():
                dve.wait_ge(f_done, 1)
                v.tensor_scalar(fz[:, 0], aux[0:4, 4, 0:SEQ], b_f[:, 0:1], -1.0, ALU.add, ALU.mult).then_inc(f_in, 1)

            def forget_sums():
                for b in (q_b, k_b):
                    v.memset(b[HD:HD + 2, 0, :, :], 1.0)
                dve.wait_ge(f_e, 3)
                chain(v.scalar_tensor_tensor(fz[:, 0], fz[:, 0], 0.0, fz[:, 1], ALU.max, ALU.add))
                chain(v.tensor_tensor_scan(cum[:, 1], fz[:, 0], fz[:, 0], 0.0, ALU.add, ALU.max))
                v.tensor_scalar(cum[:, 0], cum[:, 1], -1.0, None, ALU.mult).then_inc(cum_out, 1)
                dve.wait_ge(act_step, 1)
                chain(v.tensor_tensor(lam[:, 4:5], lam[:, 2:3], lam[:, 3:4], ALU.subtract))
                chain(v.tensor_scalar(lam[:, 5:6], lam[:, 4:5], LAMBDA_INIT, -1.0, ALU.add, ALU.mult))

            def k_out(p):
                g = GROUP["qkv"] + 3 * p + 1
                dve.wait_ge(mm_done, 3 * p + 2)
                wait(dve, scores_done, p - 1)
                bank = acc[g % 2]
                if p < 5:
                    for half in range(2):
                        ins = v.tensor_copy(k_b[0:HD, p % 2].rearrange("p (s h) n -> p s h n", h=2)[:, :, half, :],
                                            bank[HD * half:HD * half + HD, :].rearrange("p (s n) -> p s n", s=2))
                    ins.then_inc(acc_out[g % 2], 1)
                else:
                    dve.wait_ge(scores_done, 5)
                    for head in range(4):
                        for comp in range(2):
                            ins = v.tensor_copy(k_b[0:32, (p + comp) % 2, head, :],
                                                bank[32 * head:32 * head + 32, comp * SEQ:(comp + 1) * SEQ])
                    ins.then_inc(acc_out[g % 2], 1)

            def heads(ap):
                return ap.rearrange("p (h n) -> p h n", h=4)

            def softmax_in(b):
                dve.wait_ge(scores_done, b + 1)
                dve.wait_ge(bias_in[b % 2], 16 * (b // 2 + 1))
                wait(dve, probs_turned, 3 * b)
                bias = bias_b[:, b % 2]
                chain(v.tensor_tensor(heads(s_b1[:, 0:512]), heads(aux[:, 0, :]), bias[:, :, P:SEQ], ALU.add))
                ins = v.tensor_tensor(s_b1[:, 512:1536].rearrange("p (h n) -> p h n", h=4),
                                      aux[:, 1:3, :].rearrange("p a (h n) -> p (a h) n", h=2), bias, ALU.add)
                ins.then_inc(scores_out, 1)
                dve.wait_ge(scores_out, b + 1)
                if b == 0:
                    t = pt_b1[:].rearrange("p a n -> p (a n)")
                    dve.wait_ge(sb_l, 3)
                    chain(v.scalar_tensor_tensor(t, s_b1[:], 0.0, t, ALU.max, ALU.add))
                    for tt in range(TT):
                        for h in range(4):
                            w = P * (tt + 1)
                            lo = h * P if tt == 0 else 512 + h * SEQ
                            seg = t[:, lo:lo + w][:, ::-1]
                            ins = v.tensor_tensor_scan(seg, seg, seg, 0.0, ALU.add, ALU.max)
                    chain(ins)
                    v.tensor_tensor(s_b1[:], s_b1[:], t, ALU.subtract).then_inc(sb_e, 1)
                    return
                v.tensor_reduce(negmax[:, b, 0:4], heads(s_b1[:, 0:512]), AX_X, ALU.max, negate=True).then_inc(probs_max, 1)
                v.tensor_reduce(negmax[:, b, 4:8], heads(s_b1[:, 512:1536]), AX_X, ALU.max, negate=True).then_inc(probs_max, 1)

            def cols(ap, branch):
                return ap[:, :, branch * CW:(branch + 1) * CW].rearrange("p t (h d) -> p t h d", h=4)

            def per_row(c):
                return c.rearrange("p (t h a) -> p t h a", t=2, a=1).broadcast_to([P, 2, 4, HD])

            def o_bank():
                return aux[:, 5, :].rearrange("p (t h d) -> p t h d", t=2, h=4)

            def og_of(i):
                return og[:, i].rearrange("p t (h d) -> p t h d", h=4)

            def attn_out(b):
                dve.wait_ge(pv_done, b + 1)
                if b == 0:
                    v.tensor_copy(cols(ys1, 0), o_bank()).then_inc(o_out, 1)
                elif b < 4:
                    v.tensor_copy(og_of(b - 1), o_bank()).then_inc(o_out, 1)
                elif b == 4:
                    chain(v.reciprocal(coef[:, 4, :], rowsum[:, 4, :]))
                    v.tensor_tensor(cols(ys1, 2), o_bank(), per_row(coef[:, 4, :]), ALU.mult).then_inc(o_out, 1)
                elif b == 5:
                    chain(v.reciprocal(coef[:, 5, :], rowsum[:, 5, :]))
                    v.tensor_tensor(og_of(0), o_bank(), per_row(coef[:, 5, :]), ALU.mult).then_inc(o_out, 1)
                else:
                    chain(v.reciprocal(coef[:, 6, :], rowsum[:, 6, :]))
                    chain(v.tensor_scalar(coef[:, 7, :], coef[:, 6, :], lam[:, 5:6], None, ALU.mult))
                    v.tensor_tensor(og_of(1), o_bank(), per_row(coef[:, 7, :]), ALU.mult).then_inc(o_out, 1)

            def dilated():
                m = small[:, 0, :]
                dve.wait_ge(o_out, 4)
                chain(v.tensor_tensor(small[:, 1, :], negmax[:, 1, :], negmax[:, 2, :], ALU.min))
                chain(v.tensor_tensor(m, small[:, 1, :], negmax[:, 3, :], ALU.min))
                for i in range(3):
                    ins = v.tensor_tensor(small[:, 2 + i, :], m, negmax[:, 1 + i, :], ALU.subtract)
                ins.then_inc(sb_c, 1)
                dve.wait_ge(act_step, 2)
                for i in range(3):
                    ins = v.tensor_tensor(small[:, 5 + i, :], small[:, 2 + i, :], rowsum[:, 1 + i, :], ALU.mult)
                chain(ins)
                chain(v.tensor_tensor(small[:, 5, :], small[:, 5, :], small[:, 6, :], ALU.add))
                chain(v.tensor_tensor(small[:, 5, :], small[:, 5, :], small[:, 7, :], ALU.add))
                chain(v.reciprocal(small[:, 6, :], small[:, 5, :]))
                for i in range(3):
                    ins = v.tensor_tensor(coef[:, i, :], small[:, 2 + i, :], small[:, 6, :], ALU.mult)
                chain(ins)
                for i in range(3):
                    ins = v.tensor_tensor(og_of(i), og_of(i), per_row(coef[:, i, :]), ALU.mult)
                chain(ins)
                chain(v.tensor_tensor(og[:, 0], og[:, 0], og[:, 1], ALU.add))
                chain(v.tensor_tensor(ys1[:, :, CW:2 * CW], og[:, 0], og[:, 2], ALU.add))

            def differential():
                dve.wait_ge(o_out, 7)
                chain(v.tensor_tensor(og[:, 2], og[:, 0], og[:, 1], ALU.add))
                chain(v.tensor_tensor(og[:, 0], og[:, 2], og[:, 2], ALU.mult))
                v.tensor_reduce(small[:, 1, :], og_of(0).rearrange("p t h d -> p (t h) d"), AX_X, ALU.add).then_inc(ro_sq, 1)
                chain(v.tensor_tensor(og_of(1), og_of(2), diff_g[:].rearrange("p (a b d) -> p a b d", a=1, b=1)
                                      .broadcast_to([P, 2, 4, HD]), ALU.mult))
                dve.wait_ge(ro_r, 1)
                chain(v.tensor_scalar(small[:, 3, :], small[:, 2, :], 1.0 - LAMBDA_INIT, None, ALU.mult))
                v.tensor_tensor(cols(ys1, 3), og_of(1), per_row(small[:, 3, :]), ALU.mult).then_inc(ys_ready, 1)

            for p in range(6):
                split_lo(dve, 3 * p + 3)
                if p == 0:
                    forget_z()
                split_lo(dve, 3 * p + 4)
                k_out(p)
                if p == 0:
                    forget_sums()
                split_lo(dve, 3 * p + 5)
                if p:
                    attn_out(p - 1)
                softmax_in(p)
                if p == 4:
                    dilated()
            c = START["gates"]
            split_lo(dve, c + 3)
            split_lo(dve, c + 4)
            attn_out(5)
            softmax_in(6)
            split_lo(dve, c + 5)
            split_lo(dve, c + 6)
            attn_out(6)
            differential()
            with dve.Fori(0, 3) as it:
                for s in range(4):
                    split_lo(dve, At(c + 7 + s, 4, it))
            for k in range(KT):
                if k % 2 == 0:
                    dve.wait_ge(ys_hi, k + 2)
                v.tensor_tensor(ysl1[:, k, :], aux[:, k // 2, (k % 2) * SEQ:(k % 2 + 1) * SEQ],
                                ysh1[:, k, :].bitcast(F32), ALU.subtract).then_inc(ys_lo, 1)
            def mix_lo(j):
                dve.wait_ge(norm_hi, KT + j + 1)
                v.tensor_tensor(hl[:, 2 * j:2 * j + 2, :], gate[:, 2 * j:2 * j + 2, :],
                                hh[:, 2 * j:2 * j + 2, :].bitcast(F32), ALU.subtract).then_inc(norm_lo, 1)

            for n in range(4):
                for j in range(4):
                    if j == 2 and n < 3:
                        split_lo(dve, START["branch"] + n + 3)
                    m = 4 * n + j
                    if j < 3:
                        dve.wait_ge(branch_done, 3 * n + j + 1)
                    else:
                        dve.wait_ge(mm_done, START["branch"] + n + 1)
                    if n == 0:
                        group_out(dve, GROUP["gates"] + 14)
                        group_out(dve, GROUP["gates"] + 15)
                    gg = gate[:, n * KT + 2 * j:n * KT + 2 * j + 2, :].rearrange("p k n -> p (k n)")
                    v.tensor_tensor(gg, gg, branch_bank(m), ALU.mult).then_inc(branch_out, 1)
                    if n == 3:
                        dve.wait_ge(mix_sum, 4 + j + 1)
                        dve.wait_ge(branch_out, m + 1)
                        aa = gate[:, 2 * j:2 * j + 2, :]
                        v.tensor_tensor(aa, aa, gate[:, n * KT + 2 * j:n * KT + 2 * j + 2, :], ALU.add).then_inc(mix_ready, 1)
                        if j:
                            mix_lo(j - 1)
            mix_lo(3)
            split_lo(dve, START["branch"] + 6)

            def add_to_x(name, per):
                c0, g0 = START[name], GROUP[name]
                for cb in range(4):
                    for i in range(per):
                        split_lo(dve, c0 + per * cb + i + 3)
                    g = g0 + cb
                    dve.wait_ge(mm_done, c0 + per * (cb + 1))
                    xs = x[:, :, cb * CW:(cb + 1) * CW]
                    v.tensor_tensor(xs, xs, acc[g % 2][:].rearrange("p (t n) -> p t n", t=2), ALU.add
                                    ).then_inc(acc_out[g % 2], 1)

            def lo_part(slot, dst, hi, before):
                for k in range(KT):
                    if k % 2 == 0:
                        dve.wait_ge(norm_hi, before + k + 2)
                    v.scalar_tensor_tensor(dst[:, k, :], aux[:, k // 2, (k % 2) * SEQ:(k % 2 + 1) * SEQ],
                                           gains[:, slot, k:k + 1], hi[:, k, :].bitcast(F32),
                                           ALU.mult, ALU.subtract).then_inc(norm_lo, 1)

            add_to_x("out", 1)
            norm_dve_scale(dve, 1)
            lo_part(1, hl, hh, 12)
            with dve.Fori(0, 4) as it:
                for s in range(4):
                    c = At(START["up"] + s, 4, it)
                    n = At(s, 4, it)
                    g = At(GROUP["up"] + s, 4, it)
                    split_lo(dve, c + 3)
                    wait(dve, acc_out[g.mod(2)], g.div(2) + 1)
                    wait(dve, hid_lo, n + 1)
                    rr = r1[:, s % 2, 0]
                    v.tensor_tensor(r1[:, s % 2, 1], rr, rr, ALU.mult).then_inc(sq_ready, 1)
            add_to_x("down", 4)
            dve.wait_ge(rstd_ready, 3 * TT)
            dve.wait_ge(grow_in[0], 16)
            for t in range(TT):
                v.scalar_tensor_tensor(x[:, t, :], x[:, t, :], rstd[:, t:t + 1], grow1[:], ALU.mult,
                                       ALU.mult).then_inc(first_done, 1)
            norm_dve_scale(dve, 3)
            lo_part(2, hl, hh, 20)
            dve.wait_ge(ret_const, 32)
            def yt_lo_out(h):
                for kk in range(4):
                    if kk % 2 == 0:
                        dve.wait_ge(yt_hi, 4 * h + kk + 2)
                    v.tensor_tensor(ytl[:, 4 * h + kk, :], aux[:, 1 + kk // 2, (kk % 2) * SEQ:(kk % 2 + 1) * SEQ],
                                    yth[:, 4 * h + kk, :].bitcast(F32), ALU.subtract).then_inc(yt_lo, 1)

            for h in range(RET_HEADS):
                c0, g0 = START["ret"] + 6 * h, GROUP["ret"] + 6 * h
                for i in range(6):
                    split_lo(dve, c0 + i + 3)
                    g = g0 + i
                    if i < 2:
                        dve.wait_ge(mm_done, c0 + i + 1)
                        wait(dve, rot_out, 2 * h + i)
                        both = acc[g % 2][:].rearrange("p (a n) -> p a n", a=2)
                        v.tensor_tensor(ra[:, 0], both, cs[:, 0:1, :].broadcast_to([P, 2, SEQ]), ALU.mult)
                        v.tensor_tensor(ra[:, 1], both, cs[:, 1:2, :].broadcast_to([P, 2, SEQ]), ALU.mult
                                        ).then_inc(acc_out[g % 2], 1)
                    if i == 1 and h:
                        yt_lo_out(h - 1)
                    if i == 2:
                        dve.wait_ge(st_done, h + 1)
                        wait(dve, ro_done, 2 * h)
                        v.tensor_tensor(rst[:, 0:SEQ], aux[:, 0, 0:SEQ], decay[:, h, :], ALU.mult)
                        v.tensor_tensor(rst[:, SEQ:384], aux[:, 0, SEQ:384], decay[:, h, 0:P], ALU.mult).then_inc(st_out, 1)
                for t in range(TT):
                    dve.wait_ge(ro_r, 1 + h + 1)
                    dve.wait_ge(ro_sq, 1 + 2 * (h + 1))
                    if t == 0:
                        for i in (4, 5):
                            group_out(dve, g0 + i)
                    v.scalar_tensor_tensor(ry[:, t, :], aux[:, 3 + t, :], small[:, 5, t:t + 1], rg[:, t, :],
                                           ALU.mult, ALU.mult).then_inc(ro_y, 1)
            yt_lo_out(RET_HEADS - 1)

            def post(n, name, per, mixed, grow):
                c0, g0 = START[name], GROUP[name]
                dve.wait_ge(grow_in[n + 1], 16)
                for cb in range(4):
                    for i in range(per):
                        split_lo(dve, c0 + per * cb + i + 3)
                    g = g0 + cb
                    dve.wait_ge(post_sq, 8 * n + 2 * cb + 2)
                    if cb == 3:
                        v.tensor_reduce(psum1[:], psums[:], AX_X, ALU.add).then_inc(post_step, 1)
                    cols = slice(cb * CW, (cb + 1) * CW)
                    v.tensor_tensor(mixed[:, :, cols], acc[g % 2][:].rearrange("p (t n) -> p t n", t=2),
                                    grow[:, cols].rearrange("p (a n) -> p a n", a=1).broadcast_to([P, TT, CW]), ALU.mult
                                    ).then_inc(acc_out[g % 2], 1)
                group_out(dve, g0 + 2)
                group_out(dve, g0 + 3)
                dve.wait_ge(post_r, n + 1)
                for t in range(TT):
                    v.scalar_tensor_tensor(x[:, t, :], mixed[:, t, :], rstd[:, t:t + 1], x[:, t, :], ALU.mult,
                                           ALU.add).then_inc(post_done, 1)

            def ffn_dve(layer):
                name = f"ffn_in_{layer}"
                n0 = 16 + FFN_KT * layer
                s0 = FFN_KT * layer

                def one(c, g, n, m, s):
                    split_lo(dve, c + 3)
                    wait(dve, sil_out, m + 1)
                    wait(dve, hid_lo, n + 1)
                    v.tensor_tensor(ft[:, s % 2, :], fsil[:, s % 2, :], acc[g.mod(2)][:, SEQ:2 * SEQ], ALU.mult
                                    ).then_inc(acc_out[g.mod(2)], 1)
                with dve.Fori(0, 5) as it:
                    for s in range(4):
                        one(At(START[name] + s, 4, it), At(GROUP[name] + s, 4, it), At(n0 + s, 4, it), At(s0 + s, 4, it),
                            s)
                for s in range(20, 22):
                    one(At(START[name] + s), At(GROUP[name] + s), At(n0 + s), At(s0 + s), s)

            dve.wait_ge(setup, 2)
            post(0, "ret_out", 2, mixed0, grow0)
            norm_dve_scale(dve, 4)
            lo_part(3, hl, hh, 28)
            ffn_dve(0)
            post(1, "ffn_out_0", 3, mixed2, grow2)
            norm_dve_scale(dve, 5)
            lo_part(6, kvl, kvh, 36)
            lo_part(4, hl, hh, 36 + KT)
            kv, g0 = START["kv"], GROUP["kv"]

            def t2_take(i):
                g = g0 + i
                dve.wait_ge(mm_done, kv + i + 1)
                if i:
                    dve.wait_ge(gath, 4 * i)
                bank = acc[g % 2]
                for half in range(2):
                    for sh in range(2):
                        ins = v.tensor_copy(
                            t2[HD * sh:HD * sh + HD].rearrange("p (s h) n -> p s h n", h=2)[:, :, half, 0:SEQ - sh],
                            bank[HD * half:HD * half + HD, :].rearrange("p (s n) -> p s n", s=2)[:, :, sh:SEQ])
                ins.then_inc(acc_out[g % 2], 1)
                dve.wait_ge(acc_out[g % 2], g // 2 + 1)
                src = t2[:].rearrange("p g (n r) -> p r g n", r=CMP_STRIDE)
                for half in range(2):
                    s_ap = src[:, 0:CMP_STRIDE:2, :, half:half + N_CMP]
                    v.tensor_copy(rgh[:, i, 8 * half:8 * half + 8, 0:60].rearrange("p j (g n) -> p j g n", g=4), s_ap
                                  ).then_inc(gath, 1)
                v.tensor_copy(rgh[:, i, :, 60:62], pe_in[:, i]).then_inc(gath, 1)
                dve.wait_ge(gath, 4 * i + 3)
                for half in range(2):
                    s_ap = src[:, 0:CMP_STRIDE:2, :, half:half + N_CMP]
                    part = lambda r: r[:, i, 8 * half:8 * half + 8, 0:60].rearrange("p j (g n) -> p j g n", g=4)
                    v.tensor_tensor(part(rgl), s_ap, part(rgh).bitcast(F32), ALU.subtract)
                v.tensor_tensor(rgl[:, i, :, 60:62], pe_in[:, i], rgh[:, i, :, 60:62].bitcast(F32), ALU.subtract).then_inc(gath, 1)

            def plain_k(i, dst):
                g = g0 + i
                dve.wait_ge(mm_done, kv + i + 1)
                for half in range(2):
                    ins = v.tensor_copy(dst.rearrange("p (s h) n -> p s h n", h=2)[:, :, half, :],
                                        acc[g % 2][HD * half:HD * half + HD, :].rearrange("p (s n) -> p s n", s=2))
                ins.then_inc(acc_out[g % 2], 1)

            def plain_v(i, dst):
                g = g0 + i
                dve.wait_ge(mm_done, kv + i + 1)
                v.tensor_copy(dst.rearrange("p t n -> p (t n)"), acc[g % 2][:]).then_inc(acc_out[g % 2], 1)

            def cmp_bias(j):
                dve.wait_ge(cmp_turned, j + 1)
                v.tensor_copy(peb[:, j, 0:2], aux[:, 2 + j, 60:125:64]).then_inc(cmp_b, 1)

            def cmp_out(j):
                dve.wait_ge(mm_done, START["cmp"] + 2 * (j + 1))
                v.tensor_copy(cmp_s[:, j], aux[0:62, j, 0:CW]).then_inc(cmp_raw, 1)

            dve.wait_ge(nsa_const, 16 * 5)
            v.tensor_copy(wgh[:], w_gate[:]).then_inc(wg_ready, 1)
            dve.wait_ge(wg_ready, 1)
            v.tensor_tensor(wgl[:], w_gate[:], wgh[:].bitcast(F32), ALU.subtract).then_inc(wg_ready, 1)
            split_lo(dve, kv + 3)
            t2_take(0)
            split_lo(dve, kv + 4)
            t2_take(1)
            split_lo(dve, kv + 5)
            dve.wait_ge(strip_mm, 1)
            v.tensor_copy(stripsb[:], aux[0:16, 4, 0:384]).then_inc(strip_out, 1)
            plain_k(2, ksw[:, 0])
            split_lo(dve, kv + 6)
            plain_v(3, vsw[:, 0])
            split_lo(dve, kv + 7)
            plain_k(4, ksw[:, 1])
            split_lo(dve, kv + 8)
            plain_v(5, vsw[:, 1])
            for j in range(2):
                split_lo(dve, START["cmp"] + 2 * j + 3)
                split_lo(dve, START["cmp"] + 2 * j + 4)
                cmp_out(j)
            def n_softmax(b):
                g, kind = n_batch(b)
                dve.wait_ge(n_scores, b + 1)
                if b == 0:
                    dve.wait_ge(nbias_in, 16)
                nm, nsb = negmax[:, b % 4, :], ns[:, b % 2]
                if kind < 2:
                    bias = nbias[:, 4 * g:4 * g + 4, :]
                    chain(v.tensor_tensor(heads(nsb[:, 0:512]), heads(aux[:, 0, :]), bias[:, :, P:SEQ], ALU.add))
                    v.tensor_tensor(nsb[:, 512:1536].rearrange("p (h n) -> p h n", h=4),
                                    aux[:, 1:3, :].rearrange("p a (h n) -> p (a h) n", h=2), bias, ALU.add
                                    ).then_inc(n_sout, 1)
                    dve.wait_ge(n_sout, b + 1)
                    v.tensor_reduce(nm[:, 0:4], heads(nsb[:, 0:512]), AX_X, ALU.max, negate=True)
                    v.tensor_reduce(nm[:, 4:8], heads(nsb[:, 512:1536]), AX_X, ALU.max, negate=True).then_inc(n_max, 1)
                else:
                    if b == 2:
                        dve.wait_ge(cb_out, 1)
                    s = nsb[:, 0:120].rearrange("p (t h n) -> p t h n", t=2, h=4)
                    v.tensor_tensor(s, aux[:, 0, 0:120].rearrange("p (t h n) -> p t h n", t=2, h=4),
                                    cbias[:, :, 4 * g:4 * g + 4, :], ALU.add).then_inc(n_sout, 1)
                    dve.wait_ge(n_sout, b + 1)
                    rows = nsb[:, 0:120].rearrange("p (t n) -> p t n", n=N_CMP)
                    chain(v.tensor_reduce(nm, rows, AX_X, ALU.max, negate=True))
                    chain(v.tensor_scalar(nm, nm, 1e20, None, ALU.min))
                    v.tensor_tensor(rows, rows, nm.rearrange("p (t a) -> p t a", a=1).broadcast_to([P, 8, N_CMP]),
                                    ALU.add).then_inc(n_max, 1)

            def n_out(b):
                g, kind = n_batch(b)
                dve.wait_ge(n_pv, b + 1)
                cc = coef[:, b % 2, :]
                which = (1, 2, 0)[kind]
                chain(v.tensor_scalar(small[:, 0, :], rowsum[:, b % 4, :], 1.1754944e-38, None, ALU.max))
                chain(v.reciprocal(small[:, 1, :], small[:, 0, :]))
                gg = gate_n[:, :, 12 * g:12 * g + 12].rearrange("p t (h b) -> p t h b", b=3)[:, :, :, which]
                chain(v.tensor_tensor(cc.rearrange("p (t h) -> p t h", t=2),
                                      small[:, 1, :].rearrange("p (t h) -> p t h", t=2), gg, ALU.mult))
                dst = cols(ys2, g)
                if kind == 0:
                    v.tensor_tensor(dst, o_bank(), per_row(cc), ALU.mult).then_inc(n_o, 1)
                else:
                    tmp = o_n[:].rearrange("p t (h d) -> p t h d", h=4)
                    v.tensor_tensor(tmp, o_bank(), per_row(cc), ALU.mult).then_inc(n_o, 1)
                    dve.wait_ge(n_o, b + 1)
                    ins = v.tensor_tensor(dst, dst, tmp, ALU.add)
                    if b == 11:
                        ins.then_inc(nys_ready, 1)
                    else:
                        chain(ins)

            q = START["nsa_q"]
            split_lo(dve, q + 3)
            cmp_bias(0)
            split_lo(dve, q + 4)
            cmp_bias(1)
            split_lo(dve, q + 5)
            dve.wait_ge(cmp_kv, 1)
            v.tensor_copy(kct[:], aux[0:HD, 4, 0:60])
            v.tensor_copy(vct[:], aux[0:N_CMP, 5, 0:256].rearrange("p (g d) -> p g d", g=4)).then_inc(kct_out, 1)
            dve.wait_ge(ng_mm, 2)
            chain(v.tensor_copy(gate_n[:].rearrange("p t n -> p (t n)"), aux[:, 3, 0:96]))
            n_softmax(0)
            split_lo(dve, q + 6)
            n_softmax(1)
            n_out(0)
            n_softmax(2)
            n_out(1)
            n_softmax(3)
            for b in range(2, 12):
                if b % 3 == 2:
                    dve.wait_ge(n_exp, b + 1)
                    chain(v.tensor_reduce(rowsum[:, b % 4, :], ns[:, b % 2, 0:120].rearrange("p (t n) -> p t n", n=N_CMP),
                                          AX_X, ALU.add))
                if b + 2 < 12:
                    n_softmax(b + 2)
                n_out(b)
            for k in range(KT):
                if k % 2 == 0:
                    dve.wait_ge(nys_hi, k + 2)
                v.tensor_tensor(ysl2[:, k, :].rearrange("p (t n) -> p t n", t=2), turned_back(k),
                                ysh2[:, k, :].bitcast(F32).rearrange("p (t n) -> p t n", t=2), ALU.subtract).then_inc(nys_lo, 1)
            post(2, "nsa_out", 1, mixed1, growb)
            norm_dve_scale(dve, 6)
            lo_part(5, hl, hh, 52)
            ffn_dve(1)
            post(3, "ffn_out_1", 3, mixed2, grow2)

        @block.tensor
        def _(pe):
            pe.wait_ge(const_in, 16 * 2)
            norm_pe(pe, 0)

            def few_rows(h, l, n, bank):
                out = aux[0:n, bank, 0:SEQ]
                for k in range(KT):
                    mm(out, h[:, k, :], hh[:, k, :], start=(k == 0))
                    mm(out, h[:, k, :], hl[:, k, :])
                    last = mm(out, l[:, k, :], hh[:, k, :], stop=(k == KT - 1))
                return last

            def scores(b):
                p = min(b, 5)
                group_out(pe, GROUP["qkv"] + 3 * p)
                group_out(pe, GROUP["qkv"] + 3 * p + 1)
                wait(pe, scores_out, b)
                if b:
                    wait(pe, pt_ready, 3 * b if b < 6 else 3 * 6)
                n = 32 if b > 4 else HD
                if b == 4:
                    pe.wait_ge(cum_in, 32)
                    n = HD + 2
                q, k = q_b[0:n, b % 2], k_b[0:n, b % 2]
                for h in range(4):
                    for t in range(TT):
                        w = P * (t + 1)
                        out = (aux[:, 0, h * P:(h + 1) * P] if t == 0 else
                               aux[:, 1 + h // 2, (h % 2) * SEQ:(h % 2 + 1) * SEQ])
                        toks = slice(t * P, (t + 1) * P)
                        last = mm(out, q[:, h, toks], k[:, h, 0:w], start=True, stop=True)
                last.then_inc(scores_done, 1)

            def turn_probs(s, ready, count, turned_sem):
                wait(pe, ready, count)
                for j in range(3):
                    for h in range(4):
                        src = s[:, h * P:(h + 1) * P] if j == 0 else s[:, 512 + h * SEQ + (j - 1) * P:512 + h * SEQ + j * P]
                        tr = nc.tensor.transpose(aux[:, (3, 4, 0)[j], h * P:(h + 1) * P], src, ident[:])
                    tr.then_inc(turned_sem, 1)

            def turn(b):
                turn_probs(s_b1, probs_ready, b + 1, probs_turned)

            def pv(b):
                p = min(b, 5)
                group_out(pe, GROUP["qkv"] + 3 * p + 2)
                wait(pe, o_out, b)
                for h in range(4):
                    vh = lambda kt: v_b[:, p % 2, kt, h * HD:(h + 1) * HD]
                    if h == 0:
                        pe.wait_ge(pt_ready, 3 * b + 3)
                    mm(aux[:, 5, h * HD:(h + 1) * HD], pt_b1[:, 0, h * P:(h + 1) * P], vh(0), start=True, stop=True)
                    out = aux[:, 5, 256 + h * HD:256 + (h + 1) * HD]
                    mm(out, pt_b1[:, 1, h * P:(h + 1) * P], vh(0), start=True)
                    last = mm(out, pt_b1[:, 2, h * P:(h + 1) * P], vh(1), stop=True)
                last.then_inc(pv_done, 1)

            for p in range(6):
                product_t(pe, 3 * p, GROUP["qkv"] + 3 * p, hh, hl, None if p else normed(0))
                if p == 0:
                    pe.wait_ge(wf_ready, 2)
                    few_rows(wfh, wfl, 4, 4).then_inc(f_done, 1)
                product_t(pe, 3 * p + 1, GROUP["qkv"] + 3 * p + 1, hh, hl)
                if p > 1:
                    turn(p - 1)
                product_n(pe, 3 * p + 2, GROUP["qkv"] + 3 * p + 2, hh, hl)
                if p == 1:
                    turn(0)
                if p:
                    pv(p - 1)
                scores(p)
            c, g = START["gates"], GROUP["gates"]
            product_t(pe, c, g, hh, hl)
            turn(5)
            product_t(pe, c + 1, g + 1, hh, hl)
            pv(5)
            scores(6)
            product_t(pe, c + 2, g + 2, hh, hl)
            product_t(pe, c + 3, g + 3, hh, hl)
            turn(6)
            pv(6)
            with pe.Fori(0, 3) as it:
                for s in range(4):
                    product_t(pe, At(c + 4 + s, 4, it), At(g + 4 + s, 4, it), hh, hl)

            def turn_ys(ys, sem_, ready):
                pe.wait_ge(ready, 1)
                for k in range(KT):
                    for t in range(TT):
                        c0 = (k % 2) * SEQ + t * P
                        tr = nc.tensor.transpose(aux[:, k // 2, c0:c0 + P], ys[:, t, k * P:(k + 1) * P], ident[:])
                    if k % 2:
                        tr.then_inc(sem_, 1)

            turn_ys(ys1, ys_turned, ys_ready)
            for n in range(4):
                c = At(START["branch"] + n)
                take(pe, c)
                s = c.mod(SLOTS)
                for j in range(4):
                    m = 4 * n + j
                    wait(pe, branch_out, m - 3)
                    bank = branch_bank(m)
                    if m == 2:
                        group_out(pe, GROUP["gates"] + 15)
                        group_out(pe, GROUP["gates"] + 14)
                    for sub in range(2):
                        out = bank[:, sub * SEQ:(sub + 1) * SEQ]
                        for k in range(2):
                            if sub == 0:
                                pe.wait_ge(ys_lo, 2 * n + k + 1)
                            w = slice(k * D + (2 * j + sub) * P, k * D + (2 * j + sub + 1) * P)
                            mm(out, wh[:, s, w], ysh1[:, 2 * n + k, :], start=(k == 0))
                            mm(out, wh[:, s, w], ysl1[:, 2 * n + k, :])
                            last = mm(out, wl[:, s, w], ysh1[:, 2 * n + k, :], stop=(k == 1))
                    last.then_inc(branch_done if j < 3 else mm_done, 1)
            pe.wait_ge(branch_out, 16)
            for i in range(4):
                product_n(pe, START["out"] + i, GROUP["out"] + i, hh, hl,
                          ready=None if i else lambda k: (norm_lo, KT + k // 2 + 1))

            norm_pe(pe, 1)
            with pe.Fori(0, 4) as it:
                for s in range(4):
                    product_t(pe, At(START["up"] + s, 4, it), At(GROUP["up"] + s, 4, it), hh, hl,
                              None if s else normed(12))
            with pe.Fori(0, 2) as it:
                for cb in range(2):
                    for i in range(4):
                        product_n(pe, At(START["down"] + 4 * cb + i, 8, it), At(GROUP["down"] + cb, 2, it),
                                  hid1h, hid1l, KT * i, KT, 4 * KT,
                                  None if cb else lambda k: (hid_lo, 2 + k // 2 + 1))
            norm_pe(pe, 2)
            def turn_head(h):
                pe.wait_ge(ro_y, 2 * h + 2)
                wait(pe, yt_lo, 4 * h)
                for kk in range(4):
                    for t in range(TT):
                        cc = (kk % 2) * SEQ + t * P
                        tr = nc.tensor.transpose(aux[:, 1 + kk // 2, cc:cc + P], ry[:, t, kk * P:(kk + 1) * P], ident[:])
                    if kk % 2:
                        tr.then_inc(ry_turned, 1)

            for h in range(RET_HEADS):
                c0, g0 = START["ret"] + 6 * h, GROUP["ret"] + 6 * h
                product_t(pe, c0, g0, hh, hl, None if h else normed(20))
                if h:
                    turn_head(h - 1)
                product_t(pe, c0 + 1, g0 + 1, hh, hl)
                product_n(pe, c0 + 2, g0 + 2, hh, hl)
                pe.wait_ge(rot_out, 2 * h + 2)
                wait(pe, st_out, h)
                for half in range(2):
                    mm(aux[:, 0, 0:SEQ], rk[:, half, 0:P], rq[:, half, :], start=(half == 0), stop=(half == 1))
                for half in range(2):
                    last = mm(aux[:, 0, SEQ:384], rk[:, half, P:SEQ], rq[:, half, P:SEQ], start=(half == 0), stop=(half == 1))
                last.then_inc(st_done, 1)
                product_n(pe, c0 + 3, g0 + 3, hh, hl)
                product_n(pe, c0 + 4, g0 + 4, hh, hl)
                pe.wait_ge(st_out, h + 1)
                group_out(pe, g0 + 2)
                group_out(pe, g0 + 3)
                wait(pe, ro_y, 2 * h)
                mm(aux[:, 3, :], rst[:, 0:P], rv[:, 0, :], start=True, stop=True).then_inc(ro_done, 1)
                mm(aux[:, 4, :], rst[:, P:SEQ], rv[:, 0, :], start=True)
                mm(aux[:, 4, :], rst[:, SEQ:384], rv[:, 1, :], stop=True).then_inc(ro_done, 1)
                product_n(pe, c0 + 5, g0 + 5, hh, hl)
            turn_head(RET_HEADS - 1)
            for cb in range(4):
                for i in range(2):
                    product_n(pe, START["ret_out"] + 2 * cb + i, GROUP["ret_out"] + cb, yth, ytl, KT * i, KT, 2 * KT,
                              None if cb else lambda k: (yt_lo, k + 1))

            def ffn_pe(layer, before):
                i0, g0 = START[f"ffn_in_{layer}"], GROUP[f"ffn_in_{layer}"]
                with pe.Fori(0, 5) as it:
                    for s in range(4):
                        product_t(pe, At(i0 + s, 4, it), At(g0 + s, 4, it), hh, hl, None if s else normed(before))
                for s in range(20, 22):
                    product_t(pe, i0 + s, g0 + s, hh, hl)
                o0, g0 = START[f"ffn_out_{layer}"], GROUP[f"ffn_out_{layer}"]
                for cb in range(4):
                    for i in range(3):
                        product_n(pe, o0 + 3 * cb + i, g0 + cb, hid2h, hid2l, KT * i, min(KT, FFN_KT - KT * i), FFN_KT,
                                  None if cb else lambda k: (hid_lo, 2 + 16 + FFN_KT * layer + k + 1))

            norm_pe(pe, 3)
            ffn_pe(0, 28)
            norm_pe(pe, 4)
            kv, g0 = START["kv"], GROUP["kv"]
            product_t(pe, kv, g0, kvh, kvl, normed(36))
            pe.wait_ge(nsa_const, 16 * 5)
            pe.wait_ge(wg_ready, 2)
            pe.wait_ge(norm_lo, 36 + 2 * KT)
            few_rows(wgh, wgl, 48, 0).then_inc(ng_mm, 1)
            mm(aux[0:16, 4, 0:384], relb[:], hot[:], start=True, stop=True).then_inc(strip_mm, 1)
            product_t(pe, kv + 1, g0 + 1, kvh, kvl)
            product_t(pe, kv + 2, g0 + 2, kvh, kvl)
            product_n(pe, kv + 3, g0 + 3, kvh, kvl)
            product_t(pe, kv + 4, g0 + 4, kvh, kvl)
            product_n(pe, kv + 5, g0 + 5, kvh, kvl)
            pe.wait_ge(ng_out, 1)
            for i in range(2):
                pe.wait_ge(gath, 4 * (i + 1))
                for ch in range(2):
                    c = At(START["cmp"] + 2 * i + ch)
                    take(pe, c)
                    s = c.mod(SLOTS)
                    out = aux[0:62, i, 0:CW]
                    for jj in range(8):
                        j = 8 * ch + jj
                        w = slice(jj * CW, (jj + 1) * CW)
                        mm(out, rgh[:, i, j, :], wh[:, s, w], start=(j == 0))
                        mm(out, rgh[:, i, j, :], wl[:, s, w])
                        last = mm(out, rgl[:, i, j, :], wh[:, s, w], stop=(j == 15))
                    last.then_inc(mm_done, 1)

            def turn_cmp(j):
                pe.wait_ge(cmp_raw, j + 1)
                for sub in range(2):
                    tr = nc.tensor.transpose(aux[:, 2 + j, 64 * sub:64 * sub + 62], cmp_s[:, j, P * sub:P * (sub + 1)],
                                             ident[0:62, 0:62])
                tr.then_inc(cmp_turned, 1)

            turn_cmp(0)
            product_t(pe, START["nsa_q"], GROUP["nsa_q"], hh, hl)
            turn_cmp(1)
            product_t(pe, START["nsa_q"] + 1, GROUP["nsa_q"] + 1, hh, hl)
            pe.wait_ge(cmp_hid, 4)
            pe.wait_ge(strip_out, 1)
            for sub in range(2):
                mm(aux[0:HD, 4, 0:60], w2k[:, sub, :], hidc[:, 0, sub, :], start=(sub == 0), stop=(sub == 1))
            for g in range(GROUPS):
                for sub in range(2):
                    last = mm(aux[0:N_CMP, 5, g * HD:(g + 1) * HD], hidc[:, 1, sub, g * N_CMP:(g + 1) * N_CMP],
                              w2v[:, sub, :], start=(sub == 0), stop=(sub == 1))
            last.then_inc(cmp_kv, 1)
            for t in range(TT):
                tr = nc.tensor.transpose(aux[:, 3, t * 48:(t + 1) * 48], gate_f[:, t * P:(t + 1) * P], ident[0:48, 0:48])
            tr.then_inc(ng_mm, 1)

            def n_scores_of(b):
                g, kind = n_batch(b)
                wait(pe, n_sout, b)
                if 0 < b <= 2:
                    pe.wait_ge(n_pt, n_turns_before(b - 1) + 1)
                for h in range(4):
                    for t in range(TT):
                        toks = slice(t * P, (t + 1) * P)
                        if kind == 2:
                            out, rhs = aux[:, 0, (t * 4 + h) * N_CMP:(t * 4 + h + 1) * N_CMP], kct[:, g * N_CMP:(g + 1) * N_CMP]
                        else:
                            out = (aux[:, 0, h * P:(h + 1) * P] if t == 0 else
                                   aux[:, 1 + h // 2, (h % 2) * SEQ:(h % 2 + 1) * SEQ])
                            rhs = ksw[:, kind, g, 0:P * (t + 1)]
                        last = mm(out, nq[:, g, h, toks], rhs, start=True, stop=True)
                last.then_inc(n_scores, 1)

            def n_turn_of(b):
                pe.wait_ge(n_exp, b + 1)
                s = ns[:, b % 2]
                for j in n_turn_order(b):
                    for h in range(4):
                        if b % 3 == 2:
                            lo = (j * 4 + h) * N_CMP
                            tr = nc.tensor.transpose(aux[0:N_CMP, 3 + j, h * P:(h + 1) * P], s[:, lo:lo + N_CMP], ident[:])
                        else:
                            lo = h * P if j == 0 else 512 + h * SEQ + (j - 1) * P
                            tr = nc.tensor.transpose(n_turn_bank(b, j)[:, h * P:(h + 1) * P], s[:, lo:lo + P], ident[:])
                    tr.then_inc(n_turn, 1)

            def n_pv_of(b):
                g, kind = n_batch(b)
                pe.wait_ge(n_pt, n_turns_before(b + 1))
                wait(pe, n_o, b)
                for h in range(4):
                    o0, o1 = aux[:, 5, h * HD:(h + 1) * HD], aux[:, 5, 256 + h * HD:256 + (h + 1) * HD]
                    if kind == 2:
                        mm(o0, npt[0:N_CMP, 0, h * P:(h + 1) * P], vct[:, g, :], start=True, stop=True)
                        last = mm(o1, npt[0:N_CMP, 1, h * P:(h + 1) * P], vct[:, g, :], start=True, stop=True)
                    else:
                        vv = lambda kt: vsw[:, kind, kt, g * HD:(g + 1) * HD]
                        mm(o0, npt[:, 0, h * P:(h + 1) * P], vv(0), start=True, stop=True)
                        mm(o1, npt[:, 1, h * P:(h + 1) * P], vv(0), start=True)
                        last = mm(o1, npt[:, 2, h * P:(h + 1) * P], vv(1), stop=True)
                last.then_inc(n_pv, 1)

            q, gq = START["nsa_q"], GROUP["nsa_q"]
            group_out(pe, gq)
            n_scores_of(0)
            product_t(pe, q + 2, gq + 2, hh, hl)
            n_turn_of(0)
            group_out(pe, gq + 1)
            n_scores_of(1)
            product_t(pe, q + 3, gq + 3, hh, hl)
            n_pv_of(0)
            n_turn_of(1)
            n_scores_of(2)
            n_pv_of(1)
            group_out(pe, gq + 2)
            group_out(pe, gq + 3)
            n_scores_of(3)
            for b in range(2, 12):
                n_turn_of(b)
                if b + 2 < 12:
                    n_scores_of(b + 2)
                n_pv_of(b)
            turn_ys(ys2, nys_turned, nys_ready)
            for i in range(4):
                product_n(pe, START["nsa_out"] + i, GROUP["nsa_out"] + i, ysh2, ysl2,
                          ready=None if i else lambda k: (nys_lo, k + 1))
            norm_pe(pe, 5)
            ffn_pe(1, 52)


def alibi(n=16):
    return 2.0 ** (-8.0 * np.arange(1, n + 1) / n)


def t5_bucket(dist):
    n = np.maximum(dist, 0)
    nf = np.maximum(n, 1).astype(np.float32)
    large = 16 + (np.log(nf / np.float32(16)) / np.float32(np.log(8.0)) * np.float32(16)).astype(np.int32)
    return np.where(n < 16, n, np.minimum(large, 31))


def shape_constants():
    f = np.float32
    dist = np.arange(P)[:, None] + P - np.arange(SEQ)[None, :]
    slopes = alibi()

    def tiles(valid, by_head):
        return np.stack([np.where(valid, -s * dist, MASKED) for s in by_head], axis=1)

    zero = np.zeros(4)
    bias = [tiles(dist > 0, zero)]
    for (window, dil), first in zip(((128, 1), (512, 4), (2048, 16)), (0, 8, 12)):
        bias.append(tiles((dist >= 0) & (dist <= window) & (dist % dil == 0), slopes[first:first + 4]))
    bias.append(tiles(dist >= 0, zero))
    bias += [tiles(dist >= 0, slopes[4:8])] * 2
    tok = np.arange(SEQ)
    theta = (1.0 / (f(10000.0) ** np.linspace(0.0, 1.0, P, dtype=f))).astype(f)
    ang = tok.astype(f)[None, :] * theta[:, None]
    rel = tok[None, :] - np.arange(P)[:, None]
    log_gamma = np.log(1.0 - 2.0 ** (-5.0 - np.arange(RET_HEADS)))
    decay = np.stack([np.where(rel >= 0, np.exp(np.maximum(rel, 0) * g), 0.0) / 16.0 for g in log_gamma], axis=1)

    def one_hot(d):
        hot = np.zeros((33,) + d.shape, f)
        for b in range(32):
            hot[b] = (t5_bucket(d) == b) & (d >= 0)
        hot[32] = d < 0
        return hot

    return {
        "ident": np.eye(P, dtype=f), "bias1": np.stack(bias).astype(f),
        "cs": np.stack([np.cos(ang), np.sin(ang)], axis=1).astype(f), "decay": decay.astype(f),
        "hot": one_hot(SEQ - 1 - np.arange(384)),
        "masked": np.full((1, 16), MASKED, f),
    }


def k_tiles(w, c0, k0=0, nk=KT, cols=CW):
    part = w[k0 * P:(k0 + nk) * P, c0:c0 + cols].reshape(nk, P, cols).transpose(1, 0, 2).reshape(P, nk * cols)
    if part.shape[1] == CHUNK:
        return part
    return np.concatenate([part, np.zeros((P, CHUNK - part.shape[1]), part.dtype)], axis=1)


def lay_out(a):
    w = a["w_in"][0]
    off = np.cumsum([0, 256, 256, 256, 768, 768, 768, 256, 256, 256, 4, 256, 256, 256, 4096])
    qa, ka, va, qb, kb, vb, qc, kc, vc, ff, qd, kd, vd, gates = off[:14]

    def by_component(c0):
        m = w[:, c0:c0 + CW].reshape(D, 4, 2, 32).transpose(0, 2, 1, 3).reshape(D, CW)
        return k_tiles(m, 0)

    ch = [k_tiles(w, c) for c in (qa, ka, va)]
    for g in range(3):
        ch += [k_tiles(w, c + CW * g) for c in (qb, kb, vb)]
    ch += [k_tiles(w, c) for c in (qc, kc, vc)]
    ch += [by_component(qd), by_component(kd), k_tiles(w, vd)]
    ch += [k_tiles(w, gates + CW * i) for i in range(16)]
    ch += [k_tiles(a["w_branch"][0, n], 0, 0, 2, D) for n in range(4)]
    ch += [k_tiles(a["w_out"][0], CW * i) for i in range(4)]
    ch += [k_tiles(a["w_up"][0], CW * i) for i in range(16)]
    ch += [k_tiles(a["w_down"][0], CW * cb, KT * i) for cb in range(4) for i in range(4)]
    r = a["ret_w_in_2"][0]
    for h in range(RET_HEADS):
        for c0 in (CW * h, D + CW * h):
            head = r[:, c0:c0 + CW]
            ch.append(k_tiles(np.concatenate([head[:, 0::2], head[:, 1::2]], axis=1), 0))
        ch += [k_tiles(r, 2 * D + RET_DV * h + CW * i) for i in range(2)]
        ch += [k_tiles(r, 4 * D + RET_DV * h + CW * i) for i in range(2)]
    ch += [k_tiles(a["ret_w_out_2"][0], CW * cb, KT * i) for cb in range(4) for i in range(2)]

    def ffn(layer):
        win, wout = a["ffn_w_in_2"][layer], a["ffn_w_out_2"][layer]
        res = [k_tiles(np.concatenate([win[:, P * j:P * (j + 1)], win[:, FFN + P * j:FFN + P * (j + 1)]], axis=1), 0)
               for j in range(FFN_KT)]
        return res + [k_tiles(wout, CW * cb, KT * i, min(KT, FFN_KT - KT * i)) for cb in range(4) for i in range(3)]

    ch += ffn(0)
    kv = a["kv_w_2"]
    ch += [k_tiles(kv, CW * i) for i in range(6)]
    ch += [k_tiles(a["cmp_w1_k_2"], 0, KT * i) for i in range(2)] + [k_tiles(a["cmp_w1_v_2"], 0, KT * i) for i in range(2)]
    nsa = a["nsa_w_in_2"][0]
    ch += [k_tiles(nsa, CW * i) for i in range(4)]
    ch += [k_tiles(a["nsa_w_out_2"][0], CW * i) for i in range(4)]
    ch += ffn(1)
    assert len(ch) == N_CHUNKS

    def columns(g):
        return g.reshape(KT, P).T

    def pairs(pe):
        m = pe.reshape(16, P).T
        return np.stack([m, m], axis=2)

    def narrow(m):
        return m.reshape(KT, P, m.shape[1]).transpose(1, 0, 2)

    return {
        "x": a["x"][0], "stream": np.stack(ch),
        "gains": np.stack([columns(g) for g in (
            a["mix_norm_g"][0], a["mlp_norm_g"][0], a["mix_norm_pre_2"][0], a["ffn_norm_pre_2"][0],
            a["mix_norm_pre_2"][1], a["ffn_norm_pre_2"][1], a["kv_norm_2"])], axis=1),
        "grows": np.stack([a["final_norm_g"], a["mix_norm_post_2"][0], a["ffn_norm_post_2"][0],
                           a["mix_norm_post_2"][1], a["ffn_norm_post_2"][1]]),
        "w_f": narrow(w[:, ff:ff + 4]), "w_gate": narrow(nsa[:, D:D + 48]),
        "w2k": a["cmp_w2_k_2"].reshape(2, P, HD).transpose(1, 0, 2),
        "w2v": a["cmp_w2_v_2"].reshape(2, P, HD).transpose(1, 0, 2),
        "b_forget": a["b_forget"][0],
        "lams": np.stack([a["lambda_q1"][0], a["lambda_k1"][0], a["lambda_q2"][0], a["lambda_k2"][0]]),
        "diff_g": a["diff_norm_g"][0], "rel_bias": a["rel_bias_2"],
        "pe_in": np.stack([pairs(a["cmp_pe_k_2"]), pairs(a["cmp_pe_v_2"])], axis=1),
    }


def program(nc, arrays):
    io = {n: nc.dram_tensor(f"in_{n}", v.shape, F32, kind="ExternalInput").ap() for n, v in arrays.items()}
    io["strip"] = nc.dram_tensor("strip", (16, 384), F32, kind="Internal").ap()
    io["out"] = nc.dram_tensor("y", (SEQ, D), F32, kind="ExternalOutput").ap()
    build(nc, io)


def kernel(**inputs):
    import concourse.bacc as bacc
    from concourse.bass_utils import run_bass_kernel_spmd

    arrays = lay_out({n: np.asarray(v) for n, v in inputs.items()})
    arrays.update(shape_constants())
    arrays = {n: np.ascontiguousarray(v) for n, v in arrays.items()}
    nc = bacc.Bacc("TRN2", target_bir_lowering=False, num_devices=1)
    program(nc, arrays)
    r = run_bass_kernel_spmd(nc, [{f"in_{n}": v for n, v in arrays.items()}], core_ids=[0])
    return r.results[0]["y"].reshape(1, SEQ, D)
```
